# Optimizing a Trainium2 kernel written in Bass

```python
import jax, jax.numpy as jnp
from jax import lax
import numpy as np
import math

D_MODEL = 1024
BATCH = 1
SEQ = 1024
DEPTH = 1

CTX_LEN = 256
GRID_W = 64
D_F = D_MODEL // 2
N_FG = 4
FG = D_F // N_FG
D_M = D_MODEL // 2
N_H = 4
DH = D_M // N_H
CHUNK = 64
CONV_K = 3
N_GATE_KINDS = 4
FORGET_BIAS_LO = 3.0
FORGET_BIAS_HI = 6.0
N_BRANCH = 2
N_EXPERTS = 16
CAP_FACTOR = 2
D_FF_E = D_MODEL
EPS = 1e-6
OFF_F = 0
OFF_QK = OFF_F + D_F
OFF_V = OFF_QK + 2 * D_M
OFF_O = OFF_V + D_M
OFF_G = OFF_O + D_M
OFF_BR = OFF_G + N_GATE_KINDS * N_H
IN_COLS = OFF_BR + N_BRANCH * D_MODEL


def rmsnorm(x, g):
    xf = x.astype(jnp.float32)
    y = xf * lax.rsqrt(jnp.mean(xf * xf, axis=-1, keepdims=True) + EPS)
    return (y * g.astype(jnp.float32)).astype(x.dtype)

def modulate(h, shift, scale):
    return h * (1 + scale) + shift

def grid_conv(u, w, rows):
    b, l, ch = u.shape
    ug = u.reshape(b, rows, l // rows, ch)
    out = lax.conv_general_dilated(ug, w[:, :, None, :].astype(u.dtype), (1, 1), 'SAME',
                                   dimension_numbers=('NHWC', 'HWIO', 'NHWC'),
                                   feature_group_count=ch)
    return out.reshape(b, l, ch)

def mlstm_inputs(p, rows, w_conv, b_gates):
    b, l, _ = p.shape
    qk = jax.nn.silu(grid_conv(p[..., OFF_QK:OFF_V], w_conv, rows))
    to_heads = lambda a: a.reshape(b, l, N_H, DH).transpose(0, 2, 1, 3).astype(jnp.float32)
    q = to_heads(qk[..., :D_M])
    k = to_heads(qk[..., D_M:]) * (DH ** -0.5)
    v = to_heads(p[..., OFF_V:OFF_O])
    g = (p[..., OFF_G:OFF_BR].astype(jnp.float32).reshape(b, l, N_GATE_KINDS, N_H).transpose(2, 0, 3, 1)
         + b_gates.astype(jnp.float32)[:, None, :, None])
    return q, k, v, g

def zero_state(b):
    return (jnp.zeros((b, N_H, DH, DH), jnp.float32), jnp.zeros((b, N_H, DH), jnp.float32),
            jnp.zeros((b, N_H), jnp.float32))

def mlstm_scan(q, k, v, ig, fl, state):
    b, h, l, dh = q.shape
    nc = l // CHUNK

    def chunks(a):
        return jnp.moveaxis(a.reshape((b, h, nc, CHUNK) + a.shape[3:]), 2, 0)

    tril = jnp.tril(jnp.ones((CHUNK, CHUNK), dtype=bool))

    def step(carry, inp):
        c0, n0, m0 = carry
        qc, kc, vc, ic, fc = inp
        cum = jnp.cumsum(fc, axis=-1)
        logw = jnp.where(tril, cum[..., :, None] - cum[..., None, :] + ic[..., None, :], -jnp.inf)
        inter = cum + m0[..., None]
        m = jnp.maximum(inter, logw.max(-1))
        s = jnp.einsum('bhjd,bhsd->bhjs', qc, kc) * jnp.exp(logw - m[..., None])
        dec = jnp.exp(inter - m)
        num = jnp.einsum('bhjs,bhsd->bhjd', s, vc) + dec[..., None] * jnp.einsum('bhjk,bhkv->bhjv', qc, c0)
        den = s.sum(-1) + dec * jnp.einsum('bhjk,bhk->bhj', qc, n0)
        hc = num / jnp.maximum(jnp.abs(den), jnp.exp(-m))[..., None]
        tot = cum[..., -1]
        a = tot[..., None] - cum + ic
        m_new = jnp.maximum(tot + m0, a.max(-1))
        wa = jnp.exp(a - m_new[..., None])
        dn = jnp.exp(tot + m0 - m_new)
        c_new = dn[..., None, None] * c0 + jnp.einsum('bhs,bhsk,bhsv->bhkv', wa, kc, vc)
        n_new = dn[..., None] * n0 + jnp.einsum('bhs,bhsk->bhk', wa, kc)
        return (c_new, n_new, m_new), hc

    final, hs = lax.scan(step, state, (chunks(q), chunks(k), chunks(v), chunks(ig), chunks(fl)))
    return jnp.moveaxis(hs, 0, 2).reshape(b, h, l, dh), final

def bidir_mlstm(q, k, v, g, init):
    flip = lambda a: jnp.flip(a, axis=2)
    h_f, s_f = mlstm_scan(q, k, v, g[0], jax.nn.log_sigmoid(g[1]), init[0])
    h_b, s_b = mlstm_scan(flip(q), flip(k), flip(v), flip(g[2]), flip(jax.nn.log_sigmoid(g[3])), init[1])
    return h_f + flip(h_b), (s_f, s_b)

def branch_merge(p, h_m, w_fourier, w_mlstm, w_out):
    b, l, _ = p.shape
    u = p[..., OFF_F:OFF_QK].astype(jnp.float32).reshape(b, l, N_FG, FG)
    fu = jnp.fft.fft2(u, axes=(1, 3), norm='ortho').real.astype(p.dtype).reshape(b, l, D_F)
    y_f = fu @ w_fourier
    hm = h_m.transpose(0, 2, 1, 3).reshape(b, l, D_M).astype(p.dtype)
    y_m = (jax.nn.sigmoid(p[..., OFF_O:OFF_G]) * hm) @ w_mlstm
    gates = jax.nn.sigmoid(p[..., OFF_BR:])
    merged = gates[..., :D_MODEL] * y_f + gates[..., D_MODEL:] * y_m
    return merged @ w_out

def expert_choice(h, w_router, w_gate, w_up, w_down):
    b, l, _ = h.shape
    cap = CAP_FACTOR * l // N_EXPERTS
    aff = jax.nn.softmax(jnp.einsum('bld,de->ble', h, w_router).astype(jnp.float32), axis=-1)
    vals, idx = lax.top_k(jnp.swapaxes(aff, 1, 2), cap)
    bidx = jnp.arange(b)[:, None, None]
    xs = h[bidx, idx]
    hid = jax.nn.silu(jnp.einsum('becd,edf->becf', xs, w_gate)) * jnp.einsum('becd,edf->becf', xs, w_up)
    y = jnp.einsum('becf,efd->becd', hid, w_down) * vals[..., None].astype(h.dtype)
    return jnp.zeros_like(h).at[bidx, idx].add(y)

def first_inputs(seed: int = 0) -> dict:
    key = jax.random.key(seed)
    ks = jax.random.split(key, 20)
    nrm = jax.random.normal
    forget = jnp.linspace(FORGET_BIAS_LO, FORGET_BIAS_HI, N_H)
    zeros_h = jnp.zeros((N_H,))
    gate_base = jnp.stack([zeros_h, forget, zeros_h, forget])
    return {
        'x': nrm(ks[0], (BATCH, SEQ, D_MODEL), jnp.float32),
        'c': nrm(ks[1], (BATCH, D_MODEL), jnp.float32),
        'ctx': nrm(ks[2], (BATCH, CTX_LEN, D_MODEL), jnp.float32),
        'c_ctx': nrm(ks[3], (D_MODEL,), jnp.float32),
        'w_ada': nrm(ks[4], (DEPTH, D_MODEL, 6 * D_MODEL), jnp.float32) * (0.5 * D_MODEL ** -0.5),
        'b_ada': nrm(ks[5], (DEPTH, 6 * D_MODEL), jnp.float32) * 0.02,
        'g_norm1': 1.0 + 0.02 * nrm(ks[6], (DEPTH, D_MODEL), jnp.float32),
        'w_in': nrm(ks[7], (DEPTH, D_MODEL, IN_COLS), jnp.float32) * D_MODEL ** -0.5,
        'b_gates': gate_base[None] + 0.1 * nrm(ks[8], (DEPTH, N_GATE_KINDS, N_H), jnp.float32),
        'w_conv': nrm(ks[9], (DEPTH, CONV_K, CONV_K, 2 * D_M), jnp.float32) * (1.0 / CONV_K),
        'w_fourier': nrm(ks[10], (DEPTH, D_F, D_MODEL), jnp.float32) * D_F ** -0.5,
        'w_mlstm': nrm(ks[11], (DEPTH, D_M, D_MODEL), jnp.float32) * D_M ** -0.5,
        'w_out': nrm(ks[12], (DEPTH, D_MODEL, D_MODEL), jnp.float32) * D_MODEL ** -0.5,
        'g_norm2': 1.0 + 0.02 * nrm(ks[13], (DEPTH, D_MODEL), jnp.float32),
        'w_router': nrm(ks[14], (DEPTH, D_MODEL, N_EXPERTS), jnp.float32) * D_MODEL ** -0.5,
        'w_gate_e': nrm(ks[15], (DEPTH, N_EXPERTS, D_MODEL, D_FF_E), jnp.float32) * D_MODEL ** -0.5,
        'w_up_e': nrm(ks[16], (DEPTH, N_EXPERTS, D_MODEL, D_FF_E), jnp.float32) * D_MODEL ** -0.5,
        'w_down_e': nrm(ks[17], (DEPTH, N_EXPERTS, D_FF_E, D_MODEL), jnp.float32) * D_FF_E ** -0.5,
        'g_final': 1.0 + 0.02 * nrm(ks[18], (D_MODEL,), jnp.float32),
    }

def first_block(x, c, ctx, c_ctx, w_ada, b_ada, g_norm1, w_in, b_gates, w_conv, w_fourier, w_mlstm,
              w_out, g_norm2, w_router, w_gate_e, w_up_e, w_down_e, g_final):
    b, seq, _ = x.shape
    rows = seq // GRID_W
    for l in range(DEPTH):
        last = l == DEPTH - 1
        mx = (jax.nn.silu(c) @ w_ada[l] + b_ada[l])[:, None, :]
        sh1, sc1, ga1, sh2, sc2, ga2 = jnp.split(mx, 6, axis=-1)
        mc = jax.nn.silu(c_ctx) @ w_ada[l] + b_ada[l]
        csh1, csc1, cga1, csh2, csc2, cga2 = jnp.split(mc, 6, axis=-1)
        pc = modulate(rmsnorm(ctx, g_norm1[l]), csh1, csc1) @ w_in[l]
        qc, kc, vc, gc = mlstm_inputs(pc, 1, w_conv[l], b_gates[l])
        h_mc, ctx_states = bidir_mlstm(qc, kc, vc, gc, (zero_state(b), zero_state(b)))
        px = modulate(rmsnorm(x, g_norm1[l]), sh1, sc1) @ w_in[l]
        qx, kx, vx, gx = mlstm_inputs(px, rows, w_conv[l], b_gates[l])
        h_mx, _ = bidir_mlstm(qx, kx, vx, gx, ctx_states)
        x = x + ga1 * branch_merge(px, h_mx, w_fourier[l], w_mlstm[l], w_out[l])
        hx2 = modulate(rmsnorm(x, g_norm2[l]), sh2, sc2)
        x = x + ga2 * expert_choice(hx2, w_router[l], w_gate_e[l], w_up_e[l], w_down_e[l])
        if not last:
            ctx = ctx + cga1 * branch_merge(pc, h_mc, w_fourier[l], w_mlstm[l], w_out[l])
            hc2 = modulate(rmsnorm(ctx, g_norm2[l]), csh2, csc2)
            ctx = ctx + cga2 * expert_choice(hc2, w_router[l], w_gate_e[l], w_up_e[l], w_down_e[l])
    return rmsnorm(x, g_final)


D_G = D_MODEL // 4
N_GROUPS = 5
D_MIX = N_GROUPS * D_G
N_SUB = 4
HEAD_DIM = D_G // N_SUB
CONV_A = 3
CONV_D = 31
CHUNK_2 = 128
POOL_WINDOWS = (2, 4, 8, 16)
MEM_LEN = 256
LN_EPS = 1e-5
DEEPNORM_ALPHA = (2.0 * DEPTH) ** 0.25
DEEPNORM_BETA = (8.0 * DEPTH) ** -0.25

SPLIT_SIZES = (D_G, D_G, D_G, D_G, D_G, D_G, D_G, D_G, D_G, D_MIX)
D_IN = sum(SPLIT_SIZES)
SPLIT_OFFSETS = tuple(int(o) for o in np.cumsum(SPLIT_SIZES)[:-1])


def layer_norm(x, g, b):
    xf = x.astype(jnp.float32)
    mu = jnp.mean(xf, axis=-1, keepdims=True)
    var = jnp.mean(jnp.square(xf - mu), axis=-1, keepdims=True)
    y = (xf - mu) * lax.rsqrt(var + LN_EPS) * g.astype(jnp.float32) + b.astype(jnp.float32)
    return y.astype(x.dtype)

def causal_depthwise_conv(x, w):
    k, c = w.shape
    return lax.conv_general_dilated(
        x, w[:, None, :].astype(x.dtype), window_strides=(1,), padding=[(k - 1, 0)],
        dimension_numbers=("NWC", "WIO", "NWC"), feature_group_count=c)

def short_gated_conv(xa, ba, ca, w_conv):
    return ba * causal_depthwise_conv(ca * xa, w_conv)

def spatial_gating(u, v, ln_g, ln_b, w_s, b_s):
    bn, s, _ = v.shape
    u = jax.nn.gelu(u)
    v = layer_norm(jax.nn.gelu(v), ln_g, ln_b)
    v = v.reshape(bn, s // CHUNK_2, CHUNK_2, N_SUB, HEAD_DIM)
    mask = jnp.tril(jnp.ones((CHUNK_2, CHUNK_2), dtype=bool))
    w = jnp.where(mask[None], w_s, jnp.zeros_like(w_s))
    mixed = jnp.einsum("hts,bcshd->bcthd", w, v) + b_s.T[:, :, None]
    return u * mixed.reshape(bn, s, D_G)

def multiscale_pool(xc, w_grp, scale):
    bn, s, _ = xc.shape
    xf = xc.astype(jnp.float32).reshape(bn, s, N_SUB, HEAD_DIM)
    cs = jnp.pad(jnp.cumsum(xf, axis=1), ((0, 0), (1, 0), (0, 0), (0, 0)))
    t = jnp.arange(s)
    win = jnp.array(POOL_WINDOWS, dtype=jnp.int32)
    lo = jnp.maximum(t[:, None] + 1 - win[None, :], 0)
    window_sum = cs[:, 1:] - cs[:, lo, jnp.arange(N_SUB)[None, :]]
    count = jnp.minimum(t[:, None] + 1, win[None, :]).astype(jnp.float32)
    y = (window_sum / count[None, :, :, None] - xf).astype(xc.dtype)
    y = jnp.einsum("bsgc,gcd->bsgd", y, w_grp)
    return y.reshape(bn, s, D_G) * scale

def conformer_conv(a, g, w_dw, b_dw, ln_g, ln_b, w_pw):
    h = a * jax.nn.sigmoid(g)
    h = causal_depthwise_conv(h, w_dw) + b_dw
    h = jax.nn.silu(layer_norm(h, ln_g, ln_b))
    return h @ w_pw

def memory_cross_attention(q, mem, w_kv):
    bn, s, _ = q.shape
    k, v = jnp.split(mem @ w_kv, 2, axis=-1)
    q = q.reshape(bn, s, N_SUB, HEAD_DIM)
    k = k.reshape(bn, -1, N_SUB, HEAD_DIM)
    v = v.reshape(bn, -1, N_SUB, HEAD_DIM)
    scores = jnp.einsum("bshd,bmhd->bhsm", q, k).astype(jnp.float32) * (1.0 / math.sqrt(HEAD_DIM))
    p = jax.nn.softmax(scores, axis=-1).astype(v.dtype)
    return jnp.einsum("bhsm,bmhd->bshd", p, v).reshape(bn, s, D_G)

def hybrid_mixer(x, mem, w_in, conv_a_w, sg_ln_g, sg_ln_b, sg_w, sg_b, pool_w, pool_scale,
                 cc_dw_w, cc_dw_b, cc_ln_g, cc_ln_b, cc_pw_w, w_kv, w_out):
    proj = x @ w_in
    xa, ba, ca, u, v, xc, da, dg, q, gate = jnp.split(proj, SPLIT_OFFSETS, axis=-1)
    y_a = short_gated_conv(xa, ba, ca, conv_a_w)
    y_b = spatial_gating(u, v, sg_ln_g, sg_ln_b, sg_w, sg_b)
    y_c = multiscale_pool(xc, pool_w, pool_scale)
    y_d = conformer_conv(da, dg, cc_dw_w, cc_dw_b, cc_ln_g, cc_ln_b, cc_pw_w)
    y_e = memory_cross_attention(q, mem, w_kv)
    h = jnp.concatenate([y_a, y_b, y_c, y_d, y_e], axis=-1) * jax.nn.silu(gate)
    return h @ w_out

def second_inputs(seed: int = 0) -> dict:
    key = jax.random.key(seed)
    ks = jax.random.split(key, 20)
    L = DEPTH

    def nrm(k, shape, scale):
        return jax.random.normal(k, shape, jnp.float32) * scale

    return {
        "x": nrm(ks[0], (BATCH, SEQ, D_MODEL), 1.0),
        "mem": nrm(ks[1], (BATCH, MEM_LEN, D_MODEL), 1.0),
        "w_in": nrm(ks[2], (L, D_MODEL, D_IN), D_MODEL ** -0.5),
        "conv_a_w": nrm(ks[3], (L, CONV_A, D_G), CONV_A ** -0.5),
        "sg_ln_g": 1.0 + nrm(ks[4], (L, D_G), 0.05),
        "sg_ln_b": nrm(ks[5], (L, D_G), 0.05),
        "sg_w": nrm(ks[6], (L, N_SUB, CHUNK_2, CHUNK_2), CHUNK_2 ** -0.5),
        "sg_b": 1.0 + nrm(ks[7], (L, N_SUB, CHUNK_2), 0.1),
        "pool_w": nrm(ks[8], (L, N_SUB, HEAD_DIM, HEAD_DIM), HEAD_DIM ** -0.5),
        "pool_scale": 1.0 + nrm(ks[9], (L, D_G), 0.1),
        "cc_dw_w": nrm(ks[10], (L, CONV_D, D_G), CONV_D ** -0.5),
        "cc_dw_b": nrm(ks[11], (L, D_G), 0.02),
        "cc_ln_g": 1.0 + nrm(ks[12], (L, D_G), 0.05),
        "cc_ln_b": nrm(ks[13], (L, D_G), 0.05),
        "cc_pw_w": nrm(ks[14], (L, D_G, D_G), D_G ** -0.5),
        "w_kv": nrm(ks[15], (L, D_MODEL, 2 * D_G), D_MODEL ** -0.5),
        "w_out": nrm(ks[16], (L, D_MIX, D_MODEL), D_MIX ** -0.5 * DEEPNORM_BETA),
        "ln_g": 1.0 + nrm(ks[17], (L, D_MODEL), 0.05),
        "ln_b": nrm(ks[18], (L, D_MODEL), 0.05),
    }

def second_block(x, mem, w_in, conv_a_w, sg_ln_g, sg_ln_b, sg_w, sg_b, pool_w, pool_scale,
              cc_dw_w, cc_dw_b, cc_ln_g, cc_ln_b, cc_pw_w, w_kv, w_out, ln_g, ln_b):
    for l in range(DEPTH):
        y = hybrid_mixer(x, mem, w_in[l], conv_a_w[l], sg_ln_g[l], sg_ln_b[l], sg_w[l], sg_b[l],
                         pool_w[l], pool_scale[l], cc_dw_w[l], cc_dw_b[l], cc_ln_g[l], cc_ln_b[l],
                         cc_pw_w[l], w_kv[l], w_out[l])
        x = layer_norm(DEEPNORM_ALPHA * x + y, ln_g[l], ln_b[l])
    return x


def setup_inputs(seed=0):
    out = dict(first_inputs(seed))
    for name, value in second_inputs(seed + 1).items():
        if name != "x":
            out[name + "_2"] = value
    return out


def reference(
    x, c, ctx, c_ctx, w_ada, b_ada, g_norm1, w_in, b_gates, w_conv, w_fourier, w_mlstm, w_out,
    g_norm2, w_router, w_gate_e, w_up_e, w_down_e, g_final, mem_2, w_in_2, conv_a_w_2,
    sg_ln_g_2, sg_ln_b_2, sg_w_2, sg_b_2, pool_w_2, pool_scale_2, cc_dw_w_2, cc_dw_b_2,
    cc_ln_g_2, cc_ln_b_2, cc_pw_w_2, w_kv_2, w_out_2, ln_g_2, ln_b_2,
):
    x = first_block(
        x, c, ctx, c_ctx, w_ada, b_ada, g_norm1, w_in, b_gates, w_conv, w_fourier, w_mlstm,
        w_out, g_norm2, w_router, w_gate_e, w_up_e, w_down_e, g_final,
    )
    return second_block(
        x, mem_2, w_in_2, conv_a_w_2, sg_ln_g_2, sg_ln_b_2, sg_w_2, sg_b_2, pool_w_2,
        pool_scale_2, cc_dw_w_2, cc_dw_b_2, cc_ln_g_2, cc_ln_b_2, cc_pw_w_2, w_kv_2, w_out_2,
        ln_g_2, ln_b_2,
    )


_drawn_inputs = setup_inputs


def setup_inputs(seed=0):
    import zlib

    import numpy as np

    out = dict(_drawn_inputs(seed))
    spreads = {}
    factors = {'ctx': 7.316,
     'c_ctx': 6.714,
     'b_ada': 3.637,
     'g_norm1': 8.0,
     'g_norm2': 8.0,
     'g_final': 2.789,
     'mem_2': 4.315,
     'sg_ln_g_2': 29.144,
     'sg_ln_b_2': 29.714,
     'sg_b_2': 19.687,
     'pool_scale_2': 15.641,
     'cc_dw_b_2': 28.062,
     'cc_ln_g_2': 54.871,
     'cc_ln_b_2': 51.183,
     'w_kv_2': 3.981}
    for name, (base, spread) in spreads.items():
        noise = np.random.default_rng([zlib.crc32(name.encode()), seed]).standard_normal(out[name].shape)
        drawn = base * np.exp(spread * noise) if base else spread * noise
        out[name] = __import__('jax').numpy.asarray(drawn.astype(out[name].dtype))
    for name, factor in factors.items():
        out[name] = (out[name] * factor).astype(out[name].dtype)
    return out
```

```python
import math

import numpy as np

import concourse.bass as bass
from concourse import mybir

F32 = mybir.dt.float32
U32 = mybir.dt.uint32
ALU = mybir.AluOpType
ACT = mybir.ActivationFunctionType
X = mybir.AxisListType.X

P = 128
D = 1024
KD = D // P
T = 1024
TT = T // P
NCTX = 256
TA = NCTX + T
D_F = 512
D_M = 512
NH = 4
DH = 128
OFF_QK = 512
OFF_V = 1536
OFF_O = 2048
OFF_G = 2560
OFF_BR = 2576
GRID_W = 64
ROWS = T // GRID_W
EPS = 1e-6
LN_EPS = 1e-5
NE = 16
CAP = 128
DG = 256
CONV_D = 31
CONV_A = 3
MEM = 256
DMIX = 1280
ALPHA = 2.0 ** 0.25
MASKED = -1.0e30
BANK = 512


class Flag:

    def __init__(self, nc, name):
        self.sem = nc.alloc_semaphore(name)
        self.name = name
        self.n = 0
        self.base = 0


class Program:

    def __init__(self, nc):
        self.nc = nc
        self.pe, self.ve, self.ac, self.po, self.sp = nc.tensor, nc.vector, nc.scalar, nc.gpsimd, nc.sync
        self.engines = {"pe": self.pe, "ve": self.ve, "ac": self.ac, "po": self.po, "sp": self.sp}
        self.done = {k: Flag(nc, f"{k}_done") for k in ("pe", "ve", "ac", "po")}
        self.met = {}
        self.loop_i = None
        self.loop_per = {}
        self.passed = {k: nc.alloc_semaphore(f"{k}_passed") for k in self.engines}
        self.flags = {f.name: f for f in self.done.values()}

    def flag(self, name):
        if name not in self.flags:
            self.flags[name] = Flag(self.nc, name)
        return self.flags[name]

    def up(self, e, ins):
        f = self.done[e]
        ins.then_inc(f.sem, 1)
        f.n += 1
        return (f, f.n)

    def now(self, e):
        return (self.done[e], self.done[e].n)

    def load(self, e, flag, out, in_, **kw):
        f = self.flag(flag)
        self.engines[e].dma_start(out, in_, **kw).then_inc(f.sem, 16)
        f.n += 16
        return (f, f.n)

    def before(self, flag_or_engine):
        f = self.done.get(flag_or_engine) or self.flag(flag_or_engine)
        return (f, f.base)

    def need(self, e, *ticks):
        register_wait = False
        for tick in ticks:
            if tick is None:
                continue
            f, n = tick
            if self.loop_i is not None and f.name in self.loop_per and n >= f.base:
                self.engines[e].wait_ge(f.sem, n + self.loop_i * self.loop_per[f.name])
                register_wait = True
            elif n > self.met.get((e, f.name), 0):
                self.engines[e].wait_ge(f.sem, n)
                self.met[(e, f.name)] = n
        if register_wait:
            self.engines[e].sem_inc(self.passed[e], 1)

    def loop(self, count, per, body):
        flags = {k: self.flag(k) for k in per}
        for f in flags.values():
            f.base = f.n
        start = {k: f.n for k, f in self.flags.items()}
        with self.nc.Fori(0, count) as i:
            self.loop_i, self.loop_per = i, per
            body(i)
            self.loop_i, self.loop_per = None, {}
        grown = {k: f.n - start.get(k, 0) for k, f in self.flags.items()}
        grown = {k: v for k, v in grown.items() if v}
        assert grown == per, f"the loop's turn raises {grown}"
        for f in flags.values():
            f.n = f.base + count * (f.n - f.base)


class Banks:

    def __init__(self, g, tensors):
        self.g = g
        self.t = tensors
        self.last = [None] * len(tensors)
        self.k = 0

    def take(self):
        b = self.k % len(self.t)
        self.k += 1
        self.g.need("pe", self.last[b])
        return b

    def freed(self, b, tick):
        self.last[b] = tick


class Ring:

    def __init__(self, g, name, slots):
        self.g, self.name, self.slots = g, name, slots
        self.busy = [None] * len(slots)
        self.k = 0

    def fetch(self, view, source):
        s = self.k % len(self.slots)
        self.k += 1
        self.g.need("sp", self.busy[s])
        out = view(self.slots[s])
        tick = self.g.load("sp", f"{self.name}_loaded_{s}", out, source)
        return s, out, tick

    def used(self, s, tick):
        self.busy[s] = tick


def build(nc, A, C, out, scratch, taps=None):
    g = Program(nc)
    pe, ve, ac, po, sp = g.pe, g.ve, g.ac, g.po, g.sp
    up, need, load = g.up, g.need, g.load
    psum = [nc.alloc_psum_tensor(f"bank{b}", [P, BANK], F32) for b in range(8)]
    banks = Banks(g, psum)

    class Scope:

        def __enter__(self):
            self.stack = []
            return self

        def sb(self, name, shape, dt=F32):
            cm = nc.sbuf_tensor(name, shape, dt)
            t = cm.__enter__()
            self.stack.append(cm)
            return t

        def __exit__(self, *a):
            while self.stack:
                self.stack.pop().__exit__(None, None, None)

    def all_engines_meet():
        for e in ("pe", "ve", "ac", "po", "sp"):
            need(e, *[g.now(k) for k in ("pe", "ve", "ac", "po") if k != e])

    def tap(name, view):
        if taps is not None and name in taps:
            all_engines_meet()
            need("sp", load("sp", "tap", taps[name], view))
            all_engines_meet()

    turn = [0]

    def evacuate(e, out_, in_, scale=None, bias=None, func=None):
        if e == "ac":
            if func is None and scale is None and bias is None:
                return up("ac", ac.copy(out_, in_))
            kw = {}
            if scale is not None:
                kw["scale"] = scale
            if bias is not None:
                kw["bias"] = bias
            return up("ac", ac.activation(out_, in_, func or ACT.Identity, **kw))
        if scale is None and bias is None:
            return up("ve", ve.tensor_copy(out_, in_))
        if bias is None:
            return up("ve", ve.tensor_scalar(out_, in_, scale, None, ALU.mult))
        return up("ve", ve.tensor_scalar(out_, in_, scale, bias, ALU.mult, ALU.add))

    def either():
        turn[0] += 1
        return "ac" if turn[0] % 2 else "ve"

    top = Scope().__enter__()
    sb = top.sb

    ident = sb("ident", [P, P])
    ones = sb("ones", [P, P])
    load("sp", "constants", ident[:, :], C["ident"])
    ready_ones = up("po", po.memset(ones[:, :], 1.0))
    params1 = sb("params1", [64, P])
    params2 = sb("params2", [72, P])
    params3 = sb("params3", [76, P])
    cond = sb("cond", [16, P])
    rows_of = lambda ap: ap.rearrange("a (r p) -> (a r) p", p=P)
    load("sp", "constants", cond[0:8, :], rows_of(A["c"]))
    load("sp", "constants", cond[8:16, :], A["c_ctx"].rearrange("(r p) -> r p", p=P))
    load("sp", "constants", params1[0:8, :], rows_of(A["g_norm1"]))
    load("sp", "constants", params1[8:16, :], rows_of(A["g_norm2"]))
    load("sp", "constants", params1[16:64, :], rows_of(A["b_ada"]))
    load("sp", "constants", params2[:, :], A["w_conv"].rearrange("o a b (r p) -> (o a b r) p", p=P))
    at = 0
    P3 = {}
    for name, src, n in (
        ("conv_a", A["conv_a_w_2"].rearrange("o k (r p) -> (o k r) p", p=P), 6),
        ("pool_scale", rows_of(A["pool_scale_2"]), 2),
        ("dw", A["cc_dw_w_2"].rearrange("o k (r p) -> (o k r) p", p=P), 62),
        ("dw_b", rows_of(A["cc_dw_b_2"]), 2),
        ("cc_g", rows_of(A["cc_ln_g_2"]), 2),
        ("cc_b", rows_of(A["cc_ln_b_2"]), 2),
    ):
        got_constants = load("sp", "constants", params3[at:at + n, :], src)
        P3[name] = at
        at += n
    col1 = sb("col1", [P, 64])
    col2 = sb("col2", [P, 72])
    col3 = sb("col3", [P, 76])
    silu_c = sb("silu_c", [P, 16])
    silu_rows = sb("silu_rows", [16, P])
    bgates = sb("bgates", [16, 1])
    got_bgates = load("sp", "bgates", bgates[:, :], A["b_gates"].rearrange("o k h -> (k h) o"))
    ga1b = sb("ga1b", [P, D])
    ga2b = sb("ga2b", [P, D])
    got_ga = load("sp", "b_ada_rows", ga1b[:, :], A["b_ada"][:, 2 * D:3 * D].partition_broadcast(P).rearrange("p a n -> p (a n)"))
    got_ga = load("sp", "b_ada_rows", ga2b[:, :], A["b_ada"][:, 5 * D:6 * D].partition_broadcast(P).rearrange("p a n -> p (a n)"))
    mod1 = sb("mod1", [P, 4, KD])
    mod2 = sb("mod2", [P, 2, KD])
    small = sb("small", [P, 64])
    VALC = sb("token_weights", [P, NE])
    IDXC = sb("token_of_slot", [P, NE], U32)

    need("ac", got_constants)
    silu_done = up("ac", ac.activation(silu_rows[:, :], cond[:, :], ACT.Silu))
    need("pe", got_constants, silu_done)
    for src, dst, n in ((silu_rows, silu_c, 16), (params1, col1, 64), (params2, col2, 72), (params3, col3, 76)):
        b = banks.take()
        turned = up("pe", pe.transpose(psum[b][:, 0:n], src[:, :], ident[0:n, 0:n]))
        need("ve", turned)
        columns_ready = evacuate("ve", dst[:, :], psum[b][:, 0:n])
        banks.freed(b, columns_ready)

    w_ada_v = A["w_ada"].rearrange("o (k p) n -> p (o k) n", p=P)
    w_in_v = A["w_in"].rearrange("o (k p) n -> p (o k) n", p=P)

    blk = Scope().__enter__()
    XT = blk.sb("XT", [P, KD, TA])
    wslots = [blk.sb(f"wslot{s}", [P, KD * 512]) for s in range(3)]
    as_cols = lambda s: s[:, :].rearrange("p (k n) -> p k n", k=KD)
    as_rows4 = lambda s: s[:, :].rearrange("p (k n) -> p k n", k=4)
    ring = Ring(g, "w", wslots)

    with Scope() as st:
        xl = st.sb("x_rows", [P, TT, D])
        cl = st.sb("ctx_rows", [P, 2, D])
        junk = st.sb("junk", [P, D])
        ada = st.sb("ada_rows", [2, 2 * D])
        got_x = load("ac", "x_loaded", xl[:, :, :], A["x"].rearrange("b (t p) n -> p (b t) n", p=P))
        got_ctx = load("ac", "ctx_loaded", cl[:, :, :], A["ctx"].rearrange("b (t p) n -> p (b t) n", p=P))

        for blkn in range(4):
            s, w, got = ring.fetch(as_cols, w_ada_v[:, :, blkn * 512:(blkn + 1) * 512])
            b = banks.take()
            need("pe", got, columns_ready)
            for k in range(KD):
                mm = pe.matmul(psum[b][0:2, :], silu_c[:, k:k + 9:8], w[:, k, :], start=k == 0, stop=k == KD - 1)
            t = up("pe", mm)
            ring.used(s, t)
            need("ac", t)
            ada_rows_ready = evacuate("ac", ada[:, blkn * 512:(blkn + 1) * 512], psum[b][0:2, :])
            banks.freed(b, ada_rows_ready)
        b = banks.take()
        need("pe", ada_rows_ready)
        for j in range(16):
            mm = pe.transpose(psum[b][:, 2 * j:2 * j + 2], ada[:, j * P:(j + 1) * P], ident[0:2, 0:2])
        t = up("pe", mm)
        need("ve", t)
        adac = psum[b][:, 0:32].rearrange("p (j v) -> p v j", v=2)
        sh_t = up("ve", ve.tensor_tensor(mod1[:, 1, :], adac[:, 0, 0:8], col1[:, 16:24], ALU.add))
        up("ve", ve.tensor_tensor(mod1[:, 3, :], adac[:, 1, 0:8], col1[:, 16:24], ALU.add))
        up("ve", ve.tensor_tensor(mod1[:, 0, :], adac[:, 0, 8:16], col1[:, 24:32], ALU.add))
        t = up("ve", ve.tensor_tensor(mod1[:, 2, :], adac[:, 1, 8:16], col1[:, 24:32], ALU.add))
        banks.freed(b, t)
        need("ve", t)
        for v in (0, 2):
            mod1_ready = up("ve", ve.scalar_tensor_tensor(mod1[:, v, :], mod1[:, v, :], 1.0, col1[:, 0:8], ALU.add, ALU.mult))

        need("ac", got_x, got_ctx)
        rows = [(xl, j) for j in range(TT)] + [(cl, j) for j in range(2)]
        for n, (src, j) in enumerate(rows):
            squares = up("ac", ac.activation(junk[:, :], src[:, j, :], ACT.Square, accum_out=small[:, n:n + 1]))
            need("ac", squares)
        need("ve", squares)
        t = up("ve", ve.tensor_scalar(small[:, 16:26], small[:, 0:10], 1.0 / D, EPS, ALU.mult, ALU.add))
        need("ac", t)
        t = up("ac", ac.activation(small[:, 32:42], small[:, 16:26], ACT.Sqrt))
        need("ve", t)
        t = up("ve", ve.reciprocal(small[:, 48:58], small[:, 32:42]))
        need("ve", t)
        for n, (src, j) in enumerate(rows):
            rows_scaled = up("ve", ve.tensor_scalar(src[:, j, :], src[:, j, :], small[:, 48 + n:49 + n], None, ALU.mult))

        need("pe", rows_scaled)
        for k in range(KD):
            for src, j0, nj, col, v in ((cl, 0, 2, 0, 2), (xl, 0, 4, NCTX, 0), (xl, 4, 4, NCTX + 512, 0)):
                b = banks.take()
                for j in range(nj):
                    mm = pe.transpose(psum[b][:, j * P:(j + 1) * P], src[:, j0 + j, k * P:(k + 1) * P], ident[:, :])
                t = up("pe", mm)
                e = either()
                need(e, t, mod1_ready)
                t = evacuate(e, XT[:, k, col:col + nj * P], psum[b][:, 0:nj * P], mod1[:, v, k:k + 1], mod1[:, v + 1, k:k + 1])
                banks.freed(b, t)
    XT_ready = [g.now("ac"), g.now("ve")]
    all_engines_meet()
    tap("XT", XT[:, :, :])

    spans = ((0, 256), (256, 512), (768, 512))

    def project_transposed(w, c0, column_spans, finish, m=P):
        last = None
        for c, n in column_spans:
            b = banks.take()
            for k in range(KD):
                mm = pe.matmul(psum[b][0:m, 0:n], w[:, k, c0:c0 + m], XT[:, k, c:c + n], start=k == 0, stop=k == KD - 1)
            last = up("pe", mm)
            banks.freed(b, finish(psum[b], c, n, last))
        return last

    mix = Scope().__enter__()
    H = mix.sb("H", [P, TT, D_M])
    lstm = Scope().__enter__()
    KT = lstm.sb("KT", [P, NH, TA])
    QT = lstm.sb("QT", [P, NH, T])
    V = lstm.sb("V", [P, TA // P, NH, DH + 1])
    ones_col = up("po", po.memset(V[:, :, :, DH:DH + 1], 1.0))

    with Scope() as st:
        acc = st.sb("ada_acc", [P, 4 * D])
        aslot = H[:, :, :].rearrange("p a b -> p (a b)")
        grid = [st.sb(f"grid{i}", [P, (ROWS + 2) * (GRID_W + 2)]) for i in range(2)]
        gctx = [st.sb(f"gctx{i}", [P, NCTX + 2]) for i in range(2)]
        cacc = st.sb("conv_acc", [P, T])
        cacc2 = st.sb("conv_acc_ctx", [P, NCTX])
        aring = Ring(g, "ada", [aslot])
        zero = [up("po", po.memset(x[:, :], 0.0)) for x in grid + gctx][-1]

        def ada_part(n):
            s, w, got = aring.fetch(as_cols, w_ada_v[:, :, (4 + n) * 512:(5 + n) * 512])
            need("ve", got)
            o = acc[:, n * 512:(n + 1) * 512]
            t = up("ve", ve.tensor_scalar(o, w[:, 0, :], silu_c[:, 0:1], None, ALU.mult))
            for k in range(1, KD):
                need("ve", t)
                t = up("ve", ve.scalar_tensor_tensor(o, w[:, k, :], silu_c[:, k:k + 1], o, ALU.mult, ALU.add))
            aring.used(s, t)
            return t

        conv_read = [None, None]
        silu_read = None
        for blkn in range(2):
            s, w, got = ring.fetch(as_cols, w_in_v[:, :, OFF_QK + blkn * 512:OFF_QK + (blkn + 1) * 512])
            need("pe", got, *XT_ready)
            for h in range(NH):
                tile = blkn * 4 + h
                pad = grid[tile % 2][:, :].rearrange("p (r w) -> p r w", w=GRID_W + 2)
                cpad = gctx[tile % 2]

                def into_grid(bank, c, n, t, pad=pad, cpad=cpad):
                    need("ac", t, zero, conv_read[tile % 2])
                    if c == 0:
                        return evacuate("ac", cpad[:, 1:NCTX + 1], bank[:, 0:n])
                    r = (c - NCTX) // GRID_W
                    return evacuate("ac", pad[:, 1 + r:9 + r, 1:GRID_W + 1], bank[:, :].rearrange("p (r w) -> p r w", w=GRID_W))

                last = project_transposed(w, h * P, spans if blkn else spans[1:], into_grid)
                got_grid = g.now("ac")
                o = cacc[:, :].rearrange("p (r w) -> p r w", w=GRID_W)
                need("ve", got_grid, silu_read)
                for n in range(9):
                    src = pad[:, n // 3:n // 3 + ROWS, n % 3:n % 3 + GRID_W]
                    wc = col2[:, n * 8 + tile:n * 8 + tile + 1]
                    if n == 0:
                        t = up("ve", ve.tensor_scalar(o, src, wc, None, ALU.mult))
                    else:
                        need("ve", t)
                        t = up("ve", ve.scalar_tensor_tensor(o, src, wc, o, ALU.mult, ALU.add))
                convolved = t
                if blkn:
                    for n in range(3):
                        src = cpad[:, n:n + NCTX]
                        wc = col2[:, (3 + n) * 8 + tile:(3 + n) * 8 + tile + 1]
                        if n == 0:
                            t = up("ve", ve.tensor_scalar(cacc2[:, :], src, wc, None, ALU.mult))
                        else:
                            need("ve", t)
                            t = up("ve", ve.scalar_tensor_tensor(cacc2[:, :], src, wc, cacc2[:, :], ALU.mult, ALU.add))
                conv_read[tile % 2] = t
                need("ac", t)
                if blkn:
                    up("ac", ac.activation(KT[:, h, NCTX:TA], cacc[:, :], ACT.Silu))
                    silu_read = up("ac", ac.activation(KT[:, h, 0:NCTX], cacc2[:, :], ACT.Silu))
                else:
                    silu_read = up("ac", ac.activation(QT[:, h, :], cacc[:, :], ACT.Silu))
                ada_ready = ada_part(tile)
            ring.used(s, last)
        qk_ready = silu_read

        s, w, got = ring.fetch(as_cols, w_in_v[:, :, OFF_V:OFF_V + 512])
        need("pe", got)
        for j in range(TA // P):
            b = banks.take()
            for k in range(KD):
                mm = pe.matmul(psum[b][:, :], XT[:, k, j * P:(j + 1) * P], w[:, k, :], start=k == 0, stop=k == KD - 1)
            last = up("pe", mm)
            need("ac", last)
            v_ready = evacuate("ac", V[:, j, :, 0:DH], psum[b][:, :].rearrange("p (h n) -> p h n", h=NH))
            banks.freed(b, v_ready)
        ring.used(s, last)

        need("pe", ada_ready, ready_ones)
        need("ve", got_ga)
        for dst, c in ((ga1b, 0), (ga2b, 3 * D)):
            for n in range(2):
                b = banks.take()
                t = up("pe", pe.matmul(psum[b][:, :], ones[:, :], acc[:, c + n * 512:c + (n + 1) * 512], start=True, stop=True))
                need("ve", t)
                o = dst[:, n * 512:(n + 1) * 512]
                ga_ready = up("ve", ve.tensor_tensor(o, psum[b][:, :], o, ALU.add))
                banks.freed(b, ga_ready)
        b = banks.take()
        for j in range(16):
            mm = pe.matmul(psum[b][:, j:j + 1], acc[:, D + j * P:D + (j + 1) * P], ones[:, 0:1], start=True, stop=True)
        t = up("pe", mm)
        need("ve", t)
        up("ve", ve.tensor_tensor(mod2[:, 1, :], psum[b][:, 0:8], col1[:, 40:48], ALU.add))
        t = up("ve", ve.tensor_tensor(mod2[:, 0, :], psum[b][:, 8:16], col1[:, 48:56], ALU.add))
        banks.freed(b, t)
        need("ve", t)
        mod2_ready = up("ve", ve.scalar_tensor_tensor(mod2[:, 0, :], mod2[:, 0, :], 1.0, col1[:, 8:16], ALU.add, ALU.mult))
    all_engines_meet()
    tap("KT", KT[:, :, :])
    tap("QT", QT[:, :, :])
    tap("V", V[:, :, :, :])
    tap("ga1b", ga1b[:, :])
    tap("ga2b", ga2b[:, :])
    tap("mod2", mod2[:, :, :])

    R = lstm.sb("R", [32, TA])
    COL = lstm.sb("COL", [P, TA // P, 32])
    sel = lstm.sb("sel", [32, 8, P])
    got_sel = load("sp", "sel", sel[:, :, :], C["sel"])
    with Scope() as st:
        NC = TA // P
        in_H = lambda r, n: H[0:r, :, :].rearrange("p a b -> p (a b)")[:, n * TA:(n + 1) * TA]
        G = in_H(16, 0)
        wg = st.sb("w_gates", [P, KD, 16])
        IG = st.sb("ig", [36, TA])
        FL = st.sb("fl", [36, TA])
        CU = st.sb("cum", [36, TA])
        M = in_H(36, 2)
        WA = in_H(36, 0)
        RS = in_H(36, 1)
        got_rs = load("sp", "reset", RS[:, :], C["reset"])
        got_wg = load("sp", "w_gates", wg[:, :, :], w_in_v[:, :, OFF_G:OFF_BR])
        zeroed = [up("po", po.memset(x[:, :], 0.0)) for x in (IG, FL, CU, M)][-1]
        need("pe", got_wg)

        def gate_rows(bank, c, n, t):
            need("ac", t, got_bgates)
            return evacuate("ac", G[:, c:c + n], bank[0:16, 0:n], bias=bgates[:, 0:1])

        project_transposed(wg[:, :, :], 0, spans, gate_rows, m=16)
        gates_done = g.now("ac")
        need("sp", gates_done, zeroed)
        for d in range(2):
            got_gates = load("sp", "gate_rows", IG[32 * d:32 * d + 4, :], G[8 * d:8 * d + 4, :])
            got_gates = load("sp", "gate_rows", FL[32 * d:32 * d + 4, :], G[8 * d + 4:8 * d + 8, :])
        need("ve", got_gates, got_rs)
        t = up("ve", ve.scalar_tensor_tensor(WA[:, :], FL[:, :], -1.0, FL[:, :], ALU.mult, ALU.max))
        need("ac", t)
        t = up("ac", ac.activation(WA[:, :], WA[:, :], ACT.Exp, scale=-1.0))
        need("ac", t)
        t = up("ac", ac.activation(WA[:, :], WA[:, :], ACT.Ln, bias=1.0))
        need("ve", t)
        t = up("ve", ve.scalar_tensor_tensor(FL[:, :], FL[:, :], 0.0, WA[:, :], ALU.min, ALU.subtract))
        need("ve", t)
        forward = (slice(0, TA, 1),)
        backward = (slice(NCTX - 1, None, -1), slice(TA - 1, NCTX - 1, -1))
        for d, pieces in enumerate((forward, backward)):
            q = slice(32 * d, 32 * d + 4)
            state = 0.0
            for piece in pieces:
                up("ve", ve.tensor_tensor_scan(CU[q, piece], RS[q, piece], FL[q, piece], 0.0, ALU.mult, ALU.add))
                t = up("ve", ve.tensor_tensor_scan(M[q, piece], FL[q, piece], IG[q, piece], state, ALU.add, ALU.max))
                need("ve", t)
                state = M[q, 0:1]
        scans = t
        chunked = lambda x, q: x[q, :].rearrange("r (c j) -> r c j", j=P)
        m0 = st.sb("m0", [36, NC, 1])
        t = up("ve", ve.memset(m0[:, :, :], 0.0))
        need("ve", scans, t)
        mf, mb = chunked(M, slice(0, 4)), chunked(M, slice(32, 36))
        up("ve", ve.tensor_copy(m0[0:4, 1:NC, :], mf[:, 0:NC - 1, P - 1:P]))
        up("ve", ve.tensor_copy(m0[32:36, 0:1, :], mb[:, 1:2, 0:1]))
        up("ve", ve.tensor_copy(m0[32:36, 2:NC - 1, :], mb[:, 3:NC, 0:1]))
        t = up("ve", ve.tensor_copy(m0[32:36, NC - 1:NC, :], mb[:, 0:1, 0:1]))
        need("ve", t)
        q = slice(0, 36)
        m0b = m0[:, :, :].to_broadcast([36, NC, P])
        up("ve", ve.tensor_tensor(IG[:, :], IG[:, :], CU[:, :], ALU.subtract))
        t = up("ve", ve.tensor_tensor(FL[:, :], CU[:, :], M[:, :], ALU.subtract))
        need("ve", t)
        up("ve", ve.tensor_tensor(chunked(IG, q), chunked(IG, q), m0b, ALU.subtract))
        t = up("ve", ve.tensor_tensor(chunked(FL, q), chunked(FL, q), m0b, ALU.add))
        need("ve", t)
        need("ac", t)
        lnscale = st.sb("lnscale", [36, 1])
        t = up("po", po.memset(lnscale[:, :], 0.5 * math.log(DH)))
        need("ac", t)
        up("ac", ac.activation(M[:, :], M[:, :], ACT.Exp, scale=-1.0, bias=lnscale[:, 0:1]))
        for q, end in ((slice(0, 4), P - 1), (slice(32, 36), 0)):
            lasts = chunked(FL, q)[:, :, end:end + 1].to_broadcast([4, NC, P])
            t = up("ve", ve.tensor_tensor(chunked(WA, q), chunked(IG, q), lasts, ALU.add))
        need("ac", t)
        t = up("ac", ac.activation(WA[:, :], WA[:, :], ACT.Exp))
        need("sp", t, g.now("ve"))
        for n, src in enumerate((FL, IG, WA, M)):
            for d in range(2):
                packed = load("sp", "packed", R[8 * n + 4 * d:8 * n + 4 * d + 4, :], src[32 * d:32 * d + 4, :])
        need("pe", packed)
        b = banks.take()
        for c in range(NC):
            mm = pe.transpose(psum[b][:, 32 * c:32 * c + 32], R[:, c * P:(c + 1) * P], ident[0:32, 0:32])
        t = up("pe", mm)
        need("ve", t)
        col_ready = evacuate("ve", COL[:, :, :], psum[b][:, 0:32 * NC].rearrange("p (c r) -> p c r", r=32))
        banks.freed(b, col_ready)
    all_engines_meet()
    tap("R", R[:, :])

    with Scope() as st:
        maskt = st.sb("mask", [P, 2, P])
        got_mask = load("sp", "mask", maskt[:, :, :], C["mask"])
        need("po", got_mask)
        need("pe", got_sel, ones_col)
        CS = st.sb("cell", [P, 2, NH, DH + 1])
        in_slot = lambda n: wslots[0][:, n * 512:(n + 1) * 512].rearrange("p (h j) -> p h j", h=NH)
        kc = [st.sb(f"kc{d}", [P, NH, P]) for d in range(2)]
        ld = [st.sb(f"ld{d}", [P, NH, P]) for d in range(2)]
        dec = [st.sb(f"dec{d}", [P, NH, P]) for d in range(2)]
        em = [st.sb(f"em{d}", [P, NH, P]) for d in range(2)]
        qd = [in_slot(0 + d) for d in range(2)]
        kw = [in_slot(2 + d) for d in range(2)]
        den = [st.sb(f"den{d}", [P, NH, 1]) for d in range(2)]
        need("ve", up("ve", ve.memset(CS[:, :, :, :], 0.0)))
        h_zero = up("po", po.memset(H[:, :, :], 0.0))
        all_engines_meet()

        def chunk_of(tensor3, c):
            return tensor3[:, :, bass.ds(c * P, P)]

        def turn_of_states(chunks, outputs, started):
            pre = {}
            for d in range(2):
                c, cx = chunks[d]
                s_, m_, t_, a_ = (psum[4 * d + n] for n in range(4))
                need("ac", *started)
                kc_t = up("ac", ac.copy(kc[d][:, :, :], chunk_of(KT, c)))
                need("pe", *started)
                for h in range(NH):
                    mm = pe.matmul(m_[:, h * P:(h + 1) * P], sel[:, 4 * d + h, :], R[:, bass.ds(c * P, P)], start=True, stop=True)
                m_t = up("pe", mm)
                need("pe", kc_t)
                for h in range(NH):
                    mm = pe.transpose(t_[:, h * P:(h + 1) * P], kc[d][:, h, :], ident[:, :])
                t_t = up("pe", mm)
                need("ac", m_t)
                dec_t = up("ac", ac.activation(dec[d][:, :, :], m_[:, :].rearrange("p (h j) -> p h j", h=NH), ACT.Exp))
                if outputs:
                    ld_t = up("ac", ac.copy(ld[d][:, :, :], m_[:, :].rearrange("p (h j) -> p h j", h=NH)))
                    for h in range(NH):
                        mm = pe.matmul(s_[:, h * P:(h + 1) * P], kc[d][:, h, :], QT[:, h, bass.ds(cx * P, P)], start=True, stop=True)
                    s_t = up("pe", mm)
                    need("po", ld_t, dec_t, *started)
                    masked = up("po", po.tensor_tensor(em[d][:, :, :], ld[d][:, :, :], maskt[:, d:d + 1, :].to_broadcast([P, NH, P]), ALU.add))
                    qd_t = up("po", po.tensor_tensor(qd[d][:, :, :], dec[d][:, :, :], chunk_of(QT, cx), ALU.mult))
                    need("ac", masked)
                    for h in range(NH):
                        e_t = up("ac", ac.activation(em[d][:, h, :], em[d][:, h, :], ACT.Exp, bias=COL[:, bass.ds(c, 1), 8 + 4 * d + h]))
                    pre[d] = (s_t, e_t, qd_t, t_t, dec_t)
                else:
                    pre[d] = (None, None, None, t_t, dec_t)
            for d in range(2):
                c, cx = chunks[d]
                s_, m_, t_, a_ = (psum[4 * d + n] for n in range(4))
                s_t, e_t, qd_t, t_t, dec_t = pre[d]
                need("ve", t_t)
                wa = COL[:, bass.ds(c, 1), 16 + 4 * d:20 + 4 * d].rearrange("p a h -> p (a h)").unsqueeze(2).to_broadcast([P, NH, P])
                kw_t = up("ve", ve.tensor_tensor(kw[d][:, :, :], t_[:, :].rearrange("p (h j) -> p h j", h=NH), wa, ALU.mult))
                if outputs:
                    need("ve", s_t, e_t)
                    p_t = up("ve", ve.tensor_tensor(em[d][:, :, :], s_[:, :].rearrange("p (h j) -> p h j", h=NH), em[d][:, :, :], ALU.mult))
                    need("pe", p_t, qd_t)
                    for h in range(NH):
                        o = (s_ if h < 2 else a_)[:, (h % 2) * 129:(h % 2) * 129 + 129]
                        pe.matmul(o, em[d][:, h, :], V[:, bass.ds(c, 1), h, :].rearrange("p a n -> p (a n)"), start=True, stop=False)
                        mm = pe.matmul(o, qd[d][:, h, :], CS[:, d, h, :], start=False, stop=True)
                        if h == 1:
                            a0_t = up("pe", mm)
                    a1_t = up("pe", mm)
                    for n, (bank, a_t) in enumerate(((s_, a0_t), (a_, a1_t))):
                        need("ve", a_t)
                        em_col = COL[:, bass.ds(c, 1), 24 + 4 * d + 2 * n:26 + 4 * d + 2 * n].rearrange("p a h -> p (a h)").unsqueeze(2)
                        ds_ = bank[:, 0:258].rearrange("p (h j) -> p h j", h=2)
                        t = up("ve", ve.tensor_tensor(den[d][:, 2 * n:2 * n + 2, :], ds_[:, :, DH:DH + 1], em_col, ALU.max))
                        need("ve", t)
                        t = up("ve", ve.scalar_tensor_tensor(den[d][:, 2 * n:2 * n + 2, :], ds_[:, :, DH:DH + 1], -1.0, den[d][:, 2 * n:2 * n + 2, :], ALU.mult, ALU.max))
                        need("ve", t)
                        t = up("ve", ve.reciprocal(den[d][:, 2 * n:2 * n + 2, :], den[d][:, 2 * n:2 * n + 2, :]))
                        need("ve", t)
                        for h in range(2):
                            hh = 2 * n + h
                            o = H[:, bass.ds(cx, 1), hh * P:(hh + 1) * P].rearrange("p a n -> p (a n)")
                            h_t = up("ve", ve.scalar_tensor_tensor(o, ds_[:, h, 0:DH], den[d][:, hh, :], o, ALU.mult, ALU.add))
                    need("pe", h_t)
                need("pe", kw_t)
                for h in range(NH):
                    o = (t_ if h < 2 else a_)[:, (h % 2) * 129:(h % 2) * 129 + 129]
                    mm = pe.matmul(o, kw[d][:, h, :], V[:, bass.ds(c, 1), h, :].rearrange("p a n -> p (a n)"), start=True, stop=True)
                u_t = up("pe", mm)
                end = P - 1 if d == 0 else 0
                need("ve", u_t, dec_t)
                for h in range(NH):
                    o = CS[:, d, h, :]
                    u = (t_ if h < 2 else a_)[:, (h % 2) * 129:(h % 2) * 129 + 129]
                    up("ve", ve.scalar_tensor_tensor(o, o, dec[d][:, h, end:end + 1], u, ALU.mult, ALU.add))
                need("ve", g.now("ve"))

        for step in range(2):
            turn_of_states(((step, None), (1 - step, None)), False, [g.now("ve")])
        tap("CS", CS[:, :, :, :])
        if taps is not None and "CS" in taps:
            pass

        def body(i):
            turn_of_states(((i + 2, i), (9 - i, 7 - i)), True, [g.before("ve")])

        g.loop(TT, {"pe_done": 12, "ve_done": 32, "ac_done": 14, "po_done": 4}, body)
    all_engines_meet()
    lstm.__exit__()
    tap("H", H[:, :, :])

    OT = mix.sb("OT", [P, NH, T])
    s, w, got = ring.fetch(as_cols, w_in_v[:, :, OFF_O:OFF_O + 512])
    with Scope() as st:
        og = [st.sb(f"o_gate{n}", [P, 512]) for n in range(2)]
        freed = [None, None]
        need("pe", got)
        for j in range(TT):
            b = banks.take()
            for k in range(KD):
                mm = pe.matmul(psum[b][:, :], XT[:, k, NCTX + j * P:NCTX + (j + 1) * P], w[:, k, :], start=k == 0, stop=k == KD - 1)
            last = up("pe", mm)
            need("ac", last, freed[j % 2])
            t = up("ac", ac.activation(og[j % 2][:, :], psum[b][:, :], ACT.Sigmoid))
            banks.freed(b, t)
            need("ve", t)
            t = up("ve", ve.tensor_tensor(H[:, j, :], H[:, j, :], og[j % 2][:, :], ALU.mult))
            freed[j % 2] = t
        ring.used(s, last)
        need("pe", t)
        for h in range(NH):
            for half in range(2):
                b = banks.take()
                for j in range(4):
                    mm = pe.transpose(psum[b][:, j * P:(j + 1) * P], H[:, 4 * half + j, h * P:(h + 1) * P], ident[:, :])
                t = up("pe", mm)
                e = either()
                need(e, t)
                banks.freed(b, evacuate(e, OT[:, h, half * 512:half * 512 + 512], psum[b][:, :]))
        OT_ready = [g.now("ac"), g.now("ve")]

    FT = mix.sb("FT", [P, NH, T])
    with Scope() as st:
        all_engines_meet()
        uT = st.sb("uT", [P, NH, T])
        UE = st.sb("u_even", [P, NH, 512])
        UO = st.sb("u_odd", [P, NH, 512])
        cs = st.sb("dft_channels", [P, 2 * P])
        TC = st.sb("dft_cos", [P, 4, 512])
        TS = st.sb("dft_sin", [P, 4, 512])
        alt = st.sb("alternating", [1, 512])
        altc = st.sb("alternating_col", [P, 1])
        got_dft = load("sp", "dft", cs[:, :], C["dft_channels"])
        got_dft = load("sp", "dft", TC[:, :, :], C["dft_cos"].rearrange("(k p) n -> p k n", p=P))
        got_dft = load("sp", "dft", TS[:, :, :], C["dft_sin"].rearrange("(k p) n -> p k n", p=P))
        got_dft = load("sp", "dft", alt[:, :], C["alternating"])
        got_dft = load("sp", "dft", altc[:, :], C["alternating"][:, 0:P].rearrange("a p -> p a"))
        AA = H[:, :, :].rearrange("p a (b c) -> p (a b c)", b=1).rearrange("p (t g n) -> p t g n", t=4, g=NH)
        A5 = st.sb("along_channels_512", [1, NH * P])
        Qs = st.sb("odd_part", [P, 512])
        s, w, got = ring.fetch(as_cols, w_in_v[:, :, 0:D_F])
        need("pe", got)
        t = up("ve", ve.memset(UO[:, :, 0:1], 0.0))
        for gi in range(NH):
            def into_u(bank, c, n, t, gi=gi):
                need("ac", t)
                return evacuate("ac", uT[:, gi, c - NCTX:c - NCTX + n], bank[:, 0:n])
            last = project_transposed(w, gi * P, spans[1:], into_u)
            need("ve", g.now("ac"))
            up("ve", ve.tensor_copy(UE[:, gi, 0:1], uT[:, gi, 0:1]))
            up("ve", ve.tensor_tensor(UE[:, gi, 1:512], uT[:, gi, 1:512], uT[:, gi, T - 1:512:-1], ALU.add))
            up("ve", ve.tensor_tensor(UO[:, gi, 1:512], uT[:, gi, 1:512], uT[:, gi, T - 1:512:-1], ALU.subtract))
        ring.used(s, last)
        folded = g.now("ve")
        need("pe", folded, got_dft)
        for nt in range(4):
            for pair in range(2):
                b = banks.take()
                for gi in range(2):
                    for part, src in enumerate((UE, UO)):
                        o = (gi * 2 + part) * P
                        mm = pe.matmul(psum[b][:, o:o + P], src[:, 2 * pair + gi, nt * P:(nt + 1) * P], cs[:, part * P:(part + 1) * P], start=True, stop=True)
                t = up("pe", mm)
                e = either()
                need(e, t)
                banks.freed(b, evacuate(e, AA[:, nt, 2 * pair:2 * pair + 2, :], psum[b][:, :].rearrange("p (g n) -> p g n", g=2)))
        b = banks.take()
        for gi in range(NH):
            mm = pe.matmul(psum[b][0:1, gi * P:(gi + 1) * P], uT[:, gi, 512:513], cs[:, 0:P], start=True, stop=True)
        t = up("pe", mm)
        need("ac", t)
        t = evacuate("ac", A5[:, :], psum[b][0:1, :])
        banks.freed(b, t)
        need("pe", g.now("ve"), t)
        qs_read = None
        for gi in range(NH):
            bp, bq, b5 = banks.take(), banks.take(), banks.take()
            for nt in range(4):
                mm = pe.matmul(psum[bq][:, :], AA[:, nt, gi, P:2 * P], TS[:, nt, :], start=nt == 0, stop=nt == 3)
            q_t = up("pe", mm)
            for nt in range(4):
                pe.matmul(psum[bp][:, :], AA[:, nt, gi, 0:P], TC[:, nt, :], start=nt == 0, stop=False)
            mm = pe.matmul(psum[bp][:, :], A5[0:1, gi * P:(gi + 1) * P], alt[0:1, :], start=False, stop=True)
            for nt in range(4):
                pe.matmul(psum[b5][:, 0:1], AA[:, nt, gi, 0:P], altc[:, 0:1], start=nt == 0, stop=False)
            mm = pe.matmul(psum[b5][:, 0:1], A5[0:1, gi * P:(gi + 1) * P], alt[0:1, 0:1], start=False, stop=True)
            p_t = up("pe", mm)
            need("ac", q_t, qs_read)
            t = evacuate("ac", Qs[:, :], psum[bq][:, :])
            banks.freed(bq, t)
            need("ve", t, p_t)
            up("ve", ve.tensor_tensor(FT[:, gi, 0:512], psum[bp][:, :], Qs[:, :], ALU.subtract))
            qs_read = up("ve", ve.tensor_tensor(FT[:, gi, T - 1:512:-1], psum[bp][:, 1:512], Qs[:, 1:512], ALU.add))
            banks.freed(bp, qs_read)
            fourier_ready = up("ve", ve.tensor_copy(FT[:, gi, 512:513], psum[b5][:, 0:1]))
            banks.freed(b5, fourier_ready)
    all_engines_meet()
    tap("OT", OT[:, :, :])
    tap("FT", FT[:, :, :])

    MG = mix.sb("MG", [P, KD, T])
    with Scope() as st:
        wf = H[:, :, :].rearrange("p (k a) b -> p k (a b)", k=4)
        wm = st.sb("w_mlstm", [P, 4, D])
        got_f = load("sp", "w_fourier", wf, A["w_fourier"].rearrange("o (k p) n -> p (o k) n", p=P))
        got_m = load("sp", "w_mlstm", wm[:, :, :], A["w_mlstm"].rearrange("o (k p) n -> p (o k) n", p=P))
        s1 = [st.sb(f"gate_f{n}", [P, 512]) for n in range(2)]
        s2 = [st.sb(f"gate_m{n}", [P, 512]) for n in range(2)]
        read = [None, None]
        need("pe", got_f, got_m, *OT_ready, fourier_ready)
        n = 0
        for quad in range(2):
            sA, wA, gotA = ring.fetch(as_cols, w_in_v[:, :, OFF_BR + quad * 512:OFF_BR + (quad + 1) * 512])
            sB, wB, gotB = ring.fetch(as_cols, w_in_v[:, :, OFF_BR + D + quad * 512:OFF_BR + D + (quad + 1) * 512])
            need("pe", gotA, gotB)
            for jj in range(4):
                j = 4 * quad + jj
                for half in range(2):
                    c = NCTX + half * 512
                    bg = []
                    for w in (wA, wB):
                        b = banks.take()
                        for k in range(KD):
                            mm = pe.matmul(psum[b][:, :], w[:, k, jj * P:(jj + 1) * P], XT[:, k, c:c + 512], start=k == 0, stop=k == KD - 1)
                        bg.append((b, up("pe", mm)))
                    last = bg[-1][1]
                    by = []
                    for w, src in ((wf, FT), (wm, OT)):
                        b = banks.take()
                        for k in range(4):
                            mm = pe.matmul(psum[b][:, :], w[:, k, j * P:(j + 1) * P], src[:, k, half * 512:(half + 1) * 512], start=k == 0, stop=k == 3)
                        by.append((b, up("pe", mm)))
                    for (b, t), dst in zip(bg, (s1[n % 2], s2[n % 2])):
                        need("ac", t, read[n % 2])
                        t = up("ac", ac.activation(dst[:, :], psum[b][:, :], ACT.Sigmoid))
                        banks.freed(b, t)
                    o = MG[:, j, half * 512:(half + 1) * 512]
                    need("ve", t, by[0][1])
                    t1 = up("ve", ve.tensor_tensor(s1[n % 2][:, :], psum[by[0][0]][:, :], s1[n % 2][:, :], ALU.mult))
                    banks.freed(by[0][0], t1)
                    need("ve", by[1][1])
                    t = up("ve", ve.tensor_tensor(s2[n % 2][:, :], psum[by[1][0]][:, :], s2[n % 2][:, :], ALU.mult))
                    banks.freed(by[1][0], t)
                    need("ve", t)
                    read[n % 2] = merged_ready = up("ve", ve.tensor_tensor(o, s1[n % 2][:, :], s2[n % 2][:, :], ALU.add))
                    n += 1
            ring.used(sA, last)
            ring.used(sB, last)
    all_engines_meet()
    tap("MG", MG[:, :, :])

    xn_rows, x2_rows, xf_rows = scratch["xn"], scratch["x2"], scratch["xf"]
    with Scope() as st:
        X2 = XT[:, :, 0:D]
        tmp = [st.sb(f"attn_tmp{n}", [P, 512]) for n in range(2)]
        got_x2 = load("ac", "x_again", X2[:, :, :], A["x"].rearrange("b (t p) n -> p (b t) n", p=P))
        w_out_v = A["w_out"].rearrange("o (k p) n -> p (o k) n", p=P)
        for half in range(2):
            s, w, got = ring.fetch(as_cols, w_out_v[:, :, half * 512:(half + 1) * 512])
            need("pe", got, merged_ready)
            need("ve", got_x2)
            for j in range(TT):
                b = banks.take()
                for k in range(KD):
                    mm = pe.matmul(psum[b][:, :], MG[:, k, j * P:(j + 1) * P], w[:, k, :], start=k == 0, stop=k == KD - 1)
                last = up("pe", mm)
                need("ve", last)
                hs = slice(half * 512, (half + 1) * 512)
                t = up("ve", ve.tensor_tensor(tmp[j % 2][:, :], psum[b][:, :], ga1b[:, hs], ALU.mult))
                banks.freed(b, t)
                need("ve", t)
                x2_ready = up("ve", ve.tensor_tensor(X2[:, j, hs], X2[:, j, hs], tmp[j % 2][:, :], ALU.add))
            ring.used(s, last)
        need("sp", x2_ready)
        stored = load("sp", "x2_stored", x2_rows.rearrange("(t p) n -> p t n", p=P), X2[:, :, :])
        need("ac", x2_ready)
        for j in range(TT):
            for half in range(2):
                squares = up("ac", ac.activation(tmp[half][:, :], X2[:, j, half * 512:(half + 1) * 512], ACT.Square, accum_out=small[:, 2 * j + half:2 * j + half + 1]))
                need("ac", squares)
        need("ve", squares)
        t = up("ve", ve.tensor_reduce(small[:, 16:24], small[:, 0:16].rearrange("p (j h) -> p j h", h=2), X, ALU.add))
        need("ve", t)
        t = up("ve", ve.tensor_scalar(small[:, 16:24], small[:, 16:24], 1.0 / D, EPS, ALU.mult, ALU.add))
        need("ac", t)
        t = up("ac", ac.activation(small[:, 32:40], small[:, 16:24], ACT.Sqrt))
        need("ve", t)
        t = up("ve", ve.reciprocal(small[:, 48:56], small[:, 32:40]))
        need("ve", t, stored)
        for j in range(TT):
            xn_ready = up("ve", ve.tensor_scalar(X2[:, j, :], X2[:, j, :], small[:, 48 + j:49 + j], None, ALU.mult))
        need("sp", xn_ready)
        xn_stored = load("sp", "xn_stored", xn_rows.rearrange("(t p) n -> p t n", p=P), X2[:, :, :])

        wr = st.sb("w_router", [P, KD, NE])
        got_wr = load("ac", "w_router", wr[:, :, :], A["w_router"].rearrange("o (k p) n -> p (o k) n", p=P))
        need("pe", xn_ready)
        for k in range(KD):
            for half in range(2):
                b = banks.take()
                for j in range(4):
                    mm = pe.transpose(psum[b][:, j * P:(j + 1) * P], X2[:, 4 * half + j, k * P:(k + 1) * P], ident[:, :])
                t = up("pe", mm)
                e = either()
                need(e, t, mod2_ready, last)
                t = evacuate(e, MG[:, k, half * 512:(half + 1) * 512], psum[b][:, :], mod2[:, 0, k:k + 1], mod2[:, 1, k:k + 1])
                banks.freed(b, t)
        need("pe", g.now("ac"), g.now("ve"), got_wr)
        b = banks.take()
        for j in range(TT):
            for k in range(KD):
                mm = pe.matmul(psum[b][:, j * NE:(j + 1) * NE], MG[:, k, j * P:(j + 1) * P], wr[:, k, :], start=k == 0, stop=k == KD - 1)
        logits = up("pe", mm)
        af = st.sb("affinity", [P, TT, NE])
        red = st.sb("softmax_red", [P, 2, TT, 1])
        lg = psum[b][:, 0:TT * NE].rearrange("p (j e) -> p j e", e=NE)
        need("ve", logits)
        t = up("ve", ve.tensor_reduce(red[:, 0, :, :].rearrange("p j a -> p (j a)"), lg, X, ALU.max))
        need("ve", t)
        t = up("ve", ve.tensor_tensor(af[:, :, :], lg, red[:, 0, :, :].to_broadcast([P, TT, NE]), ALU.subtract))
        banks.freed(b, t)
        need("ac", t)
        t = up("ac", ac.activation(af[:, :, :], af[:, :, :], ACT.Exp))
        need("ve", t)
        t = up("ve", ve.tensor_reduce(red[:, 1, :, :].rearrange("p j a -> p (j a)"), af[:, :, :], X, ALU.add))
        need("ve", t)
        t = up("ve", ve.reciprocal(red[:, 1, :, :], red[:, 1, :, :]))
        need("ve", t)
        af_ready = up("ve", ve.tensor_tensor(af[:, :, :], af[:, :, :], red[:, 1, :, :].to_broadcast([P, TT, NE]), ALU.mult))
        tap("af", af[:, :, :])
        AT = st.sb("affinity_T", [NE, T])
        need("pe", af_ready)
        for half in range(2):
            b = banks.take()
            for j in range(4):
                mm = pe.transpose(psum[b][0:NE, j * P:(j + 1) * P], af[:, 4 * half + j, :], ident[:, :])
            t = up("pe", mm)
            need("ve", t)
            t = evacuate("ve", AT[:, half * 512:(half + 1) * 512], psum[b][0:NE, :])
            banks.freed(b, t)
        val = st.sb("top_values", [NE, CAP])
        idx = st.sb("top_tokens", [NE, CAP], U32)
        idxf = st.sb("top_tokens_f", [NE, CAP])
        need("ve", t)
        for r in range(CAP // 8):
            v8, i8 = val[:, 8 * r:8 * r + 8], idx[:, 8 * r:8 * r + 8]
            t = up("ve", ve.max(v8, AT[:, :]))
            need("ve", t)
            t = up("ve", ve.max_index(i8, v8, AT[:, :]))
            t = up("ve", ve.match_replace(AT[:, :], v8, AT[:, :], -1.0))
            need("ve", t)
        t = up("ve", ve.tensor_copy(idxf[:, :], idx[:, :]))
        need("pe", t)
        b = banks.take()
        pe.transpose(psum[b][:, 0:NE], val[:, :], ident[0:NE, 0:NE])
        t = up("pe", pe.transpose(psum[b][:, NE:2 * NE], idxf[:, :], ident[0:NE, 0:NE]))
        need("ve", t)
        up("ve", ve.tensor_copy(VALC[:, :], psum[b][:, 0:NE]))
        top_ready = up("ve", ve.tensor_copy(IDXC[:, :], psum[b][:, NE:2 * NE]))
        banks.freed(b, top_ready)
    all_engines_meet()
    for e in ("po", "ac", "sp"):
        need(e, xn_stored, stored)
    mix.__exit__()
    blk.__exit__()

    with Scope() as st:
        MATS = ("g0", "u0", "g1", "u1", "d0", "d1")
        wt = {m: st.sb(f"expert_{m}", [P, KD, 512]) for m in MATS}
        source = {"g": A["w_gate_e"], "u": A["w_up_e"], "d": A["w_down_e"]}
        source = {k: v.rearrange("o e (k p) n -> (o e) p k n", p=P) for k, v in source.items()}
        xs = st.sb("expert_x", [P, D])
        xsT = st.sb("expert_xT", [P, KD, P])
        hid = st.sb("expert_hidden", [P, D])
        hidT = st.sb("expert_hiddenT", [P, KD, P])
        y = st.sb("expert_y", [P, D])
        idx_g = st.sb("gather_tokens", [P, 1], U32)
        idx_s = st.sb("scatter_tokens", [P, 1], U32)
        silu = st.sb("expert_silu", [P, 2, 512])

        def fetch(m, e):
            src = source[m[0]][bass.ds(e, 1), :, :, 512 * int(m[1]):512 * int(m[1]) + 512].rearrange("a p k n -> (a p) k n")
            return load("sp", f"expert_{m}_loaded", wt[m][:, :, :], src)

        def gather(e):
            t = up("po", po.tensor_copy(idx_g[:, :], IDXC[:, bass.ds(e, 1)]))
            need("po", t)
            f = g.flag("gathered")
            po.indirect_dma_start(xs[:, :], None, xn_rows, bass.IndirectOffsetOnAxis(idx_g[:, :], 0)).then_inc(f.sem, 16)
            f.n += 16
            return (f, f.n)

        def turn_x(after):
            need("pe", *after)
            for half in range(2):
                for k in range(4):
                    kk = 4 * half + k
                    mm = pe.transpose(psum[4 + half][:, k * P:(k + 1) * P], xs[:, kk * P:(kk + 1) * P], ident[:, :])
                t = up("pe", mm)
                for k in range(4):
                    kk = 4 * half + k
                    need("ac", t)
                    r = up("ac", ac.activation(xsT[:, kk, :], psum[4 + half][:, k * P:(k + 1) * P], ACT.Identity, scale=mod2[:, 0, kk:kk + 1], bias=mod2[:, 1, kk:kk + 1]))
            return t, r

        def up_products(landed, xT_ready, y_read=None):
            used = {}
            need("pe", xT_ready)
            for half in range(2):
                ts = []
                for n, m in enumerate((f"g{half}", f"u{half}")):
                    need("pe", landed[m], y_read if n else None)
                    bank = psum[2 * half + n]
                    for k in range(KD):
                        mm = pe.matmul(bank[:, :], xsT[:, k, :], wt[m][:, k, :], start=k == 0, stop=k == KD - 1)
                    used[m] = up("pe", mm)
                need("ac", used[f"g{half}"])
                t = up("ac", ac.activation(silu[:, half, :], psum[2 * half][:, :], ACT.Silu))
                need("ve", t, used[f"u{half}"])
                hid_t = up("ve", ve.tensor_tensor(hid[:, half * 512:(half + 1) * 512], psum[2 * half + 1][:, :], silu[:, half, :], ALU.mult))
                used[f"hid{half}"] = hid_t
            return used

        def down_product(e, landed, used, y_free):
            for half in range(2):
                need("pe", used[f"hid{half}"])
                for k in range(4):
                    kk = 4 * half + k
                    mm = pe.transpose(psum[6 + half][:, k * P:(k + 1) * P], hid[:, kk * P:(kk + 1) * P], ident[:, :])
                t = up("pe", mm)
                need("ve", t)
                t = up("ve", ve.tensor_copy(hidT[:, 4 * half:4 * half + 4, :], psum[6 + half][:, :].rearrange("p (k n) -> p k n", k=4)))
            need("pe", t)
            for half in range(2):
                m = f"d{half}"
                need("pe", landed[m])
                for k in range(KD):
                    mm = pe.matmul(psum[2 * half + 1][:, :], hidT[:, k, :], wt[m][:, k, :], start=k == 0, stop=k == KD - 1)
                used[m] = up("pe", mm)
                need("ve", used[m], *y_free)
                hs = slice(half * 512, (half + 1) * 512)
                t = up("ve", ve.scalar_tensor_tensor(y[:, hs], psum[2 * half + 1][:, :], VALC[:, bass.ds(e, 1)], ga2b[:, hs], ALU.mult, ALU.mult))
            need("po", *y_free)
            c = up("po", po.tensor_copy(idx_s[:, :], IDXC[:, bass.ds(e, 1)]))
            need("po", c, t)
            f = g.flag("scattered")
            po.indirect_dma_start(x2_rows, bass.IndirectOffsetOnAxis(idx_s[:, :], 0), y[:, :], None, compute_op=ALU.add).then_inc(f.sem, 16)
            f.n += 16
            return (f, f.n)

        landed = {m: fetch(m, 0) for m in MATS}
        gathered = gather(0)
        x_read, xT_ready = turn_x([gathered])
        need("pe", xT_ready)
        need("po", x_read)

        def expert(i):
            for m in MATS:
                landed[m] = (g.flag(f"expert_{m}_loaded"), g.flag(f"expert_{m}_loaded").n)
            y_free = [(g.flag("scattered"), g.flag("scattered").n)]
            gathered = gather(i + 1)
            used = up_products(landed, g.now("ac"), g.now("ve"))
            x_read, xT_next = turn_x([gathered, used["u1"]])
            down_product(i, landed, used, y_free)
            for m in MATS:
                need("sp", used[m])
                fetch(m, i + 1)
            need("po", x_read)

        expert(0)
        g.loop(NE - 2, {"pe_done": 10, "ac_done": 10, "ve_done": 6, "po_done": 2, "gathered": 16, "scattered": 16,
                        **{f"expert_{m}_loaded": 16 for m in MATS}}, lambda i: expert(i + 1))
        landed = {m: (g.flag(f"expert_{m}_loaded"), g.flag(f"expert_{m}_loaded").n) for m in MATS}
        used = up_products(landed, g.now("ac"), g.now("ve"))
        scattered = down_product(NE - 1, landed, used, [(g.flag("scattered"), g.flag("scattered").n)])
    all_engines_meet()

    two = Scope().__enter__()
    XFT = two.sb("XFT", [P, KD, T])
    need("sp", scattered)
    with Scope() as st:
        XF = st.sb("XF", [P, TT, D])
        junk = st.sb("junk2", [P, D])
        gf = st.sb("g_final", [P, D])
        got_gf = load("ac", "g_final", gf[:, :], A["g_final"].partition_broadcast(P))
        got_xf = load("sp", "xf_loaded", XF[:, :, :], x2_rows.rearrange("(t p) n -> p t n", p=P))
        tap_x3 = tap("X3", XF[:, :, :]) if taps is not None and "X3" in taps and not need("sp", got_xf) else None
        need("ac", got_xf)
        for j in range(TT):
            squares = up("ac", ac.activation(junk[:, :], XF[:, j, :], ACT.Square, accum_out=small[:, j:j + 1]))
            need("ac", squares)
        need("ve", squares, got_gf)
        t = up("ve", ve.tensor_scalar(small[:, 16:24], small[:, 0:8], 1.0 / D, EPS, ALU.mult, ALU.add))
        need("ac", t)
        t = up("ac", ac.activation(small[:, 32:40], small[:, 16:24], ACT.Sqrt))
        need("ve", t)
        t = up("ve", ve.reciprocal(small[:, 48:56], small[:, 32:40]))
        need("ve", t)
        for j in range(TT):
            xf_ready = up("ve", ve.scalar_tensor_tensor(XF[:, j, :], XF[:, j, :], small[:, 48 + j:49 + j], gf[:, :], ALU.mult, ALU.mult))
            need("pe", xf_ready)
            for half in range(2):
                b = banks.take()
                for k in range(4):
                    kk = 4 * half + k
                    mm = pe.transpose(psum[b][:, k * P:(k + 1) * P], XF[:, j, kk * P:(kk + 1) * P], ident[:, :])
                t = up("pe", mm)
                e = either()
                need(e, t)
                banks.freed(b, evacuate(e, XFT[:, 4 * half:4 * half + 4, j * P:(j + 1) * P], psum[b][:, :].rearrange("p (k n) -> p k n", k=4)))
        need("sp", xf_ready)
        xf_stored = load("sp", "xf_stored", xf_rows.rearrange("(t p) n -> p t n", p=P), XF[:, :, :])
        need("sp", xf_stored)
    for e in ("ac", "ve", "po"):
        need(e, xf_stored)
    all_engines_meet()
    tap("XFT", XFT[:, :, :])

    NMIX = DMIX // P
    HT = two.sb("HT", [P, NMIX, T])
    slots2 = [two.sb(f"w2slot{s}", [P, NMIX * 512]) for s in range(2)]
    ring2 = Ring(g, "w2", slots2)
    cols8 = lambda s: s[:, 0:KD * 512].rearrange("p (k n) -> p k n", k=KD)
    cols10 = lambda s: s[:, :].rearrange("p (k n) -> p k n", k=NMIX)
    w_in2_v = A["w_in_2"].rearrange("o (k p) n -> p (o k) n", p=P)

    def project2(w, c0, finish):
        for half in range(2):
            b = banks.take()
            for k in range(KD):
                mm = pe.matmul(psum[b][:, :], w[:, k, c0:c0 + P], XFT[:, k, half * 512:(half + 1) * 512], start=k == 0, stop=k == KD - 1)
            last = up("pe", mm)
            banks.freed(b, finish(psum[b], slice(half * 512, (half + 1) * 512), last))
        return last

    with Scope() as st:
        HP = st.sb("conformer_in", [P, 2, CONV_D - 1 + T])
        CV = st.sb("conformer_conv", [P, 2, T])
        XP = st.sb("padded_a", [P, 2, 16 + T])
        XC = st.sb("padded_b", [P, 2, 16 + T])
        VG = st.sb("gating_v", [P, TT, DG])
        memT = st.sb("memT", [P, KD, MEM])
        K2T = st.sb("mem_keys", [P, 2, MEM])
        V2 = st.sb("mem_values", [P, 2, DG])
        tm = [st.sb(f"tmp2_{n}", [P, 512]) for n in range(3)]
        WT = st.sb("gating_w", [P, NH, P])
        sgw = st.sb("gating_w_rows", [P, NH, P])
        tril = st.sb("tril", [P, P])
        SB_ = st.sb("gating_bias", [P, 2, P])
        lng = st.sb("gating_ln", [P, 2, DG])
        pw = st.sb("conformer_pw", [P, 2, DG])
        grp = st.sb("pool_grp", [P, 2, P])
        fix = st.sb("pool_fix", [P, 2, 16])
        invw = st.sb("pool_inv", [P, 2])
        stats = st.sb("gating_stats", [P, TT, 6])
        mv = st.sb("gating_mv", [P, TT, 2])
        sd = st.sb("gating_sd", [P, TT, 1])

        zeros = [up("po", po.memset(x, 0.0)) for x in (HP[:, :, 0:CONV_D - 1], XC[:, :, 0:16], grp[:, :, :])][-1]
        mem_rows = XP[:, :, 0:D]
        got_mem = load("ac", "mem", mem_rows, A["mem_2"].rearrange("b (m p) n -> p (b m) n", p=P))
        load("ac", "small2", sgw[:, :, :], A["sg_w_2"].rearrange("o h t s -> t (o h) s"))
        load("ac", "small2", tril[:, :], C["tril"])
        load("ac", "small2", lng[:, 0, :], A["sg_ln_g_2"].partition_broadcast(P).rearrange("p a n -> p (a n)"))
        load("ac", "small2", lng[:, 1, :], A["sg_ln_b_2"].partition_broadcast(P).rearrange("p a n -> p (a n)"))
        load("ac", "small2", pw[:, :, :], A["cc_pw_w_2"].rearrange("o (k p) n -> p (o k) n", p=P))
        load("ac", "small2", fix[:, :, :], C["pool_fix"])
        load("ac", "small2", invw[:, :], C["pool_inv"])
        need("ac", zeros)
        for h in range(NH):
            q = slice(64 * (h % 2), 64 * (h % 2) + 64)
            load("ac", "small2", SB_[q, h // 2, :], A["sg_b_2"][0, h:h + 1, :].partition_broadcast(64).rearrange("p a n -> p (a n)"))
            got_small = load("ac", "small2", grp[q, h // 2, 64 * (h % 2):64 * (h % 2) + 64], A["pool_w_2"][0, h, :, :])

        need("pe", got_mem)
        for k2 in range(4):
            b = banks.take()
            for k in range(2):
                for m in range(2):
                    mm = pe.transpose(psum[b][:, (2 * k + m) * P:(2 * k + m + 1) * P], XP[:, m, (2 * k2 + k) * P:(2 * k2 + k + 1) * P], ident[:, :])
            t = up("pe", mm)
            e = either()
            need(e, t)
            banks.freed(b, evacuate(e, memT[:, 2 * k2:2 * k2 + 2, :], psum[b][:, :].rearrange("p (k n) -> p k n", k=2)))
        s, w, got = ring2.fetch(cols8, A["w_kv_2"].rearrange("o (k p) n -> p (o k) n", p=P))
        need("pe", got, g.now("ac"), g.now("ve"))
        for tile in range(2):
            b = banks.take()
            for k in range(KD):
                mm = pe.matmul(psum[b][:, 0:MEM], w[:, k, tile * P:(tile + 1) * P], memT[:, k, :], start=k == 0, stop=k == KD - 1)
            t = up("pe", mm)
            need("ac", t)
            banks.freed(b, evacuate("ac", K2T[:, tile, :], psum[b][:, 0:MEM]))
        for m in range(2):
            b = banks.take()
            for k in range(KD):
                mm = pe.matmul(psum[b][:, 0:DG], memT[:, k, m * P:(m + 1) * P], w[:, k, DG:2 * DG], start=k == 0, stop=k == KD - 1)
            t = up("pe", mm)
            need("ac", t)
            banks.freed(b, evacuate("ac", V2[:, m, :], psum[b][:, 0:DG]))
        ring2.used(s, t)
        mem_ready = g.now("ac")
        zero_xp = up("po", po.memset(XP[:, :, 0:16], 0.0)) if not need("po", t) else None

        need("ve", got_small)
        for h in range(NH):
            t = up("ve", ve.tensor_tensor(sgw[:, h, :], sgw[:, h, :], tril[:, :], ALU.mult))
        need("pe", t)
        b = banks.take()
        for h in range(NH):
            mm = pe.transpose(psum[b][:, h * P:(h + 1) * P], sgw[:, h, :], ident[:, :])
        t = up("pe", mm)
        need("ve", t)
        wt_ready = evacuate("ve", WT[:, :, :], psum[b][:, :].rearrange("p (h n) -> p h n", h=NH))
        banks.freed(b, wt_ready)

        s, w, got = ring2.fetch(cols8, w_in2_v[:, :, 1536:2048])
        need("pe", got)
        tm_free = [None, None, None]
        for tile in range(2):
            def sig_g(bank, hs, t, tile=tile):
                need("ac", t)
                return up("ac", ac.activation(CV[:, tile, hs], bank[:, :], ACT.Sigmoid))
            project2(w, DG + tile * P, sig_g)

            def a_times(bank, hs, t, tile=tile):
                need("ve", t, g.now("ac"), zeros)
                return up("ve", ve.tensor_tensor(HP[:, tile, CONV_D - 1 + hs.start:CONV_D - 1 + hs.stop], bank[:, :], CV[:, tile, hs], ALU.mult))
            last = project2(w, tile * P, a_times)
        ring2.used(s, last)
        hp_ready = g.now("ve")
        conv_t = [hp_ready, hp_ready]

        def conformer_taps(first, last_):
            for n in range(first, last_):
                for tile in range(2):
                    wc = col3[:, P3["dw"] + 2 * n + tile:P3["dw"] + 2 * n + tile + 1]
                    src = HP[:, tile, n:n + T]
                    need("ve", conv_t[tile])
                    if n == 0:
                        bias = col3[:, P3["dw_b"] + tile:P3["dw_b"] + tile + 1]
                        conv_t[tile] = up("ve", ve.tensor_scalar(CV[:, tile, :], src, wc, bias, ALU.mult, ALU.add))
                    else:
                        conv_t[tile] = up("ve", ve.scalar_tensor_tensor(CV[:, tile, :], src, wc, CV[:, tile, :], ALU.mult, ALU.add))

        sA, wA, gotA = ring2.fetch(cols8, w_in2_v[:, :, 0:512])
        sB, wB, gotB = ring2.fetch(cols8, w_in2_v[:, :, 512:1024])
        need("pe", gotA)

        def copy_to(dst, e="ac", func=None):
            def finish(bank, hs, t):
                need(e, t)
                return evacuate(e, dst(hs), bank[:, :], func=func)
            return finish

        need("ac", zero_xp)
        for tile in range(2):
            project2(wA, tile * P, copy_to(lambda hs: XP[:, tile, 16 + hs.start:16 + hs.stop]))
        for tile in range(2):
            last = project2(wA, DG + tile * P, copy_to(lambda hs: HT[:, tile, hs]))
        ring2.used(sA, last)
        conformer_taps(0, 6)
        need("pe", gotB)
        for tile in range(2):
            def times_x(bank, hs, t, tile=tile):
                need("ve", t, g.now("ac"))
                o = XP[:, tile, 16 + hs.start:16 + hs.stop]
                return up("ve", ve.tensor_tensor(o, bank[:, :], o, ALU.mult))
            project2(wB, tile * P, times_x)
        ca_ready = g.now("ve")
        for tile in range(2):
            last = project2(wB, DG + tile * P, copy_to(lambda hs: HT[:, 2 + tile, hs], func=ACT.Gelu_apprx_tanh))
        ring2.used(sB, last)
        u_ready = g.now("ac")
        need("ve", ca_ready)
        acc_a = VG[:, :, :].rearrange("p (a b) n -> p a (b n)", a=2)
        for tile in range(2):
            for n in range(CONV_A):
                wc = col3[:, P3["conv_a"] + 2 * n + tile:P3["conv_a"] + 2 * n + tile + 1]
                src = XP[:, tile, 14 + n:14 + n + T]
                if n == 0:
                    t = up("ve", ve.tensor_scalar(acc_a[:, tile, :], src, wc, None, ALU.mult))
                else:
                    need("ve", t)
                    t = up("ve", ve.scalar_tensor_tensor(acc_a[:, tile, :], src, wc, acc_a[:, tile, :], ALU.mult, ALU.add))
            need("ve", t, u_ready)
            ya_ready = up("ve", ve.tensor_tensor(HT[:, tile, :], HT[:, tile, :], acc_a[:, tile, :], ALU.mult))

        s, w, got = ring2.fetch(cols8, w_in2_v[:, :, 1024:1536])
        need("pe", got)
        need("ac", ya_ready)
        for j in range(TT):
            b = banks.take()
            for k in range(KD):
                mm = pe.matmul(psum[b][:, 0:DG], XFT[:, k, j * P:(j + 1) * P], w[:, k, 0:DG], start=k == 0, stop=k == KD - 1)
            t = up("pe", mm)
            need("ac", t)
            banks.freed(b, up("ac", ac.activation(VG[:, j, :], psum[b][:, 0:DG], ACT.Gelu_apprx_tanh)))
        v_ready = g.now("ac")
        for tile in range(2):
            last = project2(w, DG + tile * P, copy_to(lambda hs: XC[:, tile, 16 + hs.start:16 + hs.stop]))
        ring2.used(s, last)
        xc_ready = g.now("ac")
        conformer_taps(6, 14)
        need("ve", v_ready)
        for j in range(TT):
            t = up("ve", ve.bn_stats(stats[:, j, :], VG[:, j, :]))
        need("ve", t)
        for j in range(TT):
            t = up("ve", ve.bn_aggr(mv[:, j, :], stats[:, j, :]))
        need("ve", t)
        t = up("ve", ve.tensor_scalar(sd[:, :, :], mv[:, :, 1:2], LN_EPS, None, ALU.add))
        need("ac", t)
        t = up("ac", ac.activation(sd[:, :, :], sd[:, :, :], ACT.Sqrt))
        need("ve", t)
        t = up("ve", ve.reciprocal(sd[:, :, :], sd[:, :, :]))
        need("ve", t)
        for j in range(TT):
            t = up("ve", ve.tensor_scalar(VG[:, j, :], VG[:, j, :], mv[:, j, 0:1], sd[:, j, :], ALU.subtract, ALU.mult))
        need("po", t, got_small)
        for j in range(TT):
            t = up("po", po.tensor_tensor(VG[:, j, :], VG[:, j, :], lng[:, 0, :], ALU.mult))
            need("po", t)
            vn_ready = up("po", po.tensor_tensor(VG[:, j, :], VG[:, j, :], lng[:, 1, :], ALU.add))
        need("pe", vn_ready, wt_ready)
        for pair in range(2):
            for quad in range(2):
                for hh in range(2):
                    b = banks.take()
                    for j in range(4):
                        mm = pe.matmul(psum[b][:, j * P:(j + 1) * P], VG[:, 4 * quad + j, pair * P:(pair + 1) * P], WT[:, 2 * pair + hh, :], start=True, stop=True)
                    t = up("pe", mm)
                    q = slice(64 * hh, 64 * hh + 64)
                    hs = slice(quad * 512, (quad + 1) * 512)
                    need("ve", t, u_ready)
                    as_chunks = lambda x: x.rearrange("p (c n) -> p c n", c=4)
                    t = up("ve", ve.tensor_tensor(as_chunks(tm[0][q, :]), as_chunks(psum[b][q, :]), SB_[q, pair:pair + 1, :].to_broadcast([64, 4, P]), ALU.add))
                    banks.freed(b, t)
                    need("ve", t)
                    yb_ready = up("ve", ve.tensor_tensor(HT[q, 2 + pair, hs], HT[q, 2 + pair, hs], tm[0][q, :], ALU.mult))

        need("ve", xc_ready)
        t = up("ve", ve.tensor_copy(HT[:, 4:6, :], XC[:, :, 16:16 + T]))
        up("ve", ve.memset(XP[:, :, 0:16], 0.0))
        need("ve", g.now("ve"))
        src, dst = XC, XP
        for n in range(4):
            shift = 1 << n
            t = up("ve", ve.tensor_tensor(dst[:, :, 16:16 + T], src[:, :, 16:16 + T], src[:, :, 16 - shift:16 - shift + T], ALU.add))
            need("ve", t)
            q, tile = slice(64 * (n % 2), 64 * (n % 2) + 64), n // 2
            t = up("ve", ve.tensor_tensor(dst[q, tile, 16:32], dst[q, tile, 16:32], fix[q, tile, :], ALU.mult))
            need("ve", t)
            t = up("ve", ve.scalar_tensor_tensor(HT[q, 4 + tile, :], dst[q, tile, 16:16 + T], invw[q, tile:tile + 1], HT[q, 4 + tile, :], ALU.mult, ALU.subtract))
            need("ve", t)
            src, dst = dst, src
        need("pe", t)
        for tile in range(2):
            for half in range(2):
                hs = slice(half * 512, (half + 1) * 512)
                b = banks.take()
                t = up("pe", pe.matmul(psum[b][:, :], grp[:, tile, :], HT[:, 4 + tile, hs], start=True, stop=True))
                need("ac", t)
                yc_ready = up("ac", ac.activation(HT[:, 4 + tile, hs], psum[b][:, :], ACT.Identity, scale=col3[:, P3["pool_scale"] + tile:P3["pool_scale"] + tile + 1]))
                banks.freed(b, yc_ready)

        s, w, got = ring2.fetch(cols8, w_in2_v[:, :, 2048:2560])
        need("pe", got)
        for tile in range(2):
            project2(w, tile * P, copy_to(lambda hs: HT[:, 8 + tile, hs]))
        q_ready = g.now("ac")
        conformer_taps(14, CONV_D)

        gate_tiles = {}
        gate_blocks = [(s, w, 2, 2)]
        qc = st.sb("attn_q", [P, 2, P])
        pr = [st.sb(f"attn_p{n}", [P, 2, MEM]) for n in range(2)]
        prT = [st.sb(f"attn_pT{n}", [P, 4, P]) for n in range(2)]
        mx = st.sb("attn_max", [P, 4, 1])
        sm = st.sb("attn_sum", [P, 4, 1])
        need("pe", mem_ready)
        need("ac", q_ready)
        all_engines_meet()

        def attend(j):
            need("ac", g.before("pe"))
            qc_t = up("ac", ac.copy(qc[:, :, :], HT[:, 8:10, bass.ds(j * P, P)]))
            s_t, e_t = [], []
            need("pe", qc_t, g.before("ve"))
            for pair in range(2):
                for hh in range(2):
                    q = slice(64 * hh, 64 * hh + 64)
                    mm = pe.matmul(psum[2 * hh + pair][:, 0:MEM], qc[q, pair, :], K2T[q, pair, :], start=True, stop=True)
                s_t.append(up("pe", mm))
            for pair in range(2):
                need("ve", s_t[pair])
                m2 = mx[:, 2 * pair:2 * pair + 2, :]
                for hh in range(2):
                    t = up("ve", ve.tensor_reduce(m2[:, hh, :], psum[2 * hh + pair][:, 0:MEM], X, ALU.max))
                need("ve", t)
                t = up("ve", ve.tensor_scalar(m2, m2, -0.125, None, ALU.mult))
                need("ac", t)
                for hh in range(2):
                    h = 2 * pair + hh
                    t = up("ac", ac.activation(pr[pair][:, hh, :], psum[2 * hh + pair][:, 0:MEM], ACT.Exp, scale=0.125, bias=mx[:, h, :], accum_out=sm[:, h, :]))
                need("ve", t)
                s2 = sm[:, 2 * pair:2 * pair + 2, :]
                t = up("ve", ve.reciprocal(s2, s2))
                need("ve", t)
                t = up("ve", ve.tensor_tensor(pr[pair][:, :, :], pr[pair][:, :, :], s2.to_broadcast([P, 2, MEM]), ALU.mult))
                e_t.append(t)
            for pair in range(2):
                need("pe", e_t[pair])
                for n in range(4):
                    mm = pe.transpose(psum[4 + pair][:, n * P:(n + 1) * P], pr[pair][:, n // 2, (n % 2) * P:(n % 2 + 1) * P], ident[:, :])
                t = up("pe", mm)
                need("ac", t)
                t = up("ac", ac.copy(prT[pair][:, :, :], psum[4 + pair][:, :].rearrange("p (n l) -> p n l", n=4)))
                need("pe", t)
                for hh in range(2):
                    for m in range(2):
                        mm = pe.matmul(psum[6 + pair][:, hh * P:(hh + 1) * P], V2[:, m, pair * P:(pair + 1) * P], prT[pair][:, 2 * hh + m, :], start=m == 0, stop=m == 1)
                t = up("pe", mm)
                need("ve", t)
                for hh in range(2):
                    q = slice(64 * hh, 64 * hh + 64)
                    t = up("ve", ve.tensor_copy(HT[q, 8 + pair, bass.ds(j * P, P)], psum[6 + pair][q, hh * P:(hh + 1) * P]))

        g.loop(TT, {"pe_done": 6, "ve_done": 14, "ac_done": 7}, attend)
        all_engines_meet()
        tap("K2T", K2T[:, :, :])

        need("pe", *conv_t)
        for half in range(2):
            hs = slice(half * 512, (half + 1) * 512)
            b = banks.take()
            for tile in range(2):
                mm = pe.matmul(psum[b][:, :], ones[:, :], CV[:, tile, hs], start=tile == 0, stop=tile == 1)
            t = up("pe", mm)
            need("ve", t)
            for tile in range(2):
                t = up("ve", ve.scalar_tensor_tensor(CV[:, tile, hs], psum[b][:, :], -1.0 / DG, CV[:, tile, hs], ALU.mult, ALU.add))
            banks.freed(b, t)
            need("ac", t)
            for tile in range(2):
                t = up("ac", ac.activation(HP[:, tile, hs], CV[:, tile, hs], ACT.Square))
            need("pe", t)
            b = banks.take()
            for tile in range(2):
                mm = pe.matmul(psum[b][:, :], ones[:, :], HP[:, tile, hs], start=tile == 0, stop=tile == 1)
            t = up("pe", mm)
            need("ve", t)
            t = up("ve", ve.tensor_scalar(tm[0][:, :], psum[b][:, :], 1.0 / DG, LN_EPS, ALU.mult, ALU.add))
            banks.freed(b, t)
            need("ac", t)
            t = up("ac", ac.activation(tm[0][:, :], tm[0][:, :], ACT.Sqrt))
            need("ve", t)
            t = up("ve", ve.reciprocal(tm[0][:, :], tm[0][:, :]))
            need("ve", t)
            for tile in range(2):
                t = up("ve", ve.tensor_tensor(CV[:, tile, hs], CV[:, tile, hs], tm[0][:, :], ALU.mult))
            need("ac", t)
            for tile in range(2):
                t = up("ac", ac.activation(CV[:, tile, hs], CV[:, tile, hs], ACT.Silu, scale=col3[:, P3["cc_g"] + tile:P3["cc_g"] + tile + 1], bias=col3[:, P3["cc_b"] + tile:P3["cc_b"] + tile + 1]))
            need("pe", t, got_small)
            for tile in range(2):
                b = banks.take()
                for k in range(2):
                    mm = pe.matmul(psum[b][:, :], pw[:, k, tile * P:(tile + 1) * P], CV[:, k, hs], start=k == 0, stop=k == 1)
                t = up("pe", mm)
                need("ac", t)
                banks.freed(b, evacuate("ac", HT[:, 6 + tile, hs], psum[b][:, :]))
        all_engines_meet()
        tap("HT", HT[:, :, :])

        n = 0
        free = [None] * 3
        for c0 in (2048, 2560, 3072):
            if c0 > 2048:
                s, w, got = ring2.fetch(cols8, w_in2_v[:, :, c0:c0 + 512])
                need("pe", got)
            for jj in range(2 if c0 == 2048 else 0, 4):
                tile = (c0 - 2304) // P + jj

                def gated(bank, hs, t, tile=tile):
                    global_n = tile * 2 + hs.start // 512
                    buf = tm[global_n % 3]
                    need("ac", t, free[global_n % 3])
                    r = up("ac", ac.activation(buf[:, :], bank[:, :], ACT.Silu))
                    need("ve", r)
                    free[global_n % 3] = up("ve", ve.tensor_tensor(HT[:, tile, hs], HT[:, tile, hs], buf[:, :], ALU.mult))
                    return r
                last = project2(w, jj * P, gated)
            ring2.used(s, last)
        ht_ready = g.now("ve")
    all_engines_meet()

    with Scope() as st:
        XR = st.sb("residual", [P, TT, D])
        lnr = st.sb("ln_rows", [P, 2, D])
        stats = st.sb("ln_stats", [P, TT, 2, 6])
        mv = st.sb("ln_mv", [P, TT, 2])
        sd = st.sb("ln_sd", [P, TT, 1])
        got_xr = load("ac", "residual", XR[:, :, :], xf_rows.rearrange("(t p) n -> p t n", p=P))
        load("ac", "ln_rows", lnr[:, 0, :], A["ln_g_2"].partition_broadcast(P).rearrange("p a n -> p (a n)"))
        got_ln = load("ac", "ln_rows", lnr[:, 1, :], A["ln_b_2"].partition_broadcast(P).rearrange("p a n -> p (a n)"))
        w_out2_v = A["w_out_2"].rearrange("o (k p) n -> p (o k) n", p=P)
        halves = [ring2.fetch(cols10, w_out2_v[:, :, half * 512:(half + 1) * 512]) for half in range(2)]
        need("pe", ht_ready)
        need("ve", got_xr)
        out_rows = out.rearrange("b (t p) n -> p (b t) n", p=P)
        for half, (s, w, got) in enumerate(halves):
            need("pe", got)
            hs = slice(half * 512, (half + 1) * 512)
            for j in range(TT):
                b = banks.take()
                for k in range(NMIX):
                    mm = pe.matmul(psum[b][:, :], HT[:, k, j * P:(j + 1) * P], w[:, k, :], start=k == 0, stop=k == NMIX - 1)
                t = up("pe", mm)
                need("ve", t)
                t = up("ve", ve.scalar_tensor_tensor(XR[:, j, hs], XR[:, j, hs], ALPHA, psum[b][:, :], ALU.mult, ALU.add))
                banks.freed(b, t)
                need("ve", t)
                t = up("ve", ve.bn_stats(stats[:, j, half, :], XR[:, j, hs]))
                if half:
                    need("ve", t)
                    t = up("ve", ve.bn_aggr(mv[:, j, :], stats[:, j, :, :].rearrange("p a b -> p (a b)")))
                    need("ve", t)
                    t = up("ve", ve.tensor_scalar(sd[:, j, :], mv[:, j, 1:2], LN_EPS, None, ALU.add))
                    need("ac", t)
                    t = up("ac", ac.activation(sd[:, j, :], sd[:, j, :], ACT.Sqrt))
                    need("ve", t)
                    t = up("ve", ve.reciprocal(sd[:, j, :], sd[:, j, :]))
                    need("ve", t)
                    t = up("ve", ve.tensor_scalar(XR[:, j, :], XR[:, j, :], mv[:, j, 0:1], sd[:, j, :], ALU.subtract, ALU.mult))
                    need("po", t, got_ln)
                    t = up("po", po.tensor_tensor(XR[:, j, :], XR[:, j, :], lnr[:, 0, :], ALU.mult))
                    need("po", t)
                    t = up("po", po.tensor_tensor(XR[:, j, :], XR[:, j, :], lnr[:, 1, :], ALU.add))
                    need("sp", t)
                    stored_out = load("sp", "out_stored", out_rows[:, j, :], XR[:, j, :])
        need("sp", stored_out)
    two.__exit__()
    top.__exit__()


INPUTS = [
    "x", "c", "ctx", "c_ctx", "w_ada", "b_ada", "g_norm1", "w_in", "b_gates", "w_conv", "w_fourier",
    "w_mlstm", "w_out", "g_norm2", "w_router", "w_gate_e", "w_up_e", "w_down_e", "g_final", "mem_2",
    "w_in_2", "conv_a_w_2", "sg_ln_g_2", "sg_ln_b_2", "sg_w_2", "sg_b_2", "pool_w_2", "pool_scale_2",
    "cc_dw_w_2", "cc_dw_b_2", "cc_ln_g_2", "cc_ln_b_2", "cc_pw_w_2", "w_kv_2", "w_out_2", "ln_g_2", "ln_b_2",
]


def constants():
    j = np.arange(P)
    tri = np.zeros((P, 2, P), np.float32)
    tri[:, 0, :] = np.where(j[:, None] <= j[None, :], 0.0, MASKED)
    tri[:, 1, :] = np.where(j[:, None] >= j[None, :], 0.0, MASKED)
    sel = np.zeros((32, 8, P), np.float32)
    for r in range(8):
        sel[r, r, :] = 1.0
    reset = np.ones((36, TA), np.float32)
    reset[0:4, 0::P] = 0.0
    reset[32:36, P - 1::P] = 0.0
    norm = 1.0 / math.sqrt(T * P)
    ang = 2 * np.pi * np.outer(j, j) / P
    channels = np.concatenate([np.cos(ang), np.sin(ang)], 1) * norm
    n = np.arange(512)
    angt = 2 * np.pi * (np.outer(n, n) % T) / T
    fix = np.ones((P, 2, 16), np.float32)
    inv = np.ones((P, 2), np.float32)
    for grp, w in enumerate((2, 4, 8, 16)):
        q = slice(64 * (grp % 2), 64 * (grp % 2) + 64)
        inv[q, grp // 2] = 1.0 / w
        for t in range(16):
            fix[q, grp // 2, t] = w / min(t + 1, w)
    return {
        "ident": np.eye(P, dtype=np.float32), "mask": tri, "sel": sel, "reset": reset,
        "dft_channels": channels.astype(np.float32), "dft_cos": np.cos(angt).astype(np.float32),
        "dft_sin": np.sin(angt).astype(np.float32),
        "alternating": np.where(n % 2 == 0, 1.0, -1.0).astype(np.float32)[None, :],
        "tril": np.tril(np.ones((P, P), np.float32)), "pool_fix": fix, "pool_inv": inv,
    }


def kernel(**inputs):
    import concourse.bacc as _bacc
    from concourse.bass_utils import run_bass_kernel_spmd as _run

    nc = _bacc.Bacc("TRN2", target_bir_lowering=False, num_devices=1)
    arrays = {f"in_{k}": np.ascontiguousarray(inputs[k]) for k in INPUTS}
    consts = {f"const_{k}": v for k, v in constants().items()}
    arrays.update(consts)
    aps = {k: nc.dram_tensor(k, a.shape, mybir.dt.from_np(a.dtype), kind="ExternalInput").ap() for k, a in arrays.items()}
    A = {k: aps[f"in_{k}"] for k in INPUTS}
    C = {k[6:]: aps[k] for k in consts}
    out = nc.dram_tensor("out", (1, T, D), F32, kind="ExternalOutput").ap()
    scratch = {k: nc.dram_tensor(f"{k}_rows", (T, D), F32, kind="Internal").ap() for k in ("xn", "x2", "xf")}
    build(nc, A, C, out, scratch)
    r = _run(nc, [arrays], core_ids=[0])
    return r.results[0]["out"]
```

```python
import math

import numpy as np

import concourse.bass as bass
from concourse import mybir

F32 = mybir.dt.float32
F32R = mybir.dt.float32r
U32 = mybir.dt.uint32
ALU = mybir.AluOpType
ACT = mybir.ActivationFunctionType
X = mybir.AxisListType.X

P = 128
D = 1024
KD = D // P
T = 1024
TT = T // P
NCTX = 256
TA = NCTX + T
D_F = 512
D_M = 512
NH = 4
DH = 128
OFF_QK = 512
OFF_V = 1536
OFF_O = 2048
OFF_G = 2560
OFF_BR = 2576
GRID_W = 64
ROWS = T // GRID_W
EPS = 1e-6
LN_EPS = 1e-5
NE = 16
CAP = 128
DG = 256
CONV_D = 31
CONV_A = 3
MEM = 256
DMIX = 1280
ALPHA = 2.0 ** 0.25
MASKED = -1.0e30
BANK = 512


class Flag:

    def __init__(self, nc, name):
        self.sem = nc.alloc_semaphore(name)
        self.name = name
        self.n = 0
        self.base = 0


class Program:

    def __init__(self, nc):
        self.nc = nc
        self.pe, self.ve, self.ac, self.po, self.sp = nc.tensor, nc.vector, nc.scalar, nc.gpsimd, nc.sync
        self.engines = {"pe": self.pe, "ve": self.ve, "ac": self.ac, "po": self.po, "sp": self.sp}
        self.done = {k: Flag(nc, f"{k}_done") for k in ("pe", "ve", "ac", "po")}
        self.met = {}
        self.loop_i = None
        self.loop_per = {}
        self.passed = {k: nc.alloc_semaphore(f"{k}_passed") for k in self.engines}
        self.flags = {f.name: f for f in self.done.values()}

    def flag(self, name):
        if name not in self.flags:
            self.flags[name] = Flag(self.nc, name)
        return self.flags[name]

    def up(self, e, ins):
        f = self.done[e]
        ins.then_inc(f.sem, 1)
        f.n += 1
        return (f, f.n)

    def now(self, e):
        return (self.done[e], self.done[e].n)

    def load(self, e, flag, out, in_, **kw):
        f = self.flag(flag)
        self.engines[e].dma_start(out, in_, **kw).then_inc(f.sem, 16)
        f.n += 16
        return (f, f.n)

    def before(self, flag_or_engine):
        f = self.done.get(flag_or_engine) or self.flag(flag_or_engine)
        return (f, f.base)

    def need(self, e, *ticks):
        register_wait = False
        for tick in ticks:
            if tick is None:
                continue
            f, n = tick[:2]
            carried = len(tick) == 3
            if self.loop_i is not None and f.name in self.loop_per and (carried or n >= f.base):
                self.engines[e].wait_ge(f.sem, n + self.loop_i * self.loop_per[f.name])
                register_wait = True
            elif n > self.met.get((e, f.name), 0):
                self.engines[e].wait_ge(f.sem, n)
                self.met[(e, f.name)] = n
        if register_wait:
            self.engines[e].sem_inc(self.passed[e], 1)

    @staticmethod
    def carry(ticks):
        return {k: v and (v[0], v[1], True) for k, v in ticks.items()}

    def after(self, ticks, count, per):
        return {k: v and (v[0], v[1] + (count - 1) * per[v[0].name]) for k, v in ticks.items()}

    def loop(self, count, per, body):
        flags = {k: self.flag(k) for k in per}
        for f in flags.values():
            f.base = f.n
        start = {k: f.n for k, f in self.flags.items()}
        with self.nc.Fori(0, count) as i:
            self.loop_i, self.loop_per = i, per
            body(i)
            self.loop_i, self.loop_per = None, {}
        grown = {k: f.n - start.get(k, 0) for k, f in self.flags.items()}
        grown = {k: v for k, v in grown.items() if v}
        assert grown == per, f"the loop's turn raises {grown}"
        for f in flags.values():
            f.n = f.base + count * (f.n - f.base)


class Banks:

    def __init__(self, g, tensors):
        self.g = g
        self.t = tensors
        self.last = [None] * len(tensors)
        self.k = 0

    def take(self):
        b = self.k % len(self.t)
        self.k += 1
        self.g.need("pe", self.last[b])
        return b

    def freed(self, b, tick):
        self.last[b] = tick


class Ring:

    def __init__(self, g, name, slots):
        self.g, self.name, self.slots = g, name, slots
        self.busy = [None] * len(slots)
        self.k = 0

    def fetch(self, view, source):
        s = self.k % len(self.slots)
        self.k += 1
        self.g.need("sp", self.busy[s])
        out = view(self.slots[s])
        tick = self.g.load("sp", f"{self.name}_loaded_{s}", out, source)
        return s, out, tick

    def used(self, s, tick):
        self.busy[s] = tick


def build(nc, A, C, out, scratch, taps=None):
    g = Program(nc)
    pe, ve, ac, po, sp = g.pe, g.ve, g.ac, g.po, g.sp
    up, need, load = g.up, g.need, g.load
    psum = [nc.alloc_psum_tensor(f"bank{b}", [P, BANK], F32) for b in range(8)]
    banks = Banks(g, psum)

    class Scope:

        def __enter__(self):
            self.stack = []
            return self

        def sb(self, name, shape, dt=F32):
            cm = nc.sbuf_tensor(name, shape, dt)
            t = cm.__enter__()
            self.stack.append(cm)
            return t

        def __exit__(self, *a):
            while self.stack:
                self.stack.pop().__exit__(None, None, None)

    def all_engines_meet():
        for e in ("pe", "ve", "ac", "po", "sp"):
            need(e, *[g.now(k) for k in ("pe", "ve", "ac", "po") if k != e])

    def tap(name, view):
        if taps is not None and name in taps:
            all_engines_meet()
            need("sp", load("sp", "tap", taps[name], view))
            all_engines_meet()

    turn = [0]

    def evacuate(e, out_, in_, scale=None, bias=None, func=None):
        if e == "ac":
            if func is None and scale is None and bias is None:
                return up("ac", ac.copy(out_, in_))
            kw = {}
            if scale is not None:
                kw["scale"] = scale
            if bias is not None:
                kw["bias"] = bias
            return up("ac", ac.activation(out_, in_, func or ACT.Identity, **kw))
        if scale is None and bias is None:
            return up("ve", ve.tensor_copy(out_, in_))
        if bias is None:
            return up("ve", ve.tensor_scalar(out_, in_, scale, None, ALU.mult))
        return up("ve", ve.tensor_scalar(out_, in_, scale, bias, ALU.mult, ALU.add))

    def either():
        turn[0] += 1
        return "ac" if turn[0] % 2 else "ve"

    top = Scope().__enter__()
    sb = top.sb

    ident = sb("ident", [P, P])
    ones = sb("ones", [P, P])
    load("sp", "constants", ident[:, :], C["ident"])
    ready_ones = up("po", po.memset(ones[:, :], 1.0))
    params1 = sb("params1", [64, P])
    params2 = sb("params2", [72, P])
    params3 = sb("params3", [76, P])
    cond = sb("cond", [16, P])
    rows_of = lambda ap: ap.rearrange("a (r p) -> (a r) p", p=P)
    load("sp", "constants", cond[0:8, :], rows_of(A["c"]))
    load("sp", "constants", cond[8:16, :], A["c_ctx"].rearrange("(r p) -> r p", p=P))
    load("sp", "constants", params1[0:8, :], rows_of(A["g_norm1"]))
    load("sp", "constants", params1[8:16, :], rows_of(A["g_norm2"]))
    load("sp", "constants", params1[16:64, :], rows_of(A["b_ada"]))
    load("sp", "constants", params2[:, :], A["w_conv"].rearrange("o a b (r p) -> (o a b r) p", p=P))
    at = 0
    P3 = {}
    for name, src, n in (
        ("conv_a", A["conv_a_w_2"].rearrange("o k (r p) -> (o k r) p", p=P), 6),
        ("pool_scale", rows_of(A["pool_scale_2"]), 2),
        ("dw", A["cc_dw_w_2"].rearrange("o k (r p) -> (o k r) p", p=P), 62),
        ("dw_b", rows_of(A["cc_dw_b_2"]), 2),
        ("cc_g", rows_of(A["cc_ln_g_2"]), 2),
        ("cc_b", rows_of(A["cc_ln_b_2"]), 2),
    ):
        got_constants = load("sp", "constants", params3[at:at + n, :], src)
        P3[name] = at
        at += n
    col1 = sb("col1", [P, 64])
    col2 = sb("col2", [P, 72])
    col3 = sb("col3", [P, 76])
    silu_c = sb("silu_c", [P, 16])
    silu_rows = sb("silu_rows", [16, P])
    bgates = sb("bgates", [16, 1])
    got_bgates = load("sp", "bgates", bgates[:, :], A["b_gates"].rearrange("o k h -> (k h) o"))
    ga1b = sb("ga1b", [P, D])
    ga2b = sb("ga2b", [P, D])
    got_ga = load("sp", "b_ada_rows", ga1b[:, :], A["b_ada"][:, 2 * D:3 * D].partition_broadcast(P).rearrange("p a n -> p (a n)"))
    got_ga = load("sp", "b_ada_rows", ga2b[:, :], A["b_ada"][:, 5 * D:6 * D].partition_broadcast(P).rearrange("p a n -> p (a n)"))
    mod1 = sb("mod1", [P, 4, KD])
    mod2 = sb("mod2", [P, 2, KD])
    small = sb("small", [P, 64])
    VALC = sb("token_weights", [P, NE])
    IDXC = sb("token_of_slot", [P, NE], U32)

    need("ac", got_constants)
    silu_done = up("ac", ac.activation(silu_rows[:, :], cond[:, :], ACT.Silu))
    need("pe", got_constants, silu_done)
    for src, dst, n in ((silu_rows, silu_c, 16), (params1, col1, 64), (params2, col2, 72), (params3, col3, 76)):
        b = banks.take()
        turned = up("pe", pe.transpose(psum[b][:, 0:n], src[:, :], ident[0:n, 0:n]))
        need("ve", turned)
        columns_ready = evacuate("ve", dst[:, :], psum[b][:, 0:n])
        banks.freed(b, columns_ready)

    w_ada_v = A["w_ada"].rearrange("o (k p) n -> p (o k) n", p=P)
    w_in_v = A["w_in"].rearrange("o (k p) n -> p (o k) n", p=P)

    wslots = [sb(f"wslot{s}", [P, KD * 512]) for s in range(3)]
    blk = Scope().__enter__()
    XT = blk.sb("XT", [P, KD, TA])
    as_cols = lambda s: s[:, :].rearrange("p (k n) -> p k n", k=KD)
    as_rows4 = lambda s: s[:, :].rearrange("p (k n) -> p k n", k=4)
    ring = Ring(g, "w", wslots)

    with Scope() as st:
        xl = st.sb("x_rows", [P, TT, D])
        cl = st.sb("ctx_rows", [P, 2, D])
        junk = st.sb("junk", [P, D])
        ada = st.sb("ada_rows", [2, 2 * D])
        got_x = load("ac", "x_loaded", xl[:, :, :], A["x"].rearrange("b (t p) n -> p (b t) n", p=P))
        got_ctx = load("ac", "ctx_loaded", cl[:, :, :], A["ctx"].rearrange("b (t p) n -> p (b t) n", p=P))

        for blkn in range(4):
            s, w, got = ring.fetch(as_cols, w_ada_v[:, :, blkn * 512:(blkn + 1) * 512])
            b = banks.take()
            need("pe", got, columns_ready)
            for k in range(KD):
                mm = pe.matmul(psum[b][0:2, :], silu_c[:, k:k + 9:8], w[:, k, :], start=k == 0, stop=k == KD - 1)
            t = up("pe", mm)
            ring.used(s, t)
            need("ac", t)
            ada_rows_ready = evacuate("ac", ada[:, blkn * 512:(blkn + 1) * 512], psum[b][0:2, :])
            banks.freed(b, ada_rows_ready)
        b = banks.take()
        need("pe", ada_rows_ready)
        for j in range(16):
            mm = pe.transpose(psum[b][:, 2 * j:2 * j + 2], ada[:, j * P:(j + 1) * P], ident[0:2, 0:2])
        t = up("pe", mm)
        need("ve", t)
        adac = psum[b][:, 0:32].rearrange("p (j v) -> p v j", v=2)
        sh_t = up("ve", ve.tensor_tensor(mod1[:, 1, :], adac[:, 0, 0:8], col1[:, 16:24], ALU.add))
        up("ve", ve.tensor_tensor(mod1[:, 3, :], adac[:, 1, 0:8], col1[:, 16:24], ALU.add))
        up("ve", ve.tensor_tensor(mod1[:, 0, :], adac[:, 0, 8:16], col1[:, 24:32], ALU.add))
        t = up("ve", ve.tensor_tensor(mod1[:, 2, :], adac[:, 1, 8:16], col1[:, 24:32], ALU.add))
        banks.freed(b, t)
        need("ve", t)
        for v in (0, 2):
            mod1_ready = up("ve", ve.scalar_tensor_tensor(mod1[:, v, :], mod1[:, v, :], 1.0, col1[:, 0:8], ALU.add, ALU.mult))

        need("ac", got_x, got_ctx)
        rows = [(xl, j) for j in range(TT)] + [(cl, j) for j in range(2)]
        for n, (src, j) in enumerate(rows):
            squares = up("ac", ac.activation(junk[:, :], src[:, j, :], ACT.Square, accum_out=small[:, n:n + 1]))
            need("ac", squares)
        need("ve", squares)
        t = up("ve", ve.tensor_scalar(small[:, 16:26], small[:, 0:10], 1.0 / D, EPS, ALU.mult, ALU.add))
        need("ac", t)
        t = up("ac", ac.activation(small[:, 32:42], small[:, 16:26], ACT.Sqrt))
        need("ve", t)
        t = up("ve", ve.reciprocal(small[:, 48:58], small[:, 32:42]))
        need("ve", t)
        for n, (src, j) in enumerate(rows):
            rows_scaled = up("ve", ve.tensor_scalar(src[:, j, :], src[:, j, :], small[:, 48 + n:49 + n], None, ALU.mult))

        need("pe", rows_scaled)
        for k in range(KD):
            for src, j0, nj, col, v in ((cl, 0, 2, 0, 2), (xl, 0, 4, NCTX, 0), (xl, 4, 4, NCTX + 512, 0)):
                b = banks.take()
                for j in range(nj):
                    mm = pe.transpose(psum[b][:, j * P:(j + 1) * P], src[:, j0 + j, k * P:(k + 1) * P], ident[:, :])
                t = up("pe", mm)
                e = either()
                need(e, t, mod1_ready)
                t = evacuate(e, XT[:, k, col:col + nj * P], psum[b][:, 0:nj * P], mod1[:, v, k:k + 1], mod1[:, v + 1, k:k + 1])
                banks.freed(b, t)
    XT_ready = [g.now("ac"), g.now("ve")]
    all_engines_meet()
    tap("XT", XT[:, :, :])

    spans = ((0, 256), (256, 512), (768, 512))

    def project_transposed(w, c0, column_spans, finish, m=P):
        last = None
        for c, n in column_spans:
            b = banks.take()
            for k in range(KD):
                mm = pe.matmul(psum[b][0:m, 0:n], w[:, k, c0:c0 + m], XT[:, k, c:c + n], start=k == 0, stop=k == KD - 1)
            last = up("pe", mm)
            banks.freed(b, finish(psum[b], c, n, last))
        return last

    mix = Scope().__enter__()
    H = mix.sb("H", [P, TT, D_M])
    lstm = Scope().__enter__()
    KT = lstm.sb("KT", [P, NH, TA])
    QT = lstm.sb("QT", [P, NH, T])
    V = lstm.sb("V", [P, TA // P, NH, DH + 1])
    ones_col = up("po", po.memset(V[:, :, :, DH:DH + 1], 1.0))

    COL = lstm.sb("COL", [P, TA // P, 32])
    NC = TA // P

    with Scope() as st:
        grid = [st.sb(f"grid{i}", [P, (ROWS + 2) * (GRID_W + 2)]) for i in range(2)]
        gctx = [st.sb(f"gctx{i}", [P, NCTX + 2]) for i in range(2)]
        cacc = st.sb("conv_acc", [P, T])
        cacc2 = st.sb("conv_acc_ctx", [P, NCTX])
        in_H = lambda r, n: H[0:r, :, :].rearrange("p a b -> p (a b)")[:, n * TA:(n + 1) * TA]
        G = in_H(16, 0)
        M = in_H(36, 2)
        WA = in_H(36, 0)
        RS = in_H(36, 1)
        IG = st.sb("IG", [36, TA])
        FL = st.sb("FL", [36, TA])
        CU = st.sb("CU", [36, TA])
        R = CU[0:32, :]
        m0 = st.sb("m0", [36, NC, 1])
        lnscale = st.sb("lnscale", [36, 1])
        wg = st.sb("w_gates", [P, KD, 16])
        got_wg = load("sp", "w_gates", wg[:, :, :], w_in_v[:, :, OFF_G:OFF_BR])
        got_rs = load("sp", "reset", RS[:, :], C["reset"])
        up("po", po.memset(lnscale[:, :], 0.5 * math.log(DH)))
        zeroed = [up("po", po.memset(x[:, :], 0.0)) for x in (IG, FL, CU, M)][-1]
        zero = [up("po", po.memset(x[:, :], 0.0)) for x in grid + gctx][-1]
        need("pe", got_wg, *XT_ready)

        def gate_rows(bank, c, n, t):
            need("ac", t, got_bgates)
            return evacuate("ac", G[:, c:c + n], bank[0:16, 0:n], bias=bgates[:, 0:1])

        project_transposed(wg[:, :, :], 0, spans, gate_rows, m=16)
        gates_done = g.now("ac")

        def gate_steps():
            need("sp", gates_done, zeroed)
            for d in range(2):
                got_gates = load("sp", "gate_rows", IG[32 * d:32 * d + 4, :], G[8 * d:8 * d + 4, :])
                got_gates = load("sp", "gate_rows", FL[32 * d:32 * d + 4, :], G[8 * d + 4:8 * d + 8, :])
            need("ve", got_gates, got_rs)
            t = up("ve", ve.scalar_tensor_tensor(WA[:, :], FL[:, :], -1.0, FL[:, :], ALU.mult, ALU.max))
            yield
            need("ac", t)
            t = up("ac", ac.activation(WA[:, :], WA[:, :], ACT.Exp, scale=-1.0))
            need("ac", t)
            t = up("ac", ac.activation(WA[:, :], WA[:, :], ACT.Ln, bias=1.0))
            need("ve", t)
            t = up("ve", ve.scalar_tensor_tensor(FL[:, :], FL[:, :], 0.0, WA[:, :], ALU.min, ALU.subtract))
            need("ve", t)
            forward = (slice(0, TA, 1),)
            backward = (slice(NCTX - 1, None, -1), slice(TA - 1, NCTX - 1, -1))
            for d, pieces in enumerate((forward, backward)):
                q = slice(32 * d, 32 * d + 4)
                state = 0.0
                for piece in pieces:
                    up("ve", ve.tensor_tensor_scan(CU[q, piece], RS[q, piece], FL[q, piece], 0.0, ALU.mult, ALU.add))
                    t = up("ve", ve.tensor_tensor_scan(M[q, piece], FL[q, piece], IG[q, piece], state, ALU.add, ALU.max))
                    need("ve", t)
                    state = M[q, 0:1]
            scans = t
            chunked = lambda x, q: x[q, :].rearrange("r (c j) -> r c j", j=P)
            t = up("ve", ve.memset(m0[:, :, :], 0.0))
            need("ve", scans, t)
            mf, mb = chunked(M, slice(0, 4)), chunked(M, slice(32, 36))
            up("ve", ve.tensor_copy(m0[0:4, 1:NC, :], mf[:, 0:NC - 1, P - 1:P]))
            up("ve", ve.tensor_copy(m0[32:36, 0:1, :], mb[:, 1:2, 0:1]))
            up("ve", ve.tensor_copy(m0[32:36, 2:NC - 1, :], mb[:, 3:NC, 0:1]))
            t = up("ve", ve.tensor_copy(m0[32:36, NC - 1:NC, :], mb[:, 0:1, 0:1]))
            need("ve", t)
            q = slice(0, 36)
            m0b = m0[:, :, :].to_broadcast([36, NC, P])
            up("ve", ve.tensor_tensor(IG[:, :], IG[:, :], CU[:, :], ALU.subtract))
            t = up("ve", ve.tensor_tensor(FL[:, :], CU[:, :], M[:, :], ALU.subtract))
            need("ve", t)
            up("ve", ve.tensor_tensor(chunked(IG, q), chunked(IG, q), m0b, ALU.subtract))
            t = up("ve", ve.tensor_tensor(chunked(FL, q), chunked(FL, q), m0b, ALU.add))
            need("ve", t)
            for q, end in ((slice(0, 4), P - 1), (slice(32, 36), 0)):
                lasts = chunked(FL, q)[:, :, end:end + 1].to_broadcast([4, NC, P])
                wa_t = up("ve", ve.tensor_tensor(chunked(WA, q), chunked(IG, q), lasts, ALU.add))
            need("sp", t)
            for d in range(2):
                tk_gates["ld_stored"] = load("sp", "ld_stored", ld_rows[4 * d:4 * d + 4, :], FL[32 * d:32 * d + 4, :])
            yield
            yield
            need("ac", t, zeroed)
            up("ac", ac.activation(M[:, :], M[:, :], ACT.Exp, scale=-1.0, bias=lnscale[:, 0:1]))
            need("ac", wa_t)
            t = up("ac", ac.activation(WA[:, :], WA[:, :], ACT.Exp))
            need("sp", t, g.now("ve"))
            for n, src in enumerate((FL, IG, WA, M)):
                for d in range(2):
                    tk_gates["packed"] = load("sp", "packed", R[8 * n + 4 * d:8 * n + 4 * d + 4, :], src[32 * d:32 * d + 4, :])

        tk_gates = {}
        ld_rows = scratch["ld"]

        s, w, got = ring.fetch(as_cols, w_in_v[:, :, OFF_V:OFF_V + 512])
        need("pe", got)
        qk_blocks = [ring.fetch(as_cols, w_in_v[:, :, OFF_QK + blkn * 512:OFF_QK + (blkn + 1) * 512]) for blkn in range(2)]
        steps = gate_steps()
        for j in range(TA // P):
            b = banks.take()
            for k in range(KD):
                mm = pe.matmul(psum[b][:, :], XT[:, k, j * P:(j + 1) * P], w[:, k, :], start=k == 0, stop=k == KD - 1)
            last = up("pe", mm)
            need("ac", last)
            v_ready = evacuate("ac", V[:, j, :, 0:DH], psum[b][:, :].rearrange("p (h n) -> p h n", h=NH))
            banks.freed(b, v_ready)
            if j > 0:
                next(steps, None)
        packed = tk_gates["packed"]
        need("sp", packed)
        need("pe", packed)
        b = banks.take()
        for c in range(NC):
            mm = pe.transpose(psum[b][:, 32 * c:32 * c + 32], R[:, c * P:(c + 1) * P], ident[0:32, 0:32])
        t = up("pe", mm)
        need("ve", t, packed)
        col_ready = evacuate("ve", COL[:, :, :], psum[b][:, 0:32 * NC].rearrange("p (c r) -> p c r", r=32))
        banks.freed(b, col_ready)

        conv_read = [None, None]
        silu_read = None
        for blkn in range(2):
            s, w, got = qk_blocks[blkn]
            need("pe", got)
            for h in range(NH):
                tile = blkn * 4 + h
                pad = grid[tile % 2][:, :].rearrange("p (r w) -> p r w", w=GRID_W + 2)
                cpad = gctx[tile % 2]

                def into_grid(bank, c, n, t, pad=pad, cpad=cpad):
                    need("ac", t, zero, conv_read[tile % 2])
                    if c == 0:
                        return evacuate("ac", cpad[:, 1:NCTX + 1], bank[:, 0:n])
                    r = (c - NCTX) // GRID_W
                    return evacuate("ac", pad[:, 1 + r:9 + r, 1:GRID_W + 1], bank[:, :].rearrange("p (r w) -> p r w", w=GRID_W))

                last = project_transposed(w, h * P, spans if blkn else spans[1:], into_grid)
                got_grid = g.now("ac")
                o = cacc[:, :].rearrange("p (r w) -> p r w", w=GRID_W)
                need("ve", got_grid, silu_read)
                for n in range(9):
                    src = pad[:, n // 3:n // 3 + ROWS, n % 3:n % 3 + GRID_W]
                    wc = col2[:, n * 8 + tile:n * 8 + tile + 1]
                    if n == 0:
                        t = up("ve", ve.tensor_scalar(o, src, wc, None, ALU.mult))
                    else:
                        need("ve", t)
                        t = up("ve", ve.scalar_tensor_tensor(o, src, wc, o, ALU.mult, ALU.add))
                if blkn:
                    for n in range(3):
                        src = cpad[:, n:n + NCTX]
                        wc = col2[:, (3 + n) * 8 + tile:(3 + n) * 8 + tile + 1]
                        if n == 0:
                            t = up("ve", ve.tensor_scalar(cacc2[:, :], src, wc, None, ALU.mult))
                        else:
                            need("ve", t)
                            t = up("ve", ve.scalar_tensor_tensor(cacc2[:, :], src, wc, cacc2[:, :], ALU.mult, ALU.add))
                conv_read[tile % 2] = t
                need("ac", t)
                if blkn:
                    up("ac", ac.activation(KT[:, h, NCTX:TA], cacc[:, :], ACT.Silu))
                    silu_read = up("ac", ac.activation(KT[:, h, 0:NCTX], cacc2[:, :], ACT.Silu))
                else:
                    silu_read = up("ac", ac.activation(QT[:, h, :], cacc[:, :], ACT.Silu))
            ring.used(s, last)

    all_engines_meet()
    tap("KT", KT[:, :, :])
    tap("QT", QT[:, :, :])
    tap("V", V[:, :, :, :])

    with Scope() as st:
        maskt = st.sb("mask", [P, 2, P])
        ld_ctx = [st.sb(f"ld_ctx{d}", [P, NH, NCTX]) for d in range(2)]
        ld_x = [wslots[d][:, :].rearrange("p (h n) -> p h n", h=NH) for d in range(2)]
        need("sp", tk_gates["ld_stored"])
        for d in range(2):
            got_ld_ctx = load("sp", "ld_ctx", ld_ctx[d][:, :, :], ld_rows[4 * d:4 * d + 4, 0:NCTX].partition_broadcast(P))
        got_mask = load("sp", "mask", maskt[:, :, :], C["mask"])
        for d in range(2):
            got_ld_x = load("sp", "ld_x", ld_x[d], ld_rows[4 * d:4 * d + 4, NCTX:TA].partition_broadcast(P))
        ring.k = 2
        o_block = ring.fetch(as_cols, w_in_v[:, :, OFF_O:OFF_O + 512])
        CS = st.sb("cell", [P, 2, NH, DH + 1])
        kc = [st.sb(f"kc{d}", [P, NH, P]) for d in range(2)]
        dec = [st.sb(f"dec{d}", [P, NH, P]) for d in range(2)]
        em = [st.sb(f"em{d}", [P, NH, P]) for d in range(2)]
        qd = [st.sb(f"qd{d}", [P, NH, P]) for d in range(2)]
        kw = [st.sb(f"kw{d}", [P, NH, P]) for d in range(2)]
        den = [st.sb(f"den{d}", [P, NH, 1]) for d in range(2)]
        cs_zero = up("ve", ve.memset(CS[:, :, :, :], 0.0))
        h_zero = up("ve", ve.memset(H[:, :, :], 0.0))
        need("ac", got_ld_ctx)
        need("po", got_mask)
        need("pe", ones_col)
        as_heads = lambda bank: bank[:, :].rearrange("p (h j) -> p h j", h=NH)

        def chunk_of(tensor3, c):
            return tensor3[:, :, bass.ds(c * P, P)]

        def value_of(c, h):
            return V[:, bass.ds(c, 1), h, :].rearrange("p a n -> p (a n)")

        def turn_of_states(chunks, outputs, tk):
            tk = dict(tk)
            for d in range(2):
                need("ac", tk[f"keys_read{d}"])
                tk[f"kc{d}"] = up("ac", ac.copy(kc[d][:, :, :], chunk_of(KT, chunks[d][0])))
            for d in range(2):
                c, cx = chunks[d]
                s_, t_, a_, b_ = (psum[4 * d + n] for n in range(4))
                ld = chunk_of(ld_x[d], cx) if outputs else chunk_of(ld_ctx[d], c)
                need("ac", tk[f"cell{d}"], tk[f"qd{d}"])
                tk[f"dec{d}"] = up("ac", ac.activation(dec[d][:, :, :], ld, ACT.Exp))
                need("pe", tk[f"kc{d}"], tk[f"cell{d}"])
                for h in range(NH):
                    mm = pe.transpose(t_[:, h * P:(h + 1) * P], kc[d][:, h, :], ident[:, :])
                tk[f"turned{d}"] = tk[f"keys_read{d}"] = up("pe", mm)
                if outputs:
                    for h in range(NH):
                        mm = pe.matmul(s_[:, h * P:(h + 1) * P], kc[d][:, h, :], QT[:, h, bass.ds(cx * P, P)], start=True, stop=True)
                    tk[f"qk{d}"] = tk[f"keys_read{d}"] = up("pe", mm)
                    need("po", tk[f"out{d}"])
                    tk[f"masked{d}"] = up("po", po.tensor_tensor(em[d][:, :, :], ld, maskt[:, d:d + 1, :].to_broadcast([P, NH, P]), ALU.add))
                    need("po", tk[f"dec{d}"])
                    tk[f"qd{d}"] = up("po", po.tensor_tensor(qd[d][:, :, :], dec[d][:, :, :], chunk_of(QT, cx), ALU.mult))
            if outputs:
                for d in range(2):
                    c = chunks[d][0]
                    need("ac", tk[f"masked{d}"])
                    for h in range(NH):
                        tk[f"e{d}"] = up("ac", ac.activation(em[d][:, h, :], em[d][:, h, :], ACT.Exp, bias=COL[:, bass.ds(c, 1), 8 + 4 * d + h]))
            for d in range(2):
                c = chunks[d][0]
                s_, t_, a_, b_ = (psum[4 * d + n] for n in range(4))
                need("ve", tk[f"turned{d}"], tk[f"added{d}"])
                wa = COL[:, bass.ds(c, 1), 16 + 4 * d:20 + 4 * d].rearrange("p a h -> p (a h)").unsqueeze(2).to_broadcast([P, NH, P])
                tk[f"kw{d}"] = up("ve", ve.tensor_tensor(kw[d][:, :, :], as_heads(t_), wa, ALU.mult))
                if outputs:
                    need("ve", tk[f"qk{d}"], tk[f"e{d}"])
                    tk[f"p{d}"] = up("ve", ve.tensor_tensor(em[d][:, :, :], as_heads(s_), em[d][:, :, :], ALU.mult))
            for d in range(2):
                c, cx = chunks[d]
                s_, t_, a_, b_ = (psum[4 * d + n] for n in range(4))
                need("pe", tk[f"cell{d}"])
                if outputs:
                    need("pe", tk[f"p{d}"], tk[f"qd{d}"], tk[f"h{d}"])
                    out_t = []
                    for h in range(NH):
                        o = (a_ if h < 2 else b_)[:, (h % 2) * 129:(h % 2) * 129 + 129]
                        pe.matmul(o, em[d][:, h, :], value_of(c, h), start=True, stop=False)
                        mm = pe.matmul(o, qd[d][:, h, :], CS[:, d, h, :], start=False, stop=True)
                        if h % 2:
                            out_t.append(up("pe", mm))
                    tk[f"out{d}"] = out_t[1]
                need("pe", tk[f"kw{d}"])
                for h in range(NH):
                    o = (t_ if h < 2 else s_)[:, (h % 2) * 129:(h % 2) * 129 + 129]
                    mm = pe.matmul(o, kw[d][:, h, :], value_of(c, h), start=True, stop=True)
                tk[f"added{d}"] = up("pe", mm)
                if outputs:
                    for n, bank in enumerate((a_, b_)):
                        need("ve", out_t[n])
                        em_col = COL[:, bass.ds(c, 1), 24 + 4 * d + 2 * n:26 + 4 * d + 2 * n].rearrange("p a h -> p (a h)").unsqueeze(2)
                        ds_ = bank[:, 0:258].rearrange("p (h j) -> p h j", h=2)
                        t = up("ve", ve.tensor_tensor(den[d][:, 2 * n:2 * n + 2, :], ds_[:, :, DH:DH + 1], em_col, ALU.max))
                        need("ve", t)
                        t = up("ve", ve.scalar_tensor_tensor(den[d][:, 2 * n:2 * n + 2, :], ds_[:, :, DH:DH + 1], -1.0, den[d][:, 2 * n:2 * n + 2, :], ALU.mult, ALU.max))
                    need("ve", t)
                    t = up("ve", ve.reciprocal(den[d][:, :, :], den[d][:, :, :]))
                    need("ve", t)
                    for h in range(NH):
                        o = H[:, bass.ds(cx, 1), h * P:(h + 1) * P].rearrange("p a n -> p (a n)")
                        tk[f"h{d}"] = up("ve", ve.scalar_tensor_tensor(o, (a_ if h < 2 else b_)[:, (h % 2) * 129:(h % 2) * 129 + DH], den[d][:, h, :], o, ALU.mult, ALU.add))
                end = P - 1 if d == 0 else 0
                need("ve", tk[f"added{d}"], tk[f"dec{d}"])
                for h in range(NH):
                    o = CS[:, d, h, :]
                    u = (t_ if h < 2 else s_)[:, (h % 2) * 129:(h % 2) * 129 + 129]
                    tk[f"cell{d}"] = up("ve", ve.scalar_tensor_tensor(o, o, dec[d][:, h, end:end + 1], u, ALU.mult, ALU.add))
            need("ve", tk["cell1"])
            return tk

        need("ve", h_zero)
        tk = {f"{k}{d}": None for d in range(2) for k in ("keys_read", "qd", "out", "added", "h")}
        tk["cell0"] = tk["cell1"] = cs_zero
        for step in range(2):
            tk = turn_of_states(((step, None), (1 - step, None)), False, tk)
        tap("CS", CS[:, :, :, :])
        need("ac", got_ld_x)
        need("po", got_ld_x)
        tk = turn_of_states(((2, 0), (9, 7)), True, tk)
        per = {"pe_done": 10, "ve_done": 30, "ac_done": 12, "po_done": 4}
        g.loop(TT - 1, per, lambda i: turn_of_states(((i + 3, i + 1), (8 - i, 6 - i)), True, g.carry(tk)))
    all_engines_meet()
    lstm.__exit__()
    tap("H", H[:, :, :])

    OT = mix.sb("OT", [P, NH, T])
    FT = mix.sb("FT", [P, NH, T])
    wm = mix.sb("w_mlstm", [P, 4, D])
    s, w, got = o_block
    u_block = ring.fetch(as_cols, w_in_v[:, :, 0:D_F])
    got_m = load("sp", "w_mlstm", wm[:, :, :], A["w_mlstm"].rearrange("o (k p) n -> p (o k) n", p=P))
    with Scope() as st:
        og = [st.sb(f"o_gate{n}", [P, 512]) for n in range(2)]
        acc = st.sb("ada_acc", [P, 4 * D])
        aslots = [st.sb("ada_block", [P, KD * 512]), FT[:, :, :].rearrange("p h n -> p (h n)")]
        aring = Ring(g, "ada", aslots)
        freed = [None, None]
        need("pe", got)

        def ada_part(n):
            s, w, got = aring.fetch(as_cols, w_ada_v[:, :, (4 + n) * 512:(5 + n) * 512])
            need("ve", got)
            o = acc[:, n * 512:(n + 1) * 512]
            t = up("ve", ve.tensor_scalar(o, w[:, 0, :], silu_c[:, 0:1], None, ALU.mult))
            for k in range(1, KD):
                need("ve", t)
                t = up("ve", ve.scalar_tensor_tensor(o, w[:, k, :], silu_c[:, k:k + 1], o, ALU.mult, ALU.add))
            aring.used(s, t)
            return t

        for j in range(TT):
            b = banks.take()
            for k in range(KD):
                mm = pe.matmul(psum[b][:, :], XT[:, k, NCTX + j * P:NCTX + (j + 1) * P], w[:, k, :], start=k == 0, stop=k == KD - 1)
            last = up("pe", mm)
            need("ac", last, freed[j % 2])
            t = up("ac", ac.activation(og[j % 2][:, :], psum[b][:, :], ACT.Sigmoid))
            banks.freed(b, t)
            need("ve", t)
            freed[j % 2] = h_gated = up("ve", ve.tensor_tensor(H[:, j, :], H[:, j, :], og[j % 2][:, :], ALU.mult))
            ada_ready = ada_part(j)
        ring.used(s, last)
        need("pe", h_gated)
        for h in range(NH):
            for half in range(2):
                b = banks.take()
                for j in range(4):
                    mm = pe.transpose(psum[b][:, j * P:(j + 1) * P], H[:, 4 * half + j, h * P:(h + 1) * P], ident[:, :])
                t = up("pe", mm)
                e = either()
                need(e, t)
                banks.freed(b, evacuate(e, OT[:, h, half * 512:half * 512 + 512], psum[b][:, :]))
        OT_ready = [g.now("ac"), g.now("ve")]

        need("pe", ada_ready, ready_ones)
        need("ve", got_ga)
        for dst, c in ((ga1b, 0), (ga2b, 3 * D)):
            for n in range(2):
                b = banks.take()
                t = up("pe", pe.matmul(psum[b][:, :], ones[:, :], acc[:, c + n * 512:c + (n + 1) * 512], start=True, stop=True))
                need("ve", t)
                o = dst[:, n * 512:(n + 1) * 512]
                ga_ready = up("ve", ve.tensor_tensor(o, psum[b][:, :], o, ALU.add))
                banks.freed(b, ga_ready)
        b = banks.take()
        for j in range(16):
            mm = pe.matmul(psum[b][:, j:j + 1], acc[:, D + j * P:D + (j + 1) * P], ones[:, 0:1], start=True, stop=True)
        t = up("pe", mm)
        need("ve", t)
        up("ve", ve.tensor_tensor(mod2[:, 1, :], psum[b][:, 0:8], col1[:, 40:48], ALU.add))
        t = up("ve", ve.tensor_tensor(mod2[:, 0, :], psum[b][:, 8:16], col1[:, 48:56], ALU.add))
        banks.freed(b, t)
        need("ve", t)
        mod2_ready = up("ve", ve.scalar_tensor_tensor(mod2[:, 0, :], mod2[:, 0, :], 1.0, col1[:, 8:16], ALU.add, ALU.mult))
    all_engines_meet()
    tap("ga1b", ga1b[:, :])
    tap("ga2b", ga2b[:, :])
    tap("mod2", mod2[:, :, :])
    with Scope() as st:
        uT = st.sb("uT", [P, NH, T])
        UE, UO = (FT[:, 2 * n:2 * n + 2, :].rearrange("p a (b n) -> p (a b) n", b=2) for n in range(2))
        cs = st.sb("dft_channels", [P, 2 * P])
        TC = st.sb("dft_cos", [P, 4, 512])
        TS = st.sb("dft_sin", [P, 4, 512])
        alt = st.sb("alternating", [1, 512])
        altc = st.sb("alternating_col", [P, 1])
        got_dft = load("sp", "dft", cs[:, :], C["dft_channels"])
        got_dft = load("sp", "dft", TC[:, :, :], C["dft_cos"].rearrange("(k p) n -> p k n", p=P))
        got_dft = load("sp", "dft", TS[:, :, :], C["dft_sin"].rearrange("(k p) n -> p k n", p=P))
        got_dft = load("sp", "dft", alt[:, :], C["alternating"])
        got_dft = load("sp", "dft", altc[:, :], C["alternating"][:, 0:P].rearrange("a p -> p a"))

        def branch_block(n):
            c = OFF_BR + (n % 2) * D + (n // 2) * 512
            return ring.fetch(as_cols, w_in_v[:, :, c:c + 512])
        branch_blocks = [branch_block(n) for n in range(2)]
        AA = H[:, :, :].rearrange("p a (b c) -> p (a b c)", b=1).rearrange("p (t g n) -> p t g n", t=4, g=NH)
        A5 = st.sb("along_channels_512", [1, NH * P])
        Qs = st.sb("odd_part", [P, 512])
        s, w, got = u_block
        need("pe", got)
        t = up("ve", ve.memset(UO[:, :, 0:1], 0.0))
        for gi in range(NH):
            def into_u(bank, c, n, t, gi=gi):
                need("ac", t)
                return evacuate("ac", uT[:, gi, c - NCTX:c - NCTX + n], bank[:, 0:n])
            last = project_transposed(w, gi * P, spans[1:], into_u)
            need("ve", g.now("ac"))
            up("ve", ve.tensor_copy(UE[:, gi, 0:1], uT[:, gi, 0:1]))
            up("ve", ve.tensor_tensor(UE[:, gi, 1:512], uT[:, gi, 1:512], uT[:, gi, T - 1:512:-1], ALU.add))
            up("ve", ve.tensor_tensor(UO[:, gi, 1:512], uT[:, gi, 1:512], uT[:, gi, T - 1:512:-1], ALU.subtract))
        ring.used(s, last)
        folded = g.now("ve")
        need("pe", folded, got_dft)
        for nt in range(4):
            for pair in range(2):
                b = banks.take()
                for gi in range(2):
                    for part, src in enumerate((UE, UO)):
                        o = (gi * 2 + part) * P
                        mm = pe.matmul(psum[b][:, o:o + P], src[:, 2 * pair + gi, nt * P:(nt + 1) * P], cs[:, part * P:(part + 1) * P], start=True, stop=True)
                t = up("pe", mm)
                e = either()
                need(e, t)
                banks.freed(b, evacuate(e, AA[:, nt, 2 * pair:2 * pair + 2, :], psum[b][:, :].rearrange("p (g n) -> p g n", g=2)))
        b = banks.take()
        for gi in range(NH):
            mm = pe.matmul(psum[b][0:1, gi * P:(gi + 1) * P], uT[:, gi, 512:513], cs[:, 0:P], start=True, stop=True)
        t = up("pe", mm)
        need("ac", t)
        t = evacuate("ac", A5[:, :], psum[b][0:1, :])
        banks.freed(b, t)
        need("pe", g.now("ve"), t)
        qs_read = None
        for gi in range(NH):
            bp, bq, b5 = banks.take(), banks.take(), banks.take()
            for nt in range(4):
                mm = pe.matmul(psum[bq][:, :], AA[:, nt, gi, P:2 * P], TS[:, nt, :], start=nt == 0, stop=nt == 3)
            q_t = up("pe", mm)
            for nt in range(4):
                pe.matmul(psum[bp][:, :], AA[:, nt, gi, 0:P], TC[:, nt, :], start=nt == 0, stop=False)
            mm = pe.matmul(psum[bp][:, :], A5[0:1, gi * P:(gi + 1) * P], alt[0:1, :], start=False, stop=True)
            for nt in range(4):
                pe.matmul(psum[b5][:, 0:1], AA[:, nt, gi, 0:P], altc[:, 0:1], start=nt == 0, stop=False)
            mm = pe.matmul(psum[b5][:, 0:1], A5[0:1, gi * P:(gi + 1) * P], alt[0:1, 0:1], start=False, stop=True)
            p_t = up("pe", mm)
            need("ac", q_t, qs_read)
            t = evacuate("ac", Qs[:, :], psum[bq][:, :])
            banks.freed(bq, t)
            need("ve", t, p_t)
            up("ve", ve.tensor_tensor(FT[:, gi, 0:512], psum[bp][:, :], Qs[:, :], ALU.subtract))
            qs_read = up("ve", ve.tensor_tensor(FT[:, gi, T - 1:512:-1], psum[bp][:, 1:512], Qs[:, 1:512], ALU.add))
            banks.freed(bp, qs_read)
            fourier_ready = up("ve", ve.tensor_copy(FT[:, gi, 512:513], psum[b5][:, 0:1]))
            banks.freed(b5, fourier_ready)
    tap("OT", OT[:, :, :])
    tap("FT", FT[:, :, :])

    MG = mix.sb("MG", [P, KD, T])
    with Scope() as st:
        wf = H[:, :, :].rearrange("p (k a) b -> p k (a b)", k=4)
        need("sp", fourier_ready)
        got_f = load("sp", "w_fourier", wf, A["w_fourier"].rearrange("o (k p) n -> p (o k) n", p=P))
        branch_blocks.append(branch_block(2))
        w_out_v = A["w_out"].rearrange("o (k p) n -> p (o k) n", p=P)
        s1 = [st.sb(f"gate_f{n}", [P, 512]) for n in range(2)]
        s2 = [st.sb(f"gate_m{n}", [P, 512]) for n in range(2)]
        read = [None, None]
        w_out_blocks = []
        need("pe", *OT_ready, fourier_ready)
        n = 0
        for quad in range(2):
            sA, wA, gotA = branch_blocks[2 * quad]
            sB, wB, gotB = branch_blocks[2 * quad + 1]
            need("pe", gotA, gotB)
            for jj in range(4):
                j = 4 * quad + jj
                for half in range(2):
                    c = NCTX + half * 512
                    bg = []
                    for w in (wA, wB):
                        b = banks.take()
                        for k in range(KD):
                            mm = pe.matmul(psum[b][:, :], w[:, k, jj * P:(jj + 1) * P], XT[:, k, c:c + 512], start=k == 0, stop=k == KD - 1)
                        bg.append((b, up("pe", mm)))
                    last = bg[-1][1]
                    need("pe", got_f, got_m)
                    by = []
                    for w, src in ((wf, FT), (wm, OT)):
                        b = banks.take()
                        for k in range(4):
                            mm = pe.matmul(psum[b][:, :], w[:, k, j * P:(j + 1) * P], src[:, k, half * 512:(half + 1) * 512], start=k == 0, stop=k == 3)
                        by.append((b, up("pe", mm)))
                    for (b, t), dst in zip(bg, (s1[n % 2], s2[n % 2])):
                        need("ac", t, read[n % 2])
                        t = up("ac", ac.activation(dst[:, :], psum[b][:, :], ACT.Sigmoid))
                        banks.freed(b, t)
                    o = MG[:, j, half * 512:(half + 1) * 512]
                    need("ve", t, by[0][1])
                    t1 = up("ve", ve.tensor_tensor(s1[n % 2][:, :], psum[by[0][0]][:, :], s1[n % 2][:, :], ALU.mult))
                    banks.freed(by[0][0], t1)
                    need("ve", by[1][1])
                    t = up("ve", ve.tensor_tensor(s2[n % 2][:, :], psum[by[1][0]][:, :], s2[n % 2][:, :], ALU.mult))
                    banks.freed(by[1][0], t)
                    need("ve", t)
                    read[n % 2] = merged_ready = up("ve", ve.tensor_tensor(o, s1[n % 2][:, :], s2[n % 2][:, :], ALU.add))
                    n += 1
            ring.used(sA, last)
            ring.used(sB, last)
            if quad == 0:
                branch_blocks.append(branch_block(3))
            w_out_blocks.append(ring.fetch(as_cols, w_out_v[:, :, quad * 512:(quad + 1) * 512]))
    tap("MG", MG[:, :, :])

    xn_rows, x2_rows, xf_rows = scratch["xn"], scratch["x2"], scratch["xf"]
    source = {"g": A["w_gate_e"], "u": A["w_up_e"], "d": A["w_down_e"]}
    source = {k: v.rearrange("o e (k p) n -> (o e) p k n", p=P) for k, v in source.items()}

    def expert_unit(u, e):
        m, half = ("g", "u", "g", "u", "d", "d")[u // 2], (0, 0, 1, 1, 0, 1)[u // 2]
        v = source[m][bass.ds(e, 1), :, 4 * (u % 2):4 * (u % 2) + 4, 512 * half:512 * half + 512]
        return v.rearrange("a p k n -> (a p) k n")

    with Scope() as st:
        X2 = XT[:, :, 0:D]
        tmp = [st.sb(f"attn_tmp{n}", [P, 512]) for n in range(2)]
        xn = [wm[:, n, :] for n in range(3)]
        junk = wm[:, 3, :]
        wr = st.sb("w_router", [P, KD, NE])
        need("ac", merged_ready)
        got_wr = load("ac", "w_router", wr[:, :, :], A["w_router"].rearrange("o (k p) n -> p (o k) n", p=P))
        need("sp", merged_ready)
        x_tile = lambda v, j: v[j * P:(j + 1) * P, :]
        got_x2 = [load("sp", f"x_again{j}", X2[:, j, :], x_tile(A["x"].rearrange("b t n -> (b t) n"), j)) for j in range(TT)]
        need("pe", merged_ready)
        x2_ready, xn_ready, turned_x = [None] * TT, [None] * TT, [None] * TT
        logits_bank = None

        def norm2(j):
            need("ac", x2_ready[j], xn_ready[j - 1] if j else None)
            t = up("ac", ac.activation(junk, X2[:, j, :], ACT.Square, accum_out=small[:, j:j + 1]))
            need("ve", t)
            t = up("ve", ve.tensor_scalar(small[:, 16 + j:17 + j], small[:, j:j + 1], 1.0 / D, EPS, ALU.mult, ALU.add))
            need("ac", t)
            t = up("ac", ac.activation(small[:, 32 + j:33 + j], small[:, 16 + j:17 + j], ACT.Sqrt))
            need("ve", t)
            t = up("ve", ve.reciprocal(small[:, 48 + j:49 + j], small[:, 32 + j:33 + j]))
            need("ve", t, xn_stored[j - 3] if j > 2 else None, turned_x[j - 3] if j > 2 else None)
            xn_ready[j] = up("ve", ve.tensor_scalar(xn[j % 3], X2[:, j, :], small[:, 48 + j:49 + j], None, ALU.mult))
            need("sp", xn_ready[j])
            xn_stored.append(load("sp", f"xn_stored{j % 3}", x_tile(xn_rows, j), xn[j % 3]))

        def turn_rows(j):
            need("pe", xn_ready[j])
            for half in range(2):
                b = banks.take()
                for k in range(4):
                    kk = 4 * half + k
                    mm = pe.transpose(psum[b][:, k * P:(k + 1) * P], xn[j % 3][:, kk * P:(kk + 1) * P], ident[:, :])
                turned_x[j] = up("pe", mm)
                need("ac", turned_x[j], mod2_ready)
                for k in range(4):
                    kk = 4 * half + k
                    t = evacuate("ac", MG[:, kk, j * P:(j + 1) * P], psum[b][:, k * P:(k + 1) * P], mod2[:, 0, kk:kk + 1], mod2[:, 1, kk:kk + 1])
                banks.freed(b, t)
            return t

        xn_stored = []
        for half in range(2):
            s, w, got = w_out_blocks[half]
            need("pe", got)
            hs = slice(half * 512, (half + 1) * 512)
            for j in range(TT):
                b = banks.take()
                for k in range(KD):
                    mm = pe.matmul(psum[b][:, :], MG[:, k, j * P:(j + 1) * P], w[:, k, :], start=k == 0, stop=k == KD - 1)
                last = up("pe", mm)
                need("ve", last, got_x2[j])
                t = up("ve", ve.tensor_tensor(tmp[j % 2][:, :], psum[b][:, :], ga1b[:, hs], ALU.mult))
                banks.freed(b, t)
                need("ve", t)
                x2_ready[j] = up("ve", ve.tensor_tensor(X2[:, j, hs], X2[:, j, hs], tmp[j % 2][:, :], ALU.add))
                if half:
                    need("sp", x2_ready[j])
                    x2_stored = load("sp", "x2_stored", x_tile(x2_rows, j), X2[:, j, :])
                    if j > 0:
                        norm2(j - 1)
                    if j > 1:
                        turn_rows(j - 2)
            ring.used(s, last)
        norm2(TT - 1)
        need("sp", last)
        for u in range(6):
            load("sp", f"expert_raw{u}_loaded", wslots[u // 2][:, (u % 2) * 2048:(u % 2) * 2048 + 2048].rearrange("p (k n) -> p k n", k=4), expert_unit(u, 0))
        turn_rows(TT - 2)
        t = turn_rows(TT - 1)
        need("pe", t, got_wr)
        b = banks.take()
        for j in range(TT):
            for k in range(KD):
                mm = pe.matmul(psum[b][:, j * NE:(j + 1) * NE], MG[:, k, j * P:(j + 1) * P], wr[:, k, :], start=k == 0, stop=k == KD - 1)
        logits = up("pe", mm)

        af = st.sb("affinity", [P, TT, NE])
        red = st.sb("softmax_red", [P, 2, TT, 1])
        lg = psum[b][:, 0:TT * NE].rearrange("p (j e) -> p j e", e=NE)
        need("ve", logits)
        t = up("ve", ve.tensor_reduce(red[:, 0, :, :].rearrange("p j a -> p (j a)"), lg, X, ALU.max))
        need("ve", t)
        t = up("ve", ve.tensor_tensor(af[:, :, :], lg, red[:, 0, :, :].to_broadcast([P, TT, NE]), ALU.subtract))
        banks.freed(b, t)
        need("ac", t)
        t = up("ac", ac.activation(af[:, :, :], af[:, :, :], ACT.Exp))
        need("ve", t)
        t = up("ve", ve.tensor_reduce(red[:, 1, :, :].rearrange("p j a -> p (j a)"), af[:, :, :], X, ALU.add))
        need("ve", t)
        t = up("ve", ve.reciprocal(red[:, 1, :, :], red[:, 1, :, :]))
        need("ve", t)
        af_ready = up("ve", ve.tensor_tensor(af[:, :, :], af[:, :, :], red[:, 1, :, :].to_broadcast([P, TT, NE]), ALU.mult))
        tap("af", af[:, :, :])
        AT = st.sb("affinity_T", [NE, T])
        need("pe", af_ready)
        for half in range(2):
            b = banks.take()
            for j in range(4):
                mm = pe.transpose(psum[b][0:NE, j * P:(j + 1) * P], af[:, 4 * half + j, :], ident[:, :])
            t = up("pe", mm)
            need("ve", t)
            t = evacuate("ve", AT[:, half * 512:(half + 1) * 512], psum[b][0:NE, :])
            banks.freed(b, t)
        val = st.sb("top_values", [NE, CAP])
        idx = st.sb("top_tokens", [NE, CAP], U32)
        idxf = st.sb("top_tokens_f", [NE, CAP])
        need("ve", t)
        for r in range(CAP // 8):
            v8, i8 = val[:, 8 * r:8 * r + 8], idx[:, 8 * r:8 * r + 8]
            t = up("ve", ve.max(v8, AT[:, :]))
            need("ve", t)
            t = up("ve", ve.max_index(i8, v8, AT[:, :]))
            t = up("ve", ve.match_replace(AT[:, :], v8, AT[:, :], -1.0))
            need("ve", t)
        t = up("ve", ve.tensor_copy(idxf[:, :], idx[:, :]))
        need("pe", t)
        b = banks.take()
        pe.transpose(psum[b][:, 0:NE], val[:, :], ident[0:NE, 0:NE])
        t = up("pe", pe.transpose(psum[b][:, NE:2 * NE], idxf[:, :], ident[0:NE, 0:NE]))
        need("ve", t)
        up("ve", ve.tensor_copy(VALC[:, :], psum[b][:, 0:NE]))
        top_ready = up("ve", ve.tensor_copy(IDXC[:, :], psum[b][:, NE:2 * NE]))
        banks.freed(b, top_ready)
    all_engines_meet()
    for e in ("po", "ac", "sp"):
        need(e, x2_stored, *xn_stored)
    mix.__exit__()
    blk.__exit__()

    with Scope() as st:
        UNITS, SLOTS, AHEAD = 12, 6, 4
        raw = [wslots[n // 2][:, (n % 2) * 2048:(n % 2) * 2048 + 2048].rearrange("p (k n) -> p k n", k=4) for n in range(SLOTS)]
        hi = [st.sb(f"expert_w_hi{n}", [P, 4, 512], F32R) for n in range(SLOTS)]
        lo = [st.sb(f"expert_w_lo{n}", [P, 4, 512], F32R) for n in range(SLOTS)]
        xs = st.sb("expert_x", [P, D])
        xm = st.sb("expert_x_mod", [P, KD, P])
        xh = st.sb("expert_xT_hi", [P, KD, P], F32R)
        xlo = st.sb("expert_xT_lo", [P, KD, P], F32R)
        hid = st.sb("expert_hidden", [P, D])
        hid_hi = st.sb("expert_hidT_hi", [P, KD, P], F32R)
        hid_lo = st.sb("expert_hidT_lo", [P, KD, P], F32R)
        y = st.sb("expert_y", [P, D])
        idx_g = st.sb("gather_tokens", [P, 1], U32)
        idx_s = st.sb("scatter_tokens", [P, 1], U32)
        silu = st.sb("expert_silu", [P, 2, 512])

        def fetch(u, e, tk):
            e, u = (e + 1, u - UNITS) if u >= UNITS else (e, u)
            r = u % SLOTS
            need("sp", tk[f"raw{r}"])
            load("sp", f"expert_raw{r}_loaded", raw[r], expert_unit(u, e))

        def split(u, tk):
            r = u % SLOTS
            landed = (g.flag(f"expert_raw{r}_loaded"), g.flag(f"expert_raw{r}_loaded").n)
            need("ac", landed, tk[f"used{r}"])
            t = up("ac", ac.copy(hi[r][:, :, :], raw[r]))
            need("ve", t, landed, tk[f"used{r}"])
            t = up("ve", ve.tensor_tensor(lo[r][:, :, :], raw[r], hi[r][:, :, :].bitcast(F32), ALU.subtract))
            tk[f"ready{r}"] = tk[f"raw{r}"] = t

        def product(bank, xhi, xlow, u, tk):
            r = u % SLOTS
            need("pe", tk[f"ready{r}"])
            for k in range(4):
                kk = 4 * (u % 2) + k
                pe.matmul(bank[:, :], xhi[:, kk, :], hi[r][:, k, :], start=kk == 0, stop=False)
                pe.matmul(bank[:, :], xhi[:, kk, :], lo[r][:, k, :], start=False, stop=False)
                mm = pe.matmul(bank[:, :], xlow[:, kk, :], hi[r][:, k, :], start=False, stop=kk == KD - 1)
            tk[f"used{r}"] = up("pe", mm)
            return tk[f"used{r}"]

        def gather(e, tk):
            need("po", tk["x_read"])
            t = up("po", po.tensor_copy(idx_g[:, :], IDXC[:, bass.ds(e, 1)]))
            need("po", t)
            f = g.flag("gathered")
            po.indirect_dma_start(xs[:, :], None, xn_rows, bass.IndirectOffsetOnAxis(idx_g[:, :], 0)).then_inc(f.sem, 16)
            f.n += 16
            tk["gathered"] = (f, f.n)

        def turn_x(tk):
            need("pe", tk["gathered"], tk["xT"])
            for half in range(2):
                for k in range(4):
                    kk = 4 * half + k
                    mm = pe.transpose(psum[4 + half][:, k * P:(k + 1) * P], xs[:, kk * P:(kk + 1) * P], ident[:, :])
                tk["x_read"] = up("pe", mm)

        def split_x(tk):
            need("ac", tk["x_read"], tk["xT"])
            for kk in range(KD):
                r = up("ac", ac.activation(xm[:, kk, :], psum[4 + kk // 4][:, (kk % 4) * P:(kk % 4 + 1) * P], ACT.Identity, scale=mod2[:, 0, kk:kk + 1], bias=mod2[:, 1, kk:kk + 1]))
            need("ac", r)
            r = up("ac", ac.copy(xh[:, :, :], xm[:, :, :]))
            need("ve", r)
            tk["xT"] = up("ve", ve.tensor_tensor(xlo[:, :, :], xm[:, :, :], xh[:, :, :].bitcast(F32), ALU.subtract))

        def turn_hidden(half, tk):
            need("pe", tk[f"hid{half}"], tk[f"hidT{half}"])
            for k in range(4):
                kk = 4 * half + k
                mm = pe.transpose(psum[6 + half][:, k * P:(k + 1) * P], hid[:, kk * P:(kk + 1) * P], ident[:, :])
            t = up("pe", mm)
            need("ac", t)
            turned = psum[6 + half][:, :].rearrange("p (k n) -> p k n", k=4)
            t = up("ac", ac.copy(hid_hi[:, 4 * half:4 * half + 4, :], turned))
            need("ve", t)
            tk[f"hidT{half}"] = up("ve", ve.tensor_tensor(hid_lo[:, 4 * half:4 * half + 4, :], turned, hid_hi[:, 4 * half:4 * half + 4, :].bitcast(F32), ALU.subtract))

        def expert(e, tk, last=False):
            tk = dict(tk)
            y_free = (g.flag("scattered"), g.flag("scattered").n)
            if not last:
                gather(e + 1, tk)
            need("pe", tk["xT"])
            for u in range(UNITS):
                if u + AHEAD < UNITS or not last:
                    split(u + AHEAD, tk)
                if u + AHEAD + SLOTS < UNITS or not last:
                    fetch(u + AHEAD + SLOTS, e, tk)
                b, half = u // 2, u // 4
                if u < 8:
                    if u % 4 == 2:
                        need("pe", tk[f"y{half}"])
                    t = product(psum[b], xh, xlo, u, tk)
                    if u % 4 == 1:
                        need("ac", t)
                        s_t = up("ac", ac.activation(silu[:, half, :], psum[b][:, :], ACT.Silu))
                    if u % 4 == 3:
                        need("ve", t, s_t)
                        tk[f"hid{half}"] = up("ve", ve.tensor_tensor(hid[:, half * 512:(half + 1) * 512], psum[b][:, :], silu[:, half, :], ALU.mult))
                    if u == 5:
                        turn_hidden(0, tk)
                    if u == 7 and not last:
                        turn_x(tk)
                else:
                    half = b - 4
                    need("pe", tk[f"hidT{u % 2}"])
                    t = product(psum[2 * half + 1], hid_hi, hid_lo, u, tk)
                    if u == 8:
                        turn_hidden(1, tk)
                        if not last:
                            split_x(tk)
                    if u % 2:
                        need("ve", t, y_free)
                        hs = slice(half * 512, (half + 1) * 512)
                        tk[f"y{half}"] = up("ve", ve.scalar_tensor_tensor(y[:, hs], psum[2 * half + 1][:, :], VALC[:, bass.ds(e, 1)], ga2b[:, hs], ALU.mult, ALU.mult))
            need("po", y_free)
            c = up("po", po.tensor_copy(idx_s[:, :], IDXC[:, bass.ds(e, 1)]))
            need("po", c, tk["y1"])
            f = g.flag("scattered")
            po.indirect_dma_start(x2_rows, bass.IndirectOffsetOnAxis(idx_s[:, :], 0), y[:, :], None, compute_op=ALU.add).then_inc(f.sem, 16)
            f.n += 16
            return tk

        tk = {k: None for k in ["x_read", "xT", "hidT0", "hidT1", "y0", "y1"] + [f"{n}{r}" for n in ("raw", "used") for r in range(SLOTS)]}
        gather(0, tk)
        for u in range(AHEAD):
            split(u, tk)
            fetch(u + SLOTS, 0, tk)
        turn_x(tk)
        split_x(tk)
        tk = expert(0, tk)
        per = {"pe_done": 16, "ac_done": 25, "ve_done": 19, "po_done": 2, "gathered": 16, "scattered": 16,
               **{f"expert_raw{r}_loaded": 32 for r in range(SLOTS)}}
        turns = []
        g.loop(NE - 2, per, lambda i: turns.append(expert(i + 1, g.carry(tk))))
        tk = expert(NE - 1, g.after(turns[0], NE - 2, per), last=True)
        scattered = (g.flag("scattered"), g.flag("scattered").n)
    all_engines_meet()
    ring.k, ring.busy = 0, [tk["raw1"], tk["raw3"], tk["raw5"]]
    two = Scope().__enter__()
    XFT = two.sb("XFT", [P, KD, T])
    need("sp", scattered)
    with Scope() as st:
        XF = st.sb("XF", [P, TT, D])
        junk = st.sb("junk2", [P, D])
        gf = st.sb("g_final", [P, D])
        got_gf = load("ac", "g_final", gf[:, :], A["g_final"].partition_broadcast(P))
        got_xf = [load("sp", f"xf_loaded{j}", XF[:, j, :], x_tile(x2_rows, j)) for j in range(TT)]
        need("ve", got_gf)
        xf_ready = [None] * TT

        def final_norm(j):
            need("ac", got_xf[j])
            t = up("ac", ac.activation(junk[:, :], XF[:, j, :], ACT.Square, accum_out=small[:, j:j + 1]))
            need("ac", t)
            need("ve", t)
            t = up("ve", ve.tensor_scalar(small[:, 16 + j:17 + j], small[:, j:j + 1], 1.0 / D, EPS, ALU.mult, ALU.add))
            need("ac", t)
            t = up("ac", ac.activation(small[:, 32 + j:33 + j], small[:, 16 + j:17 + j], ACT.Sqrt))
            need("ve", t)
            t = up("ve", ve.reciprocal(small[:, 48 + j:49 + j], small[:, 32 + j:33 + j]))
            need("ve", t)
            xf_ready[j] = up("ve", ve.scalar_tensor_tensor(XF[:, j, :], XF[:, j, :], small[:, 48 + j:49 + j], gf[:, :], ALU.mult, ALU.mult))
            need("sp", xf_ready[j])
            return load("sp", "xf_stored", x_tile(xf_rows, j), XF[:, j, :])

        def turn_final(j):
            need("pe", xf_ready[j])
            for half in range(2):
                b = banks.take()
                for k in range(4):
                    kk = 4 * half + k
                    mm = pe.transpose(psum[b][:, k * P:(k + 1) * P], XF[:, j, kk * P:(kk + 1) * P], ident[:, :])
                t = up("pe", mm)
                e = either()
                need(e, t)
                banks.freed(b, evacuate(e, XFT[:, 4 * half:4 * half + 4, j * P:(j + 1) * P], psum[b][:, :].rearrange("p (k n) -> p k n", k=4)))

        for j in range(TT):
            xf_stored = final_norm(j)
            if j > 0:
                turn_final(j - 1)
        turn_final(TT - 1)
        need("sp", xf_stored)
    for e in ("ac", "ve", "po"):
        need(e, xf_stored)
    all_engines_meet()
    tap("XFT", XFT[:, :, :])

    NMIX = DMIX // P
    HT = two.sb("HT", [P, NMIX, T])
    ring2, cols8 = ring, as_cols
    w_in2_v = A["w_in_2"].rearrange("o (k p) n -> p (o k) n", p=P)

    def project2(w, c0, finish):
        for half in range(2):
            b = banks.take()
            for k in range(KD):
                mm = pe.matmul(psum[b][:, :], w[:, k, c0:c0 + P], XFT[:, k, half * 512:(half + 1) * 512], start=k == 0, stop=k == KD - 1)
            last = up("pe", mm)
            banks.freed(b, finish(psum[b], slice(half * 512, (half + 1) * 512), last))
        return last

    with Scope() as st:
        HP = st.sb("conformer_in", [P, 2, CONV_D - 1 + T])
        CV = st.sb("conformer_conv", [P, 2, T])
        XP = st.sb("padded_a", [P, 2, 16 + T])
        XC = st.sb("padded_b", [P, 2, 16 + T])
        VG = st.sb("gating_v", [P, TT, DG])
        memT = st.sb("memT", [P, KD, MEM])
        K2T = st.sb("mem_keys", [P, 2, MEM])
        V2 = st.sb("mem_values", [P, 2, DG])
        tm = [st.sb(f"tmp2_{n}", [P, 512]) for n in range(3)]
        WT = st.sb("gating_w", [P, NH, P])
        sgw = st.sb("gating_w_rows", [P, NH, P])
        tril = st.sb("tril", [P, P])
        SB_ = st.sb("gating_bias", [P, 2, P])
        lng = st.sb("gating_ln", [P, 2, DG])
        pw = st.sb("conformer_pw", [P, 2, DG])
        grp = st.sb("pool_grp", [P, 2, P])
        fix = st.sb("pool_fix", [P, 2, 16])
        invw = st.sb("pool_inv", [P, 2])
        stats = st.sb("gating_stats", [P, TT, 6])
        mv = st.sb("gating_mv", [P, TT, 2])
        sd = st.sb("gating_sd", [P, TT, 1])

        zeros = [up("po", po.memset(x, 0.0)) for x in (HP[:, :, 0:CONV_D - 1], XC[:, :, 0:16], grp[:, :, :])][-1]
        mem_rows = XP[:, :, 0:D]
        got_mem = load("ac", "mem", mem_rows, A["mem_2"].rearrange("b (m p) n -> p (b m) n", p=P))
        load("ac", "small2", sgw[:, :, :], A["sg_w_2"].rearrange("o h t s -> t (o h) s"))
        load("ac", "small2", tril[:, :], C["tril"])
        load("ac", "small2", lng[:, 0, :], A["sg_ln_g_2"].partition_broadcast(P).rearrange("p a n -> p (a n)"))
        load("ac", "small2", lng[:, 1, :], A["sg_ln_b_2"].partition_broadcast(P).rearrange("p a n -> p (a n)"))
        load("ac", "small2", pw[:, :, :], A["cc_pw_w_2"].rearrange("o (k p) n -> p (o k) n", p=P))
        load("ac", "small2", fix[:, :, :], C["pool_fix"])
        load("ac", "small2", invw[:, :], C["pool_inv"])
        need("ac", zeros)
        for h in range(NH):
            q = slice(64 * (h % 2), 64 * (h % 2) + 64)
            load("ac", "small2", SB_[q, h // 2, :], A["sg_b_2"][0, h:h + 1, :].partition_broadcast(64).rearrange("p a n -> p (a n)"))
            got_small = load("ac", "small2", grp[q, h // 2, 64 * (h % 2):64 * (h % 2) + 64], A["pool_w_2"][0, h, :, :])

        need("pe", got_mem)
        for k2 in range(4):
            b = banks.take()
            for k in range(2):
                for m in range(2):
                    mm = pe.transpose(psum[b][:, (2 * k + m) * P:(2 * k + m + 1) * P], XP[:, m, (2 * k2 + k) * P:(2 * k2 + k + 1) * P], ident[:, :])
            t = up("pe", mm)
            e = either()
            need(e, t)
            banks.freed(b, evacuate(e, memT[:, 2 * k2:2 * k2 + 2, :], psum[b][:, :].rearrange("p (k n) -> p k n", k=2)))
        s, w, got = ring2.fetch(cols8, A["w_kv_2"].rearrange("o (k p) n -> p (o k) n", p=P))
        need("pe", got, g.now("ac"), g.now("ve"))
        for tile in range(2):
            b = banks.take()
            for k in range(KD):
                mm = pe.matmul(psum[b][:, 0:MEM], w[:, k, tile * P:(tile + 1) * P], memT[:, k, :], start=k == 0, stop=k == KD - 1)
            t = up("pe", mm)
            need("ac", t)
            banks.freed(b, evacuate("ac", K2T[:, tile, :], psum[b][:, 0:MEM]))
        for m in range(2):
            b = banks.take()
            for k in range(KD):
                mm = pe.matmul(psum[b][:, 0:DG], memT[:, k, m * P:(m + 1) * P], w[:, k, DG:2 * DG], start=k == 0, stop=k == KD - 1)
            t = up("pe", mm)
            need("ac", t)
            banks.freed(b, evacuate("ac", V2[:, m, :], psum[b][:, 0:DG]))
        ring2.used(s, t)
        mem_ready = g.now("ac")
        zero_xp = up("po", po.memset(XP[:, :, 0:16], 0.0)) if not need("po", t) else None

        need("ve", got_small)
        for h in range(NH):
            t = up("ve", ve.tensor_tensor(sgw[:, h, :], sgw[:, h, :], tril[:, :], ALU.mult))
        need("pe", t)
        b = banks.take()
        for h in range(NH):
            mm = pe.transpose(psum[b][:, h * P:(h + 1) * P], sgw[:, h, :], ident[:, :])
        t = up("pe", mm)
        need("ve", t)
        wt_ready = evacuate("ve", WT[:, :, :], psum[b][:, :].rearrange("p (h n) -> p h n", h=NH))
        banks.freed(b, wt_ready)

        s, w, got = ring2.fetch(cols8, w_in2_v[:, :, 1536:2048])
        need("pe", got)
        tm_free = [None, None, None]
        for tile in range(2):
            def sig_g(bank, hs, t, tile=tile):
                need("ac", t)
                return up("ac", ac.activation(CV[:, tile, hs], bank[:, :], ACT.Sigmoid))
            project2(w, DG + tile * P, sig_g)

            def a_times(bank, hs, t, tile=tile):
                need("ve", t, g.now("ac"), zeros)
                return up("ve", ve.tensor_tensor(HP[:, tile, CONV_D - 1 + hs.start:CONV_D - 1 + hs.stop], bank[:, :], CV[:, tile, hs], ALU.mult))
            last = project2(w, tile * P, a_times)
        ring2.used(s, last)
        hp_ready = g.now("ve")
        conv_t = [hp_ready, hp_ready]

        def conformer_taps(first, last_):
            for n in range(first, last_):
                for tile in range(2):
                    wc = col3[:, P3["dw"] + 2 * n + tile:P3["dw"] + 2 * n + tile + 1]
                    src = HP[:, tile, n:n + T]
                    need("ve", conv_t[tile])
                    if n == 0:
                        bias = col3[:, P3["dw_b"] + tile:P3["dw_b"] + tile + 1]
                        conv_t[tile] = up("ve", ve.tensor_scalar(CV[:, tile, :], src, wc, bias, ALU.mult, ALU.add))
                    else:
                        conv_t[tile] = up("ve", ve.scalar_tensor_tensor(CV[:, tile, :], src, wc, CV[:, tile, :], ALU.mult, ALU.add))

        sA, wA, gotA = ring2.fetch(cols8, w_in2_v[:, :, 0:512])
        sB, wB, gotB = ring2.fetch(cols8, w_in2_v[:, :, 512:1024])
        need("pe", gotA)

        def copy_to(dst, e="ac", func=None):
            def finish(bank, hs, t):
                need(e, t)
                return evacuate(e, dst(hs), bank[:, :], func=func)
            return finish

        need("ac", zero_xp)
        for tile in range(2):
            project2(wA, tile * P, copy_to(lambda hs: XP[:, tile, 16 + hs.start:16 + hs.stop]))
        for tile in range(2):
            last = project2(wA, DG + tile * P, copy_to(lambda hs: HT[:, tile, hs]))
        ring2.used(sA, last)
        conformer_taps(0, 6)
        need("pe", gotB)
        for tile in range(2):
            def times_x(bank, hs, t, tile=tile):
                need("ve", t, g.now("ac"))
                o = XP[:, tile, 16 + hs.start:16 + hs.stop]
                return up("ve", ve.tensor_tensor(o, bank[:, :], o, ALU.mult))
            project2(wB, tile * P, times_x)
        ca_ready = g.now("ve")
        for tile in range(2):
            last = project2(wB, DG + tile * P, copy_to(lambda hs: HT[:, 2 + tile, hs], func=ACT.Gelu_apprx_tanh))
        ring2.used(sB, last)
        u_ready = g.now("ac")
        need("ve", ca_ready)
        acc_a = VG[:, :, :].rearrange("p (a b) n -> p a (b n)", a=2)
        for tile in range(2):
            for n in range(CONV_A):
                wc = col3[:, P3["conv_a"] + 2 * n + tile:P3["conv_a"] + 2 * n + tile + 1]
                src = XP[:, tile, 14 + n:14 + n + T]
                if n == 0:
                    t = up("ve", ve.tensor_scalar(acc_a[:, tile, :], src, wc, None, ALU.mult))
                else:
                    need("ve", t)
                    t = up("ve", ve.scalar_tensor_tensor(acc_a[:, tile, :], src, wc, acc_a[:, tile, :], ALU.mult, ALU.add))
            need("ve", t, u_ready)
            ya_ready = up("ve", ve.tensor_tensor(HT[:, tile, :], HT[:, tile, :], acc_a[:, tile, :], ALU.mult))

        s, w, got = ring2.fetch(cols8, w_in2_v[:, :, 1024:1536])
        need("pe", got)
        need("ac", ya_ready)
        for j in range(TT):
            b = banks.take()
            for k in range(KD):
                mm = pe.matmul(psum[b][:, 0:DG], XFT[:, k, j * P:(j + 1) * P], w[:, k, 0:DG], start=k == 0, stop=k == KD - 1)
            t = up("pe", mm)
            need("ac", t)
            banks.freed(b, up("ac", ac.activation(VG[:, j, :], psum[b][:, 0:DG], ACT.Gelu_apprx_tanh)))
        v_ready = g.now("ac")
        for tile in range(2):
            last = project2(w, DG + tile * P, copy_to(lambda hs: XC[:, tile, 16 + hs.start:16 + hs.stop]))
        ring2.used(s, last)
        xc_ready = g.now("ac")
        conformer_taps(6, 14)
        need("ve", v_ready)
        for j in range(TT):
            t = up("ve", ve.bn_stats(stats[:, j, :], VG[:, j, :]))
        need("ve", t)
        for j in range(TT):
            t = up("ve", ve.bn_aggr(mv[:, j, :], stats[:, j, :]))
        need("ve", t)
        t = up("ve", ve.tensor_scalar(sd[:, :, :], mv[:, :, 1:2], LN_EPS, None, ALU.add))
        need("ac", t)
        t = up("ac", ac.activation(sd[:, :, :], sd[:, :, :], ACT.Sqrt))
        need("ve", t)
        t = up("ve", ve.reciprocal(sd[:, :, :], sd[:, :, :]))
        need("ve", t)
        for j in range(TT):
            t = up("ve", ve.tensor_scalar(VG[:, j, :], VG[:, j, :], mv[:, j, 0:1], sd[:, j, :], ALU.subtract, ALU.mult))
        need("po", t, got_small)
        for j in range(TT):
            t = up("po", po.tensor_tensor(VG[:, j, :], VG[:, j, :], lng[:, 0, :], ALU.mult))
            need("po", t)
            vn_ready = up("po", po.tensor_tensor(VG[:, j, :], VG[:, j, :], lng[:, 1, :], ALU.add))
        need("pe", vn_ready, wt_ready)
        for pair in range(2):
            for quad in range(2):
                for hh in range(2):
                    b = banks.take()
                    for j in range(4):
                        mm = pe.matmul(psum[b][:, j * P:(j + 1) * P], VG[:, 4 * quad + j, pair * P:(pair + 1) * P], WT[:, 2 * pair + hh, :], start=True, stop=True)
                    t = up("pe", mm)
                    q = slice(64 * hh, 64 * hh + 64)
                    hs = slice(quad * 512, (quad + 1) * 512)
                    need("ve", t, u_ready)
                    as_chunks = lambda x: x.rearrange("p (c n) -> p c n", c=4)
                    t = up("ve", ve.tensor_tensor(as_chunks(tm[0][q, :]), as_chunks(psum[b][q, :]), SB_[q, pair:pair + 1, :].to_broadcast([64, 4, P]), ALU.add))
                    banks.freed(b, t)
                    need("ve", t)
                    yb_ready = up("ve", ve.tensor_tensor(HT[q, 2 + pair, hs], HT[q, 2 + pair, hs], tm[0][q, :], ALU.mult))

        need("ve", xc_ready)
        t = up("ve", ve.tensor_copy(HT[:, 4:6, :], XC[:, :, 16:16 + T]))
        up("ve", ve.memset(XP[:, :, 0:16], 0.0))
        need("ve", g.now("ve"))
        src, dst = XC, XP
        for n in range(4):
            shift = 1 << n
            t = up("ve", ve.tensor_tensor(dst[:, :, 16:16 + T], src[:, :, 16:16 + T], src[:, :, 16 - shift:16 - shift + T], ALU.add))
            need("ve", t)
            q, tile = slice(64 * (n % 2), 64 * (n % 2) + 64), n // 2
            t = up("ve", ve.tensor_tensor(dst[q, tile, 16:32], dst[q, tile, 16:32], fix[q, tile, :], ALU.mult))
            need("ve", t)
            t = up("ve", ve.scalar_tensor_tensor(HT[q, 4 + tile, :], dst[q, tile, 16:16 + T], invw[q, tile:tile + 1], HT[q, 4 + tile, :], ALU.mult, ALU.subtract))
            need("ve", t)
            src, dst = dst, src
        need("pe", t)
        for tile in range(2):
            for half in range(2):
                hs = slice(half * 512, (half + 1) * 512)
                b = banks.take()
                t = up("pe", pe.matmul(psum[b][:, :], grp[:, tile, :], HT[:, 4 + tile, hs], start=True, stop=True))
                need("ac", t)
                yc_ready = up("ac", ac.activation(HT[:, 4 + tile, hs], psum[b][:, :], ACT.Identity, scale=col3[:, P3["pool_scale"] + tile:P3["pool_scale"] + tile + 1]))
                banks.freed(b, yc_ready)

        s, w, got = ring2.fetch(cols8, w_in2_v[:, :, 2048:2560])
        need("pe", got)
        for tile in range(2):
            project2(w, tile * P, copy_to(lambda hs: HT[:, 8 + tile, hs]))
        q_ready = g.now("ac")
        conformer_taps(14, CONV_D)

        gate_tiles = {}
        gate_blocks = [(s, w, 2, 2)]
        qc = st.sb("attn_q", [P, 2, P])
        pr = [st.sb(f"attn_p{n}", [P, 2, MEM]) for n in range(2)]
        prT = [XC[:, n, 0:512].rearrange("p (n l) -> p n l", n=4) for n in range(2)]
        mx = st.sb("attn_max", [P, 4, 1])
        sm = st.sb("attn_sum", [P, 4, 1])
        need("pe", mem_ready)
        need("ac", q_ready)
        all_engines_meet()

        def attend(j):
            need("ac", g.before("pe"))
            qc_t = up("ac", ac.copy(qc[:, :, :], HT[:, 8:10, bass.ds(j * P, P)]))
            s_t, e_t = [], []
            need("pe", qc_t, g.before("ve"))
            for pair in range(2):
                for hh in range(2):
                    q = slice(64 * hh, 64 * hh + 64)
                    mm = pe.matmul(psum[2 * hh + pair][:, 0:MEM], qc[q, pair, :], K2T[q, pair, :], start=True, stop=True)
                s_t.append(up("pe", mm))
            for pair in range(2):
                need("ve", s_t[pair])
                m2 = mx[:, 2 * pair:2 * pair + 2, :]
                for hh in range(2):
                    t = up("ve", ve.tensor_reduce(m2[:, hh, :], psum[2 * hh + pair][:, 0:MEM], X, ALU.max))
                need("ve", t)
                t = up("ve", ve.tensor_scalar(m2, m2, -0.125, None, ALU.mult))
                need("ac", t)
                for hh in range(2):
                    h = 2 * pair + hh
                    t = up("ac", ac.activation(pr[pair][:, hh, :], psum[2 * hh + pair][:, 0:MEM], ACT.Exp, scale=0.125, bias=mx[:, h, :], accum_out=sm[:, h, :]))
                need("ve", t)
                s2 = sm[:, 2 * pair:2 * pair + 2, :]
                t = up("ve", ve.reciprocal(s2, s2))
                need("ve", t)
                t = up("ve", ve.tensor_tensor(pr[pair][:, :, :], pr[pair][:, :, :], s2.to_broadcast([P, 2, MEM]), ALU.mult))
                e_t.append(t)
            for pair in range(2):
                need("pe", e_t[pair])
                for n in range(4):
                    mm = pe.transpose(psum[4 + pair][:, n * P:(n + 1) * P], pr[pair][:, n // 2, (n % 2) * P:(n % 2 + 1) * P], ident[:, :])
                t = up("pe", mm)
                need("ac", t)
                t = up("ac", ac.copy(prT[pair][:, :, :], psum[4 + pair][:, :].rearrange("p (n l) -> p n l", n=4)))
                need("pe", t)
                for hh in range(2):
                    for m in range(2):
                        mm = pe.matmul(psum[6 + pair][:, hh * P:(hh + 1) * P], V2[:, m, pair * P:(pair + 1) * P], prT[pair][:, 2 * hh + m, :], start=m == 0, stop=m == 1)
                t = up("pe", mm)
                need("ve", t)
                for hh in range(2):
                    q = slice(64 * hh, 64 * hh + 64)
                    t = up("ve", ve.tensor_copy(HT[q, 8 + pair, bass.ds(j * P, P)], psum[6 + pair][q, hh * P:(hh + 1) * P]))

        g.loop(TT, {"pe_done": 6, "ve_done": 14, "ac_done": 7}, attend)
        all_engines_meet()
        tap("K2T", K2T[:, :, :])

        need("pe", *conv_t)
        for half in range(2):
            hs = slice(half * 512, (half + 1) * 512)
            b = banks.take()
            for tile in range(2):
                mm = pe.matmul(psum[b][:, :], ones[:, :], CV[:, tile, hs], start=tile == 0, stop=tile == 1)
            t = up("pe", mm)
            need("ve", t)
            for tile in range(2):
                t = up("ve", ve.scalar_tensor_tensor(CV[:, tile, hs], psum[b][:, :], -1.0 / DG, CV[:, tile, hs], ALU.mult, ALU.add))
            banks.freed(b, t)
            need("ac", t)
            for tile in range(2):
                t = up("ac", ac.activation(HP[:, tile, hs], CV[:, tile, hs], ACT.Square))
            need("pe", t)
            b = banks.take()
            for tile in range(2):
                mm = pe.matmul(psum[b][:, :], ones[:, :], HP[:, tile, hs], start=tile == 0, stop=tile == 1)
            t = up("pe", mm)
            need("ve", t)
            t = up("ve", ve.tensor_scalar(tm[0][:, :], psum[b][:, :], 1.0 / DG, LN_EPS, ALU.mult, ALU.add))
            banks.freed(b, t)
            need("ac", t)
            t = up("ac", ac.activation(tm[0][:, :], tm[0][:, :], ACT.Sqrt))
            need("ve", t)
            t = up("ve", ve.reciprocal(tm[0][:, :], tm[0][:, :]))
            need("ve", t)
            for tile in range(2):
                t = up("ve", ve.tensor_tensor(CV[:, tile, hs], CV[:, tile, hs], tm[0][:, :], ALU.mult))
            need("ac", t)
            for tile in range(2):
                t = up("ac", ac.activation(CV[:, tile, hs], CV[:, tile, hs], ACT.Silu, scale=col3[:, P3["cc_g"] + tile:P3["cc_g"] + tile + 1], bias=col3[:, P3["cc_b"] + tile:P3["cc_b"] + tile + 1]))
            need("pe", t, got_small)
            for tile in range(2):
                b = banks.take()
                for k in range(2):
                    mm = pe.matmul(psum[b][:, :], pw[:, k, tile * P:(tile + 1) * P], CV[:, k, hs], start=k == 0, stop=k == 1)
                t = up("pe", mm)
                need("ac", t)
                banks.freed(b, evacuate("ac", HT[:, 6 + tile, hs], psum[b][:, :]))
        all_engines_meet()
        tap("HT", HT[:, :, :])

        n = 0
        free = [None] * 3
        for c0 in (2048, 2560, 3072):
            if c0 > 2048:
                s, w, got = ring2.fetch(cols8, w_in2_v[:, :, c0:c0 + 512])
                need("pe", got)
            for jj in range(2 if c0 == 2048 else 0, 4):
                tile = (c0 - 2304) // P + jj

                def gated(bank, hs, t, tile=tile):
                    global_n = tile * 2 + hs.start // 512
                    buf = tm[global_n % 3]
                    need("ac", t, free[global_n % 3])
                    r = up("ac", ac.activation(buf[:, :], bank[:, :], ACT.Silu))
                    need("ve", r)
                    free[global_n % 3] = up("ve", ve.tensor_tensor(HT[:, tile, hs], HT[:, tile, hs], buf[:, :], ALU.mult))
                    return r
                last = project2(w, jj * P, gated)
            ring2.used(s, last)
        ht_ready = g.now("ve")
    all_engines_meet()

    with Scope() as st:
        XR = st.sb("residual", [P, TT, D])
        lnr = st.sb("ln_rows", [P, 2, D])
        stats = st.sb("ln_stats", [P, TT, 2, 6])
        mv = st.sb("ln_mv", [P, TT, 2])
        sd = st.sb("ln_sd", [P, TT, 1])
        got_xr = load("ac", "residual", XR[:, :, :], xf_rows.rearrange("(t p) n -> p t n", p=P))
        load("ac", "ln_rows", lnr[:, 0, :], A["ln_g_2"].partition_broadcast(P).rearrange("p a n -> p (a n)"))
        got_ln = load("ac", "ln_rows", lnr[:, 1, :], A["ln_b_2"].partition_broadcast(P).rearrange("p a n -> p (a n)"))
        w_out2_v = A["w_out_2"].rearrange("o (k p) n -> p (o k) n", p=P)
        halves = [ring2.fetch(cols8, w_out2_v[:, 0:KD, half * 512:(half + 1) * 512]) for half in range(2)]
        _, w_rest, got_rest = ring2.fetch(lambda s: s[:, 0:2 * D].rearrange("p (k n) -> p k n", k=2), w_out2_v[:, KD:NMIX, :])
        need("pe", ht_ready)
        need("ve", got_xr)
        out_rows = out.rearrange("b (t p) n -> p (b t) n", p=P)
        for half, (s, w, got) in enumerate(halves):
            need("pe", got, got_rest)
            hs = slice(half * 512, (half + 1) * 512)
            for j in range(TT):
                b = banks.take()
                for k in range(NMIX):
                    wk = w[:, k, :] if k < KD else w_rest[:, k - KD, hs]
                    mm = pe.matmul(psum[b][:, :], HT[:, k, j * P:(j + 1) * P], wk, start=k == 0, stop=k == NMIX - 1)
                t = up("pe", mm)
                need("ve", t)
                t = up("ve", ve.scalar_tensor_tensor(XR[:, j, hs], XR[:, j, hs], ALPHA, psum[b][:, :], ALU.mult, ALU.add))
                banks.freed(b, t)
                need("ve", t)
                t = up("ve", ve.bn_stats(stats[:, j, half, :], XR[:, j, hs]))
                if half:
                    need("ve", t)
                    t = up("ve", ve.bn_aggr(mv[:, j, :], stats[:, j, :, :].rearrange("p a b -> p (a b)")))
                    need("ve", t)
                    t = up("ve", ve.tensor_scalar(sd[:, j, :], mv[:, j, 1:2], LN_EPS, None, ALU.add))
                    need("ac", t)
                    t = up("ac", ac.activation(sd[:, j, :], sd[:, j, :], ACT.Sqrt))
                    need("ve", t)
                    t = up("ve", ve.reciprocal(sd[:, j, :], sd[:, j, :]))
                    need("ve", t)
                    t = up("ve", ve.tensor_scalar(XR[:, j, :], XR[:, j, :], mv[:, j, 0:1], sd[:, j, :], ALU.subtract, ALU.mult))
                    need("po", t, got_ln)
                    t = up("po", po.tensor_tensor(XR[:, j, :], XR[:, j, :], lnr[:, 0, :], ALU.mult))
                    need("po", t)
                    t = up("po", po.tensor_tensor(XR[:, j, :], XR[:, j, :], lnr[:, 1, :], ALU.add))
                    need("sp", t)
                    stored_out = load("sp", "out_stored", out_rows[:, j, :], XR[:, j, :])
        need("sp", stored_out)
    two.__exit__()
    top.__exit__()


INPUTS = [
    "x", "c", "ctx", "c_ctx", "w_ada", "b_ada", "g_norm1", "w_in", "b_gates", "w_conv", "w_fourier",
    "w_mlstm", "w_out", "g_norm2", "w_router", "w_gate_e", "w_up_e", "w_down_e", "g_final", "mem_2",
    "w_in_2", "conv_a_w_2", "sg_ln_g_2", "sg_ln_b_2", "sg_w_2", "sg_b_2", "pool_w_2", "pool_scale_2",
    "cc_dw_w_2", "cc_dw_b_2", "cc_ln_g_2", "cc_ln_b_2", "cc_pw_w_2", "w_kv_2", "w_out_2", "ln_g_2", "ln_b_2",
]


def constants():
    j = np.arange(P)
    tri = np.zeros((P, 2, P), np.float32)
    tri[:, 0, :] = np.where(j[:, None] <= j[None, :], 0.0, MASKED)
    tri[:, 1, :] = np.where(j[:, None] >= j[None, :], 0.0, MASKED)
    sel = np.zeros((32, 8, P), np.float32)
    for r in range(8):
        sel[r, r, :] = 1.0
    reset = np.ones((36, TA), np.float32)
    reset[0:4, 0::P] = 0.0
    reset[32:36, P - 1::P] = 0.0
    norm = 1.0 / math.sqrt(T * P)
    ang = 2 * np.pi * np.outer(j, j) / P
    channels = np.concatenate([np.cos(ang), np.sin(ang)], 1) * norm
    n = np.arange(512)
    angt = 2 * np.pi * (np.outer(n, n) % T) / T
    fix = np.ones((P, 2, 16), np.float32)
    inv = np.ones((P, 2), np.float32)
    for grp, w in enumerate((2, 4, 8, 16)):
        q = slice(64 * (grp % 2), 64 * (grp % 2) + 64)
        inv[q, grp // 2] = 1.0 / w
        for t in range(16):
            fix[q, grp // 2, t] = w / min(t + 1, w)
    return {
        "ident": np.eye(P, dtype=np.float32), "mask": tri, "sel": sel, "reset": reset,
        "dft_channels": channels.astype(np.float32), "dft_cos": np.cos(angt).astype(np.float32),
        "dft_sin": np.sin(angt).astype(np.float32),
        "alternating": np.where(n % 2 == 0, 1.0, -1.0).astype(np.float32)[None, :],
        "tril": np.tril(np.ones((P, P), np.float32)), "pool_fix": fix, "pool_inv": inv,
    }


def kernel(**inputs):
    import concourse.bacc as _bacc
    from concourse.bass_utils import run_bass_kernel_spmd as _run

    nc = _bacc.Bacc("TRN2", target_bir_lowering=False, num_devices=1)
    arrays = {f"in_{k}": np.ascontiguousarray(inputs[k]) for k in INPUTS}
    consts = {f"const_{k}": v for k, v in constants().items()}
    arrays.update(consts)
    aps = {k: nc.dram_tensor(k, a.shape, mybir.dt.from_np(a.dtype), kind="ExternalInput").ap() for k, a in arrays.items()}
    A = {k: aps[f"in_{k}"] for k in INPUTS}
    C = {k[6:]: aps[k] for k in consts}
    out = nc.dram_tensor("out", (1, T, D), F32, kind="ExternalOutput").ap()
    scratch = {k: nc.dram_tensor(f"{k}_rows", (T, D), F32, kind="Internal").ap() for k in ("xn", "x2", "xf")}
    scratch["ld"] = nc.dram_tensor("ld_rows", (2 * NH, TA), F32, kind="Internal").ap()
    build(nc, A, C, out, scratch)
    r = _run(nc, [arrays], core_ids=[0])
    return r.results[0]["out"]
```

```python
import math

import numpy as np

import concourse.bass as bass
from concourse import mybir

F32 = mybir.dt.float32
F32R = mybir.dt.float32r
U32 = mybir.dt.uint32
ALU = mybir.AluOpType
ACT = mybir.ActivationFunctionType
X = mybir.AxisListType.X

P = 128
D = 1024
KD = D // P
T = 1024
TT = T // P
NCTX = 256
TA = NCTX + T
D_F = 512
D_M = 512
NH = 4
DH = 128
OFF_QK = 512
OFF_V = 1536
OFF_O = 2048
OFF_G = 2560
OFF_BR = 2576
GRID_W = 64
ROWS = T // GRID_W
EPS = 1e-6
LN_EPS = 1e-5
NE = 16
CAP = 128
DG = 256
CONV_D = 31
CONV_A = 3
MEM = 256
DMIX = 1280
ALPHA = 2.0 ** 0.25
MASKED = -1.0e30
BANK = 512


class Flag:

    def __init__(self, nc, name):
        self.sem = nc.alloc_semaphore(name)
        self.name = name
        self.n = 0
        self.base = 0


class Program:

    def __init__(self, nc):
        self.nc = nc
        self.pe, self.ve, self.ac, self.po, self.sp = nc.tensor, nc.vector, nc.scalar, nc.gpsimd, nc.sync
        self.engines = {"pe": self.pe, "ve": self.ve, "ac": self.ac, "po": self.po, "sp": self.sp}
        self.done = {k: Flag(nc, f"{k}_done") for k in ("pe", "ve", "ac", "po")}
        self.met = {}
        self.loop_i = None
        self.loop_per = {}
        self.passed = {k: nc.alloc_semaphore(f"{k}_passed") for k in self.engines}
        self.flags = {f.name: f for f in self.done.values()}

    def flag(self, name):
        if name not in self.flags:
            self.flags[name] = Flag(self.nc, name)
        return self.flags[name]

    def up(self, e, ins):
        f = self.done[e]
        ins.then_inc(f.sem, 1)
        f.n += 1
        return (f, f.n)

    def now(self, e):
        return (self.done[e], self.done[e].n)

    def load(self, e, flag, out, in_, **kw):
        f = self.flag(flag)
        self.engines[e].dma_start(out, in_, **kw).then_inc(f.sem, 16)
        f.n += 16
        return (f, f.n)

    def before(self, flag_or_engine):
        f = self.done.get(flag_or_engine) or self.flag(flag_or_engine)
        return (f, f.base)

    def need(self, e, *ticks):
        register_wait = False
        latest = {}
        for tick in ticks:
            if tick is None:
                continue
            f, n = tick[:2]
            by_turn = self.loop_i is not None and f.name in self.loop_per and (len(tick) == 3 or n >= f.base)
            latest[(f.name, by_turn)] = max((n, f), latest.get((f.name, by_turn), (0, f)), key=lambda v: v[0])
        for (name, by_turn), (n, f) in latest.items():
            if by_turn:
                self.engines[e].wait_ge(f.sem, n + self.loop_i * self.loop_per[name])
                register_wait = True
            elif n > self.met.get((e, name), 0):
                self.engines[e].wait_ge(f.sem, n)
                self.met[(e, name)] = n
        if register_wait:
            self.engines[e].sem_inc(self.passed[e], 1)

    @staticmethod
    def carry(ticks):
        return {k: v and (v[0], v[1], True) for k, v in ticks.items()}

    def after(self, ticks, count, per):
        return {k: v and (v[0], v[1] + (count - 1) * per[v[0].name]) for k, v in ticks.items()}

    def loop(self, count, per, body):
        flags = {k: self.flag(k) for k in per}
        for f in flags.values():
            f.base = f.n
        start = {k: f.n for k, f in self.flags.items()}
        with self.nc.Fori(0, count) as i:
            self.loop_i, self.loop_per = i, per
            body(i)
            self.loop_i, self.loop_per = None, {}
        grown = {k: f.n - start.get(k, 0) for k, f in self.flags.items()}
        grown = {k: v for k, v in grown.items() if v}
        assert grown == per, f"the loop's turn raises {grown}"
        for f in flags.values():
            f.n = f.base + count * (f.n - f.base)


class Banks:

    def __init__(self, g, tensors):
        self.g = g
        self.t = tensors
        self.last = [None] * len(tensors)
        self.k = 0

    def take(self):
        b = self.k % len(self.t)
        self.k += 1
        self.g.need("pe", self.last[b])
        return b

    def freed(self, b, tick):
        self.last[b] = tick


class Ring:

    def __init__(self, g, name, slots):
        self.g, self.name, self.slots = g, name, slots
        self.busy = [None] * len(slots)
        self.k = 0

    def fetch(self, view, source):
        s = self.k % len(self.slots)
        self.k += 1
        self.g.need("sp", self.busy[s])
        out = view(self.slots[s])
        tick = self.g.load("sp", f"{self.name}_loaded_{s}", out, source)
        return s, out, tick

    def used(self, s, tick):
        self.busy[s] = tick


def build(nc, A, C, out, scratch, taps=None):
    g = Program(nc)
    pe, ve, ac, po, sp = g.pe, g.ve, g.ac, g.po, g.sp
    up, need, load = g.up, g.need, g.load
    psum = [nc.alloc_psum_tensor(f"bank{b}", [P, BANK], F32) for b in range(8)]
    banks = Banks(g, psum)

    class Scope:

        def __enter__(self):
            self.stack = []
            return self

        def sb(self, name, shape, dt=F32):
            cm = nc.sbuf_tensor(name, shape, dt)
            t = cm.__enter__()
            self.stack.append(cm)
            return t

        def __exit__(self, *a):
            while self.stack:
                self.stack.pop().__exit__(None, None, None)

    def all_engines_meet():
        for e in ("pe", "ve", "ac", "po", "sp"):
            need(e, *[g.now(k) for k in ("pe", "ve", "ac", "po") if k != e])

    def tap(name, view):
        if taps is not None and name in taps:
            all_engines_meet()
            need("sp", load("sp", "tap", taps[name], view))
            all_engines_meet()

    turn = [0]

    def evacuate(e, out_, in_, scale=None, bias=None, func=None):
        if e == "ac":
            if func is None and scale is None and bias is None:
                return up("ac", ac.copy(out_, in_))
            kw = {}
            if scale is not None:
                kw["scale"] = scale
            if bias is not None:
                kw["bias"] = bias
            return up("ac", ac.activation(out_, in_, func or ACT.Identity, **kw))
        if scale is None and bias is None:
            return up("ve", ve.tensor_copy(out_, in_))
        if bias is None:
            return up("ve", ve.tensor_scalar(out_, in_, scale, None, ALU.mult))
        return up("ve", ve.tensor_scalar(out_, in_, scale, bias, ALU.mult, ALU.add))

    def either():
        turn[0] += 1
        return "ac" if turn[0] % 2 else "ve"

    top = Scope().__enter__()
    sb = top.sb

    ident = sb("ident", [P, P])
    ones = sb("ones", [P, P])
    load("sp", "constants", ident[:, :], C["ident"])
    ready_ones = up("po", po.memset(ones[:, :], 1.0))
    params1 = sb("params1", [64, P])
    params2 = sb("params2", [72, P])
    params3 = sb("params3", [76, P])
    cond = sb("cond", [16, P])
    rows_of = lambda ap: ap.rearrange("a (r p) -> (a r) p", p=P)
    load("sp", "constants", cond[0:8, :], rows_of(A["c"]))
    load("sp", "constants", cond[8:16, :], A["c_ctx"].rearrange("(r p) -> r p", p=P))
    load("sp", "constants", params1[0:8, :], rows_of(A["g_norm1"]))
    load("sp", "constants", params1[8:16, :], rows_of(A["g_norm2"]))
    load("sp", "constants", params1[16:64, :], rows_of(A["b_ada"]))
    load("sp", "constants", params2[:, :], A["w_conv"].rearrange("o a b (r p) -> (o a b r) p", p=P))
    at = 0
    P3 = {}
    for name, src, n in (
        ("conv_a", A["conv_a_w_2"].rearrange("o k (r p) -> (o k r) p", p=P), 6),
        ("pool_scale", rows_of(A["pool_scale_2"]), 2),
        ("dw", A["cc_dw_w_2"].rearrange("o k (r p) -> (o k r) p", p=P), 62),
        ("dw_b", rows_of(A["cc_dw_b_2"]), 2),
        ("cc_g", rows_of(A["cc_ln_g_2"]), 2),
        ("cc_b", rows_of(A["cc_ln_b_2"]), 2),
    ):
        got_constants = load("sp", "constants", params3[at:at + n, :], src)
        P3[name] = at
        at += n
    col1 = sb("col1", [P, 64])
    col2 = sb("col2", [P, 72])
    col3 = sb("col3", [P, 76])
    silu_c = sb("silu_c", [P, 16])
    silu_rows = sb("silu_rows", [16, P])
    bgates = sb("bgates", [16, 1])
    got_bgates = load("sp", "bgates", bgates[:, :], A["b_gates"].rearrange("o k h -> (k h) o"))
    ga1b = sb("ga1b", [P, D])
    ga2b = sb("ga2b", [P, D])
    got_ga = load("sp", "b_ada_rows", ga1b[:, :], A["b_ada"][:, 2 * D:3 * D].partition_broadcast(P).rearrange("p a n -> p (a n)"))
    got_ga = load("sp", "b_ada_rows", ga2b[:, :], A["b_ada"][:, 5 * D:6 * D].partition_broadcast(P).rearrange("p a n -> p (a n)"))
    mod1 = sb("mod1", [P, 4, KD])
    mod2 = sb("mod2", [P, 2, KD])
    small = sb("small", [P, 64])
    VALC = sb("token_weights", [P, NE])
    IDXC = sb("token_of_slot", [P, NE], U32)

    need("ac", got_constants)
    silu_done = up("ac", ac.activation(silu_rows[:, :], cond[:, :], ACT.Silu))
    need("pe", got_constants, silu_done)
    for src, dst, n in ((silu_rows, silu_c, 16), (params1, col1, 64), (params2, col2, 72), (params3, col3, 76)):
        b = banks.take()
        turned = up("pe", pe.transpose(psum[b][:, 0:n], src[:, :], ident[0:n, 0:n]))
        need("ve", turned)
        columns_ready = evacuate("ve", dst[:, :], psum[b][:, 0:n])
        banks.freed(b, columns_ready)

    w_ada_v = A["w_ada"].rearrange("o (k p) n -> p (o k) n", p=P)
    w_in_v = A["w_in"].rearrange("o (k p) n -> p (o k) n", p=P)

    memory = sb("memory", [P, 2, 2, MEM])
    K2T, V2 = memory[:, 0, :, :], memory[:, 1, :, :]

    def address():
        return (nc.sbuf_base + 31) // 32 * 32

    wslots_at = address()
    wslots = [sb(f"wslot{s}", [P, KD * 512]) for s in range(3)]
    half_of_slot = [wslots[n // 2][:, (n % 2) * 2048:(n % 2) * 2048 + 2048] for n in range(6)]
    part_of_slot = [nc.alloc_sbuf_tensor_at(f"slot_part{n}", [P, 2048], F32R, offset=wslots_at + 8192 * n) for n in range(6)]

    class Pair:

        def __init__(self, raw, hi):
            self.raw, self.at_hi, self.used = raw, hi, None

        def fetch(self, source, *after):
            k, cols = source.shape[1:]
            view = lambda t: t[:, 0:k * cols].rearrange("p (k n) -> p k n", k=k)
            self.w, self.hi, self.lo = view(half_of_slot[self.raw]), view(part_of_slot[self.at_hi]), view(part_of_slot[self.raw])
            need("sp", self.used, *after)
            self.got = load("sp", f"half_slot{self.raw}_loaded", self.w, source)

        def split(self, *after):
            need("ac", self.got, self.used, *after)
            t = up("ac", ac.copy(self.hi, self.w))
            need("ve", t, self.got)
            self.ready = up("ve", ve.tensor_tensor(self.lo, self.w, self.hi.bitcast(F32), ALU.subtract))

    blk = Scope().__enter__()
    XT_at = address()
    XT = blk.sb("XT", [P, KD, TA])
    as_cols = lambda s: s[:, :].rearrange("p (k n) -> p k n", k=KD)
    as_rows4 = lambda s: s[:, :].rearrange("p (k n) -> p k n", k=4)
    ring = Ring(g, "w", wslots)

    with Scope() as st:
        xl = st.sb("x_rows", [P, TT, D])
        cl = st.sb("ctx_rows", [P, 2, D])
        junk = st.sb("junk", [P, D])
        ada = st.sb("ada_rows", [2, 2 * D])
        row_tiles = [(xl, j, A["x"]) for j in range(TT)] + [(cl, j, A["ctx"]) for j in range(2)]
        got_rows = []

        def fetch_rows(first, last_):
            for n in range(first, last_):
                dst, j, src = row_tiles[n]
                got_rows.append(load("sp", f"rows{n}_loaded", dst[:, j, :], src[0, j * P:(j + 1) * P, :]))

        ada_block = lambda blkn: ring.fetch(as_cols, w_ada_v[:, :, blkn * 512:(blkn + 1) * 512])
        ada_blocks = [ada_block(blkn) for blkn in range(3)]
        fetch_rows(0, 5)
        for blkn in range(4):
            if blkn == 3:
                ada_blocks.append(ada_block(3))
                fetch_rows(5, 10)
            s, w, got = ada_blocks[blkn]
            b = banks.take()
            need("pe", got, columns_ready)
            for k in range(KD):
                mm = pe.matmul(psum[b][0:2, :], silu_c[:, k:k + 9:8], w[:, k, :], start=k == 0, stop=k == KD - 1)
            t = up("pe", mm)
            ring.used(s, t)
            need("ve", t)
            ada_rows_ready = evacuate("ve", ada[:, blkn * 512:(blkn + 1) * 512], psum[b][0:2, :])
            banks.freed(b, ada_rows_ready)
        b = banks.take()
        need("pe", ada_rows_ready)
        for j in range(16):
            mm = pe.transpose(psum[b][:, 2 * j:2 * j + 2], ada[:, j * P:(j + 1) * P], ident[0:2, 0:2])
        t = up("pe", mm)
        need("ve", t)
        adac = psum[b][:, 0:32].rearrange("p (j v) -> p v j", v=2)
        sh_t = up("ve", ve.tensor_tensor(mod1[:, 1, :], adac[:, 0, 0:8], col1[:, 16:24], ALU.add))
        up("ve", ve.tensor_tensor(mod1[:, 3, :], adac[:, 1, 0:8], col1[:, 16:24], ALU.add))
        up("ve", ve.tensor_tensor(mod1[:, 0, :], adac[:, 0, 8:16], col1[:, 24:32], ALU.add))
        t = up("ve", ve.tensor_tensor(mod1[:, 2, :], adac[:, 1, 8:16], col1[:, 24:32], ALU.add))
        banks.freed(b, t)
        need("ve", t)
        for v in (0, 2):
            mod1_ready = up("ve", ve.scalar_tensor_tensor(mod1[:, v, :], mod1[:, v, :], 1.0, col1[:, 0:8], ALU.add, ALU.mult))

        for n, (src, j, _) in enumerate(row_tiles):
            need("ac", got_rows[n])
            squares = up("ac", ac.activation(junk[:, :], src[:, j, :], ACT.Square, accum_out=small[:, n:n + 1]))
            need("ac", squares)
        need("ve", squares)
        t = up("ve", ve.tensor_scalar(small[:, 16:26], small[:, 0:10], 1.0 / D, EPS, ALU.mult, ALU.add))
        need("ac", t)
        t = up("ac", ac.activation(small[:, 32:42], small[:, 16:26], ACT.Sqrt))
        need("ve", t)
        t = up("ve", ve.reciprocal(small[:, 48:58], small[:, 32:42]))
        need("ve", t)
        need("ac", t)
        for n, (src, j, _) in enumerate(row_tiles):
            e = "ac" if n % 3 == 1 else "ve"
            rows_scaled = evacuate(e, src[:, j, :], src[:, j, :], small[:, 48 + n:49 + n])

        need("pe", g.now("ac"), g.now("ve"))
        for k in range(KD):
            for src, j0, nj, col, v in ((cl, 0, 2, 0, 2), (xl, 0, 4, NCTX, 0), (xl, 4, 4, NCTX + 512, 0)):
                b = banks.take()
                for j in range(nj):
                    mm = pe.transpose(psum[b][:, j * P:(j + 1) * P], src[:, j0 + j, k * P:(k + 1) * P], ident[:, :])
                t = up("pe", mm)
                e = either()
                need(e, t, mod1_ready)
                t = evacuate(e, XT[:, k, col:col + nj * P], psum[b][:, 0:nj * P], mod1[:, v, k:k + 1], mod1[:, v + 1, k:k + 1])
                banks.freed(b, t)
    XT_ready = [g.now("ac"), g.now("ve")]
    all_engines_meet()
    tap("XT", XT[:, :, :])

    spans = ((0, 256), (256, 512), (768, 512))

    def project_transposed(w, c0, column_spans, finish, m=P):
        last = None
        for c, n in column_spans:
            b = banks.take()
            for k in range(KD):
                mm = pe.matmul(psum[b][0:m, 0:n], w[:, k, c0:c0 + m], XT[:, k, c:c + n], start=k == 0, stop=k == KD - 1)
            last = up("pe", mm)
            banks.freed(b, finish(psum[b], c, n, last))
        return last

    mix = Scope().__enter__()
    H_at = address()
    H = mix.sb("H", [P, TT, D_M])
    lstm = Scope().__enter__()
    KT = lstm.sb("KT", [P, NH, TA])
    QT = lstm.sb("QT", [P, NH, T])
    V = lstm.sb("V", [P, TA // P, NH, DH + 1])
    ones_col = up("po", po.memset(V[:, :, :, DH:DH + 1], 1.0))

    COL = lstm.sb("COL", [P, TA // P, 32])
    NC = TA // P

    def ada_half(n, aring, acc, first_part):
        part, k0 = n // 2, 4 * (n % 2)
        s, w, got = aring.fetch(as_rows4, w_ada_v[:, k0:k0 + 4, (4 + part) * 512:(5 + part) * 512])
        need("ve", got)
        o = acc[:, (part - first_part) * 512:(part - first_part + 1) * 512]
        for k in range(4):
            if k0 + k == 0:
                t = up("ve", ve.tensor_scalar(o, w[:, 0, :], silu_c[:, 0:1], None, ALU.mult))
            else:
                need("ve", g.now("ve"))
                t = up("ve", ve.scalar_tensor_tensor(o, w[:, k, :], silu_c[:, k0 + k:k0 + k + 1], o, ALU.mult, ALU.add))
        aring.used(s, t)
        return t

    def ada_rows(dst, acc, acc_ready):
        need("pe", acc_ready, ready_ones)
        need("ve", got_ga)
        for n in range(2):
            b = banks.take()
            t = up("pe", pe.matmul(psum[b][:, :], ones[:, :], acc[:, n * 512:(n + 1) * 512], start=True, stop=True))
            need("ve", t)
            o = dst[:, n * 512:(n + 1) * 512]
            banks.freed(b, up("ve", ve.tensor_tensor(o, psum[b][:, :], o, ALU.add)))

    with Scope() as st:
        acc_ga1 = st.sb("ada_acc_ga1", [P, D])
        aring_H = Ring(g, "ada", [H[:, 4 * n:4 * n + 4, :].rearrange("p a b -> p (a b)") for n in range(2)])
        grid = [st.sb(f"grid{i}", [P, (ROWS + 2) * (GRID_W + 2)]) for i in range(2)]
        gctx = [st.sb(f"gctx{i}", [P, NCTX + 2]) for i in range(2)]
        cacc = st.sb("conv_acc", [P, T])
        cacc2 = st.sb("conv_acc_ctx", [P, NCTX])
        in_H = lambda r, n: H[0:r, :, :].rearrange("p a b -> p (a b)")[:, n * TA:(n + 1) * TA]
        G = in_H(16, 0)
        M = in_H(36, 2)
        WA = in_H(36, 0)
        RS = in_H(36, 1)
        IG = KT[0:36, 0, :]
        FL = st.sb("FL", [36, TA])
        CU = KT[0:36, 1, :]
        R = CU[0:32, :]
        m0 = st.sb("m0", [36, NC, 1])
        lnscale = st.sb("lnscale", [36, 1])
        wg = st.sb("w_gates", [P, KD, 16])
        got_wg = load("sp", "w_gates", wg[:, :, :], w_in_v[:, :, OFF_G:OFF_BR])
        got_rs = load("sp", "reset", RS[:, :], C["reset"])
        up("po", po.memset(lnscale[:, :], 0.5 * math.log(DH)))
        zeroed = [up("po", po.memset(x[:, :], 0.0)) for x in (IG, FL, CU, M)][-1]
        zero = [up("po", po.memset(x[:, :], 0.0)) for x in grid + gctx][-1]
        need("pe", got_wg, *XT_ready)

        def gate_rows(bank, c, n, t):
            need("ac", t, got_bgates)
            return evacuate("ac", G[:, c:c + n], bank[0:16, 0:n], bias=bgates[:, 0:1])

        project_transposed(wg[:, :, :], 0, spans, gate_rows, m=16)
        gates_done = g.now("ac")

        def gate_steps():
            need("sp", gates_done, zeroed)
            for d in range(2):
                got_gates = load("sp", "gate_rows", IG[32 * d:32 * d + 4, :], G[8 * d:8 * d + 4, :])
                got_gates = load("sp", "gate_rows", FL[32 * d:32 * d + 4, :], G[8 * d + 4:8 * d + 8, :])
            need("ve", got_gates, got_rs)
            t = up("ve", ve.scalar_tensor_tensor(WA[:, :], FL[:, :], -1.0, FL[:, :], ALU.mult, ALU.max))
            yield
            need("ac", t)
            t = up("ac", ac.activation(WA[:, :], WA[:, :], ACT.Exp, scale=-1.0))
            need("ac", t)
            t = up("ac", ac.activation(WA[:, :], WA[:, :], ACT.Ln, bias=1.0))
            need("ve", t)
            t = up("ve", ve.scalar_tensor_tensor(FL[:, :], FL[:, :], 0.0, WA[:, :], ALU.min, ALU.subtract))
            need("ve", t)
            forward = (slice(0, TA, 1),)
            backward = (slice(NCTX - 1, None, -1), slice(TA - 1, NCTX - 1, -1))
            for d, pieces in enumerate((forward, backward)):
                q = slice(32 * d, 32 * d + 4)
                state = 0.0
                for piece in pieces:
                    up("ve", ve.tensor_tensor_scan(CU[q, piece], RS[q, piece], FL[q, piece], 0.0, ALU.mult, ALU.add))
                    t = up("ve", ve.tensor_tensor_scan(M[q, piece], FL[q, piece], IG[q, piece], state, ALU.add, ALU.max))
                    need("ve", t)
                    state = M[q, 0:1]
            scans = t
            chunked = lambda x, q: x[q, :].rearrange("r (c j) -> r c j", j=P)
            t = up("ve", ve.memset(m0[:, :, :], 0.0))
            need("ve", scans, t)
            mf, mb = chunked(M, slice(0, 4)), chunked(M, slice(32, 36))
            up("ve", ve.tensor_copy(m0[0:4, 1:NC, :], mf[:, 0:NC - 1, P - 1:P]))
            up("ve", ve.tensor_copy(m0[32:36, 0:1, :], mb[:, 1:2, 0:1]))
            up("ve", ve.tensor_copy(m0[32:36, 2:NC - 1, :], mb[:, 3:NC, 0:1]))
            t = up("ve", ve.tensor_copy(m0[32:36, NC - 1:NC, :], mb[:, 0:1, 0:1]))
            need("ve", t)
            q = slice(0, 36)
            m0b = m0[:, :, :].to_broadcast([36, NC, P])
            up("ve", ve.tensor_tensor(IG[:, :], IG[:, :], CU[:, :], ALU.subtract))
            t = up("ve", ve.tensor_tensor(FL[:, :], CU[:, :], M[:, :], ALU.subtract))
            need("ve", t)
            up("ve", ve.tensor_tensor(chunked(IG, q), chunked(IG, q), m0b, ALU.subtract))
            t = up("ve", ve.tensor_tensor(chunked(FL, q), chunked(FL, q), m0b, ALU.add))
            need("ve", t)
            for q, end in ((slice(0, 4), P - 1), (slice(32, 36), 0)):
                lasts = chunked(FL, q)[:, :, end:end + 1].to_broadcast([4, NC, P])
                wa_t = up("ve", ve.tensor_tensor(chunked(WA, q), chunked(IG, q), lasts, ALU.add))
            need("sp", t)
            for d in range(2):
                tk_gates["ld_stored"] = load("sp", "ld_stored", ld_rows[4 * d:4 * d + 4, :], FL[32 * d:32 * d + 4, :])
            yield
            yield
            need("ac", t, zeroed)
            up("ac", ac.activation(M[:, :], M[:, :], ACT.Exp, scale=-1.0, bias=lnscale[:, 0:1]))
            need("ac", wa_t)
            t = up("ac", ac.activation(WA[:, :], WA[:, :], ACT.Exp))
            need("sp", t, g.now("ve"))
            for n, src in enumerate((FL, IG, WA, M)):
                for d in range(2):
                    tk_gates["packed"] = load("sp", "packed", R[8 * n + 4 * d:8 * n + 4 * d + 4, :], src[32 * d:32 * d + 4, :])

        tk_gates = {}
        ld_rows = scratch["ld"]

        ring.k = 0
        s, w, got = ring.fetch(as_cols, w_in_v[:, :, OFF_V:OFF_V + 512])
        need("pe", got)
        qk_blocks = [ring.fetch(as_cols, w_in_v[:, :, OFF_QK + blkn * 512:OFF_QK + (blkn + 1) * 512]) for blkn in range(2)]
        steps = gate_steps()
        w_v = w

        def value_rows(j):
            b = banks.take()
            for k in range(KD):
                mm = pe.matmul(psum[b][:, :], XT[:, k, j * P:(j + 1) * P], w_v[:, k, :], start=k == 0, stop=k == KD - 1)
            last = up("pe", mm)
            ring.used(0, last)
            need("ac", last)
            banks.freed(b, evacuate("ac", V[:, j, :, 0:DH], psum[b][:, :].rearrange("p (h n) -> p h n", h=NH)))

        V_LATER = 2
        for j in range(TA // P - V_LATER):
            value_rows(j)
            if j > 0:
                next(steps, None)
        packed = tk_gates["packed"]
        need("sp", packed)
        need("pe", packed)
        b = banks.take()
        for c in range(NC):
            mm = pe.transpose(psum[b][:, 32 * c:32 * c + 32], R[:, c * P:(c + 1) * P], ident[0:32, 0:32])
        t = up("pe", mm)
        need("ve", t, packed)
        col_ready = evacuate("ve", COL[:, :, :], psum[b][:, 0:32 * NC].rearrange("p (c r) -> p c r", r=32))
        banks.freed(b, col_ready)

        conv_read = [None, None]
        silu_read = None
        for blkn in range(2):
            s, w, got = qk_blocks[blkn]
            need("pe", got)
            for h in range(NH):
                tile = blkn * 4 + h
                pad = grid[tile % 2][:, :].rearrange("p (r w) -> p r w", w=GRID_W + 2)
                cpad = gctx[tile % 2]

                def into_grid(bank, c, n, t, pad=pad, cpad=cpad):
                    need("ac", t, zero, conv_read[tile % 2])
                    if c == 0:
                        return evacuate("ac", cpad[:, 1:NCTX + 1], bank[:, 0:n])
                    r = (c - NCTX) // GRID_W
                    return evacuate("ac", pad[:, 1 + r:9 + r, 1:GRID_W + 1], bank[:, :].rearrange("p (r w) -> p r w", w=GRID_W))

                last = project_transposed(w, h * P, spans if blkn else spans[1:], into_grid)
                got_grid = g.now("ac")
                o = cacc[:, :].rearrange("p (r w) -> p r w", w=GRID_W)
                need("ve", got_grid, silu_read)
                for n in range(9):
                    src = pad[:, n // 3:n // 3 + ROWS, n % 3:n % 3 + GRID_W]
                    wc = col2[:, n * 8 + tile:n * 8 + tile + 1]
                    if n == 0:
                        t = up("ve", ve.tensor_scalar(o, src, wc, None, ALU.mult))
                    else:
                        need("ve", t)
                        t = up("ve", ve.scalar_tensor_tensor(o, src, wc, o, ALU.mult, ALU.add))
                if blkn:
                    for n in range(3):
                        src = cpad[:, n:n + NCTX]
                        wc = col2[:, (3 + n) * 8 + tile:(3 + n) * 8 + tile + 1]
                        if n == 0:
                            t = up("ve", ve.tensor_scalar(cacc2[:, :], src, wc, None, ALU.mult))
                        else:
                            need("ve", t)
                            t = up("ve", ve.scalar_tensor_tensor(cacc2[:, :], src, wc, cacc2[:, :], ALU.mult, ALU.add))
                conv_read[tile % 2] = t
                need("ac", t)
                if blkn:
                    up("ac", ac.activation(KT[:, h, NCTX:TA], cacc[:, :], ACT.Silu))
                    silu_read = up("ac", ac.activation(KT[:, h, 0:NCTX], cacc2[:, :], ACT.Silu))
                else:
                    silu_read = up("ac", ac.activation(QT[:, h, :], cacc[:, :], ACT.Silu))
                if tile == 0:
                    need("sp", col_ready, g.now("ve"), g.now("ac"))
                if 1 <= tile <= 4:
                    ada_ready = ada_half(tile - 1, aring_H, acc_ga1, 0)
                if tile == 5:
                    ada_rows(ga1b, acc_ga1, ada_ready)
            ring.used(s, last)
            if blkn == 0:
                ld_x = [wslots[d][:, :].rearrange("p (h n) -> p h n", h=NH) for d in range(2)]
                need("sp", tk_gates["ld_stored"])

                def fetch_ld_x(d):
                    need("sp", ring.busy[d])
                    return load("sp", "ld_x", ld_x[d], ld_rows[4 * d:4 * d + 4, NCTX:TA].partition_broadcast(P))
                fetch_ld_x(1)
        for j in range(TA // P - V_LATER, TA // P):
            value_rows(j)
        got_ld_x = fetch_ld_x(0)

    all_engines_meet()
    tap("KT", KT[:, :, :])
    tap("QT", QT[:, :, :])
    tap("V", V[:, :, :, :])

    with Scope() as st:
        maskt = st.sb("mask", [P, 2, P])
        ld_ctx = [st.sb(f"ld_ctx{d}", [P, NH, NCTX]) for d in range(2)]
        need("sp", tk_gates["ld_stored"])
        for d in range(2):
            got_ld_ctx = load("sp", "ld_ctx", ld_ctx[d][:, :, :], ld_rows[4 * d:4 * d + 4, 0:NCTX].partition_broadcast(P))
        got_mask = load("sp", "mask", maskt[:, :, :], C["mask"])
        pairs = [Pair(4, 0), Pair(5, 1)]
        for n in range(2):
            pairs[n].fetch(w_in_v[:, :, OFF_O + 256 * n:OFF_O + 256 * n + 256], ring.busy[2])
        CS = st.sb("cell", [P, 2, NH, DH + 1])
        kc = [st.sb(f"kc{d}", [P, NH, P]) for d in range(2)]
        dec = [st.sb(f"dec{d}", [P, NH, P]) for d in range(2)]
        dec_end = [st.sb(f"dec_end{d}", [P, NH, 1]) for d in range(2)]
        em = [st.sb(f"em{d}", [P, NH, P]) for d in range(2)]
        qd = [st.sb(f"qd{d}", [P, NH, P]) for d in range(2)]
        kw = [t[:, :, :].rearrange("p a (b j) -> p (a b) j", b=2) for t in (K2T, V2)]
        den = [st.sb(f"den{d}", [P, NH, 1]) for d in range(2)]
        cs_zero = up("ve", ve.memset(CS[:, :, :, :], 0.0))
        h_zero = up("po", po.memset(H[:, :, :], 0.0))
        need("po", got_mask)
        need("pe", ones_col)
        need("ac", silu_read)
        as_heads = lambda bank: bank[:, :].rearrange("p (h j) -> p h j", h=NH)

        def chunk_of(tensor3, c):
            return tensor3[:, :, bass.ds(c * P, P)]

        def value_of(c, h):
            return V[:, bass.ds(c, 1), h, :].rearrange("p a n -> p (a n)")

        def turn_of_states(chunks, outputs, tk):
            tk = dict(tk)
            for d in range(2):
                need("ac", tk[f"keys_read{d}"])
                tk[f"kc{d}"] = up("ac", ac.copy(kc[d][:, :, :], chunk_of(KT, chunks[d][0])))
            for d in range(2):
                c, cx = chunks[d]
                s_, t_, a_, b_ = (psum[4 * d + n] for n in range(4))
                ld = chunk_of(ld_x[d], cx) if outputs else chunk_of(ld_ctx[d], c)
                if outputs:
                    need("ac", tk[f"qd{d}"])
                    tk[f"dec{d}"] = up("ac", ac.activation(dec[d][:, :, :], ld, ACT.Exp))
                need("pe", tk[f"kc{d}"], tk[f"cell{d}"])
                for h in range(NH):
                    mm = pe.transpose(t_[:, h * P:(h + 1) * P], kc[d][:, h, :], ident[:, :])
                tk[f"turned{d}"] = tk[f"keys_read{d}"] = up("pe", mm)
                if outputs:
                    for h in range(NH):
                        mm = pe.matmul(s_[:, h * P:(h + 1) * P], kc[d][:, h, :], QT[:, h, bass.ds(cx * P, P)], start=True, stop=True)
                    tk[f"qk{d}"] = tk[f"keys_read{d}"] = up("pe", mm)
                    need("po", tk[f"out{d}"])
                    tk[f"masked{d}"] = up("po", po.tensor_tensor(em[d][:, :, :], ld, maskt[:, d:d + 1, :].to_broadcast([P, NH, P]), ALU.add))
                    need("po", tk[f"dec{d}"])
                    tk[f"qd{d}"] = up("po", po.tensor_tensor(qd[d][:, :, :], dec[d][:, :, :], chunk_of(QT, cx), ALU.mult))
            for d in range(2):
                c, cx = chunks[d]
                if outputs:
                    need("ac", tk[f"masked{d}"])
                    for h in range(NH):
                        tk[f"e{d}"] = up("ac", ac.activation(em[d][:, h, :], em[d][:, h, :], ACT.Exp, bias=COL[:, bass.ds(c, 1), 8 + 4 * d + h]))
                end = P - 1 if d == 0 else 0
                ld_end = (ld_x[d] if outputs else ld_ctx[d])[:, :, bass.ds((cx if outputs else c) * P + end, 1)]
                need("ac", tk[f"cell{d}"], tk.pop("ld_rows", None))
                tk[f"end{d}"] = up("ac", ac.activation(dec_end[d][:, :, :], ld_end, ACT.Exp))
            for d in range(2):
                c = chunks[d][0]
                s_, t_, a_, b_ = (psum[4 * d + n] for n in range(4))
                need("ve", tk[f"turned{d}"], tk[f"added{d}"])
                wa = COL[:, bass.ds(c, 1), 16 + 4 * d:20 + 4 * d].rearrange("p a h -> p (a h)").unsqueeze(2).to_broadcast([P, NH, P])
                tk[f"kw{d}"] = up("ve", ve.tensor_tensor(kw[d][:, :, :], as_heads(t_), wa, ALU.mult))
                if outputs:
                    need("ve", tk[f"qk{d}"], tk[f"e{d}"])
                    tk[f"p{d}"] = up("ve", ve.tensor_tensor(em[d][:, :, :], as_heads(s_), em[d][:, :, :], ALU.mult))
            for d in range(2):
                c, cx = chunks[d]
                s_, t_, a_, b_ = (psum[4 * d + n] for n in range(4))
                need("pe", tk[f"cell{d}"])
                if outputs:
                    need("pe", tk[f"p{d}"], tk[f"qd{d}"], tk[f"h{d}"])
                    out_t = []
                    for h in range(NH):
                        o = (a_ if h < 2 else b_)[:, (h % 2) * 129:(h % 2) * 129 + 129]
                        pe.matmul(o, em[d][:, h, :], value_of(c, h), start=True, stop=False)
                        mm = pe.matmul(o, qd[d][:, h, :], CS[:, d, h, :], start=False, stop=True)
                        if h % 2:
                            out_t.append(up("pe", mm))
                    tk[f"out{d}"] = out_t[1]
                need("pe", tk[f"kw{d}"])
                for h in range(NH):
                    o = (t_ if h < 2 else s_)[:, (h % 2) * 129:(h % 2) * 129 + 129]
                    mm = pe.matmul(o, kw[d][:, h, :], value_of(c, h), start=True, stop=True)
                tk[f"added{d}"] = up("pe", mm)
                if outputs:
                    for n, bank in enumerate((a_, b_)):
                        need("ve", out_t[n])
                        em_col = COL[:, bass.ds(c, 1), 24 + 4 * d + 2 * n:26 + 4 * d + 2 * n].rearrange("p a h -> p (a h)").unsqueeze(2)
                        ds_ = bank[:, 0:258].rearrange("p (h j) -> p h j", h=2)
                        t = up("ve", ve.tensor_tensor(den[d][:, 2 * n:2 * n + 2, :], ds_[:, :, DH:DH + 1], em_col, ALU.max))
                        need("ve", t)
                        t = up("ve", ve.scalar_tensor_tensor(den[d][:, 2 * n:2 * n + 2, :], ds_[:, :, DH:DH + 1], -1.0, den[d][:, 2 * n:2 * n + 2, :], ALU.mult, ALU.max))
                    need("ve", t)
                    t = up("ve", ve.reciprocal(den[d][:, :, :], den[d][:, :, :]))
                    need("ve", t)
                    for h in range(NH):
                        o = H[:, bass.ds(cx, 1), h * P:(h + 1) * P].rearrange("p a n -> p (a n)")
                        tk[f"h{d}"] = up("ve", ve.scalar_tensor_tensor(o, (a_ if h < 2 else b_)[:, (h % 2) * 129:(h % 2) * 129 + DH], den[d][:, h, :], o, ALU.mult, ALU.add))
                need("ve", tk[f"added{d}"], tk[f"end{d}"])
                for h in range(NH):
                    o = CS[:, d, h, :]
                    u = (t_ if h < 2 else s_)[:, (h % 2) * 129:(h % 2) * 129 + 129]
                    tk[f"cell{d}"] = up("ve", ve.scalar_tensor_tensor(o, o, dec_end[d][:, h, :], u, ALU.mult, ALU.add))
            need("ve", tk["cell1"])
            return tk

        need("ve", cs_zero)
        tk = {f"{k}{d}": None for d in range(2) for k in ("keys_read", "qd", "out", "added", "h")}
        tk["cell0"] = tk["cell1"] = cs_zero
        tk["ld_rows"] = got_ld_ctx
        for step in range(2):
            tk = turn_of_states(((step, None), (1 - step, None)), False, tk)
        tap("CS", CS[:, :, :, :])
        need("ac", got_ld_x)
        need("po", got_ld_x)
        need("ve", h_zero)
        def x_turn(i, tk):
            return turn_of_states(((i + 2, i), (TT + 1 - i, TT - 1 - i)), True, tk)

        tk = x_turn(0, tk)
        per = {"pe_done": 10, "ve_done": 30, "ac_done": 14, "po_done": 4}
        g.loop(TT - 1, per, lambda i: x_turn(i + 1, g.carry(tk)))
    all_engines_meet()
    lstm.__exit__()
    tap("H", H[:, :, :])

    OT = mix.sb("OT", [P, NH, T])
    FT = mix.sb("FT", [P, NH, T])
    XH_at = address()
    XH_place = mix.sb("XT_hi_place", [P, KD * T])
    XH = nc.alloc_sbuf_tensor_at("XT_hi", [P, KD, T], F32R, offset=XH_at)
    XL_all = nc.alloc_sbuf_tensor_at("XT_lo", [P, KD, TA], F32R, offset=XT_at)
    XL = lambda k, cols: XL_all[:, k, NCTX + cols.start:NCTX + cols.stop]
    F, M_ = Pair(2, 3), Pair(0, 1)
    F_columns = lambda n: w_in_v[:, :, OFF_BR + 256 * n:OFF_BR + 256 * n + 256]
    M_columns = lambda n: w_in_v[:, :, OFF_BR + D + 256 * n:OFF_BR + D + 256 * n + 256]

    def product3(bank, pair, c0, cols):
        need("pe", pair.ready)
        for k in range(KD):
            pe.matmul(bank, pair.hi[:, k, c0:c0 + P], XH[:, k, cols], start=k == 0, stop=False)
            pe.matmul(bank, pair.hi[:, k, c0:c0 + P], XL(k, cols), start=False, stop=False)
            mm = pe.matmul(bank, pair.lo[:, k, c0:c0 + P], XH[:, k, cols], start=False, stop=k == KD - 1)
        pair.used = up("pe", mm)
        return pair.used

    with Scope() as st:
        og = [st.sb(f"o_gate{n}", [P, 256]) for n in range(2)]
        acc = st.sb("ada_acc", [P, 3 * D])
        aring = Ring(g, "ada", [FT[:, 2 * n:2 * n + 2, :].rearrange("p h n -> p (h n)") for n in range(2)] + [st.sb("ada_block", [P, 2048])])
        freed = [None, None]
        pairs[0].split()
        x_split = []
        for k in range(KD):
            t = up("ac", ac.copy(XH[:, k, :], XT[:, k, NCTX:TA]))
            e = "po" if k % 3 == 2 else "ve"
            need(e, t)
            x_split.append(up(e, g.engines[e].tensor_tensor(XL(k, slice(0, T)), XT[:, k, NCTX:TA], XH[:, k, :].bitcast(F32), ALU.subtract)))
        pairs[1].split()
        F.fetch(F_columns(0))
        for n in range(2):
            pair = pairs[n]
            need("pe", pair.ready)
            for j in range(TT):
                b = banks.take()
                js = slice(j * P, (j + 1) * P)
                for k in range(KD):
                    need("pe", x_split[k])
                    pe.matmul(psum[b][:, 0:256], XH[:, k, js], pair.hi[:, k, :], start=k == 0, stop=False)
                    pe.matmul(psum[b][:, 0:256], XH[:, k, js], pair.lo[:, k, :], start=False, stop=False)
                    mm = pe.matmul(psum[b][:, 0:256], XL(k, js), pair.hi[:, k, :], start=False, stop=k == KD - 1)
                pair.used = up("pe", mm)
                need("ac", pair.used, freed[j % 2])
                t = up("ac", ac.activation(og[j % 2][:, :], psum[b][:, 0:256], ACT.Sigmoid))
                banks.freed(b, t)
                need("ve", t)
                o = H[:, j, 256 * n:256 * n + 256]
                freed[j % 2] = h_gated = up("ve", ve.tensor_tensor(o, o, og[j % 2][:, :], ALU.mult))
                if 8 * n + j < 12:
                    ada_ready = ada_half(4 + 8 * n + j, aring, acc, 2)
            pair.fetch(w_in_v[:, :, 256 * n:256 * n + 256])
        for pair in pairs:
            pair.split()
        F.split()
        need("pe", h_gated)
        for h in range(NH):
            for half in range(2):
                b = banks.take()
                for j in range(4):
                    mm = pe.transpose(psum[b][:, j * P:(j + 1) * P], H[:, 4 * half + j, h * P:(h + 1) * P], ident[:, :])
                t = up("pe", mm)
                e = "ac"
                need(e, t)
                banks.freed(b, evacuate(e, OT[:, h, half * 512:half * 512 + 512], psum[b][:, :]))
        OT_ready = [g.now("ac"), g.now("ve")]

        ada_rows(ga2b, acc[:, 2 * D:3 * D], ada_ready)
        b = banks.take()
        for j in range(16):
            mm = pe.matmul(psum[b][:, j:j + 1], acc[:, j * P:(j + 1) * P], ones[:, 0:1], start=True, stop=True)
        t = up("pe", mm)
        need("ve", t)
        up("ve", ve.tensor_tensor(mod2[:, 1, :], psum[b][:, 0:8], col1[:, 40:48], ALU.add))
        t = up("ve", ve.tensor_tensor(mod2[:, 0, :], psum[b][:, 8:16], col1[:, 48:56], ALU.add))
        banks.freed(b, t)
        need("ve", t)
        mod2_ready = up("ve", ve.scalar_tensor_tensor(mod2[:, 0, :], mod2[:, 0, :], 1.0, col1[:, 8:16], ALU.add, ALU.mult))
    all_engines_meet()
    tap("ga1b", ga1b[:, :])
    tap("ga2b", ga2b[:, :])
    tap("mod2", mod2[:, :, :])
    with Scope() as st:
        uT = st.sb("uT", [P, NH, T])
        UE, UO = (FT[:, 2 * n:2 * n + 2, :].rearrange("p a (b n) -> p (a b) n", b=2) for n in range(2))
        cs = st.sb("dft_channels", [P, 2 * P])
        TC, TS = (half_of_slot[n].rearrange("p (k n) -> p k n", k=4) for n in (4, 5))
        alt = st.sb("alternating", [1, 512])
        altc = st.sb("alternating_col", [P, 1])
        got_dft = load("sp", "dft", cs[:, :], C["dft_channels"])
        got_dft = load("sp", "dft", alt[:, :], C["alternating"])
        got_dft = load("sp", "dft", altc[:, :], C["alternating"][:, 0:P].rearrange("a p -> p a"))

        AA = H[:, :, :].rearrange("p a (b c) -> p (a b c)", b=1).rearrange("p (t g n) -> p t g n", t=4, g=NH)
        A5 = st.sb("along_channels_512", [1, NH * P])
        Qs = K2T[:, :, :].rearrange("p a n -> p (a n)")
        t = up("ve", ve.memset(UO[:, :, 0:1], 0.0))
        for gi in range(NH):
            def into_u(bank, c, n, t, gi=gi):
                need("ac", t)
                return evacuate("ac", uT[:, gi, c - NCTX:c - NCTX + n], bank[:, 0:n])
            for half in range(2):
                b = banks.take()
                hs = slice(half * 512, half * 512 + 512)
                t = product3(psum[b][:, :], pairs[gi // 2], (gi % 2) * P, hs)
                banks.freed(b, into_u(psum[b], NCTX + half * 512, 512, t))
            if gi == 1:
                need("sp", pairs[0].used)
                load("sp", "dft", TC, C["dft_cos"].rearrange("(k p) n -> p k n", p=P))
                M_.fetch(M_columns(0))
            need("ve", g.now("ac"))
            up("ve", ve.tensor_copy(UE[:, gi, 0:1], uT[:, gi, 0:1]))
            up("ve", ve.tensor_tensor(UE[:, gi, 1:512], uT[:, gi, 1:512], uT[:, gi, T - 1:512:-1], ALU.add))
            up("ve", ve.tensor_tensor(UO[:, gi, 1:512], uT[:, gi, 1:512], uT[:, gi, T - 1:512:-1], ALU.subtract))
        need("sp", pairs[1].used)
        got_dft = load("sp", "dft", TS, C["dft_sin"].rearrange("(k p) n -> p k n", p=P))
        M_.split(pairs[1].used)
        folded = g.now("ve")
        need("pe", folded, got_dft)
        for nt in range(4):
            for pair in range(2):
                b = banks.take()
                for gi in range(2):
                    for part, src in enumerate((UE, UO)):
                        o = (gi * 2 + part) * P
                        mm = pe.matmul(psum[b][:, o:o + P], src[:, 2 * pair + gi, nt * P:(nt + 1) * P], cs[:, part * P:(part + 1) * P], start=True, stop=True)
                t = up("pe", mm)
                e = either()
                need(e, t)
                banks.freed(b, evacuate(e, AA[:, nt, 2 * pair:2 * pair + 2, :], psum[b][:, :].rearrange("p (g n) -> p g n", g=2)))
        b = banks.take()
        for gi in range(NH):
            mm = pe.matmul(psum[b][0:1, gi * P:(gi + 1) * P], uT[:, gi, 512:513], cs[:, 0:P], start=True, stop=True)
        t = up("pe", mm)
        need("ac", t)
        t = evacuate("ac", A5[:, :], psum[b][0:1, :])
        banks.freed(b, t)
        need("pe", g.now("ve"), t)
        qs_read = None
        for gi in range(NH):
            bp, bq, b5 = banks.take(), banks.take(), banks.take()
            for nt in range(4):
                mm = pe.matmul(psum[bq][:, :], AA[:, nt, gi, P:2 * P], TS[:, nt, :], start=nt == 0, stop=nt == 3)
            q_t = up("pe", mm)
            for nt in range(4):
                pe.matmul(psum[bp][:, :], AA[:, nt, gi, 0:P], TC[:, nt, :], start=nt == 0, stop=False)
            mm = pe.matmul(psum[bp][:, :], A5[0:1, gi * P:(gi + 1) * P], alt[0:1, :], start=False, stop=True)
            for nt in range(4):
                pe.matmul(psum[b5][:, 0:1], AA[:, nt, gi, 0:P], altc[:, 0:1], start=nt == 0, stop=False)
            mm = pe.matmul(psum[b5][:, 0:1], A5[0:1, gi * P:(gi + 1) * P], alt[0:1, 0:1], start=False, stop=True)
            p_t = up("pe", mm)
            need("ac", q_t, qs_read)
            t = evacuate("ac", Qs, psum[bq][:, :])
            banks.freed(bq, t)
            need("ve", t, p_t)
            up("ve", ve.tensor_tensor(FT[:, gi, 0:512], psum[bp][:, :], Qs[:, :], ALU.subtract))
            qs_read = up("ve", ve.tensor_tensor(FT[:, gi, T - 1:512:-1], psum[bp][:, 1:512], Qs[:, 1:512], ALU.add))
            banks.freed(bp, qs_read)
            fourier_ready = up("ve", ve.tensor_copy(FT[:, gi, 512:513], psum[b5][:, 0:1]))
            banks.freed(b5, fourier_ready)
    tap("OT", OT[:, :, :])
    tap("FT", FT[:, :, :])

    MG_b_at = address()
    MG_b = mix.sb("merged_b", [P, 4, T])
    MG_a = H[:, :, :].rearrange("p (k a) b -> p k (a b)", k=4)
    MG = lambda k, cols: (MG_a if k < 4 else MG_b)[:, k % 4, cols]
    with Scope() as st:
        w_out_v = A["w_out"].rearrange("o (k p) n -> p (o k) n", p=P)
        s1 = [st.sb(f"gate_f{n}", [P, 512]) for n in range(2)]
        s2 = [t[:, :, :].rearrange("p a n -> p (a n)") for t in (K2T, V2)]
        read = [None, None]
        w_out_blocks = []
        GROUPS = D // 256
        Y = [half_of_slot[4 + n].rearrange("p (m k n) -> p m k n", m=2, k=4) for n in range(2)]
        y_used = [fourier_ready, fourier_ready]

        def fetch_y(n):
            need("sp", y_used[n % 2])
            for m, name in enumerate(("w_fourier", "w_mlstm")):
                t = load("sp", f"half_slot{4 + n % 2}_loaded", Y[n % 2][:, m, :, :], A[name].rearrange("o (k p) n -> p (o k) n", p=P)[:, :, 256 * n:256 * n + 256])
            return t
        got_y = [fetch_y(0), fetch_y(1)]
        need("pe", *OT_ready, fourier_ready)
        n = 0
        for group in range(GROUPS):
            last_group = group == GROUPS - 1
            for jj in range(2):
                j = 2 * group + jj
                for half in range(2):
                    hs = slice(half * 512, (half + 1) * 512)
                    final = jj == 1 and half == 1
                    bg = []
                    for pair, columns in ((F, F_columns), (M_, M_columns)):
                        b = banks.take()
                        bg.append((b, product3(psum[b][:, :], pair, jj * P, hs)))
                        if final and not last_group:
                            pair.fetch(columns(group + 1))
                        elif final:
                            s = len(w_out_blocks)
                            need("sp", pair.used)
                            w = as_cols(wslots[1 - s])
                            w_out_blocks.append((s, w, load("sp", f"w_out{s}", w, w_out_v[:, :, s * 512:(s + 1) * 512])))
                        if group and jj == 0 and half == 0 and pair is F:
                            M_.split()
                    need("pe", got_y[group])
                    by = []
                    for m, src in enumerate((FT, OT)):
                        b = banks.take()
                        for k in range(4):
                            mm = pe.matmul(psum[b][:, :], Y[group % 2][:, m, k, jj * P:(jj + 1) * P], src[:, k, hs], start=k == 0, stop=k == 3)
                        by.append((b, up("pe", mm)))
                    if final:
                        y_used[group % 2] = by[-1][1]
                        if group + 2 < GROUPS:
                            got_y.append(fetch_y(group + 2))
                    for (b, t), dst in zip(bg, (s1[n % 2][:, :], s2[n % 2])):
                        need("ac", t, read[n % 2])
                        t = up("ac", ac.activation(dst, psum[b][:, :], ACT.Sigmoid))
                        banks.freed(b, t)
                    if final and not last_group:
                        F.split()
                    need("ve", t, by[0][1])
                    t1 = up("ve", ve.tensor_tensor(s1[n % 2][:, :], psum[by[0][0]][:, :], s1[n % 2][:, :], ALU.mult))
                    banks.freed(by[0][0], t1)
                    need("ve", by[1][1])
                    t = up("ve", ve.tensor_tensor(s2[n % 2], psum[by[1][0]][:, :], s2[n % 2], ALU.mult))
                    banks.freed(by[1][0], t)
                    need("ve", t)
                    read[n % 2] = merged_ready = up("ve", ve.tensor_tensor(MG(j, hs), s1[n % 2][:, :], s2[n % 2], ALU.add))
                    n += 1

    xn_rows, x2_rows, xf_rows = scratch["xn"], scratch["x2"], scratch["xf"]
    UNITS, SLOTS, AHEAD = 12, 6, 4
    source = {"g": A["w_gate_e"], "u": A["w_up_e"], "d": A["w_down_e"]}
    source = {k: v.rearrange("o e (k p) n -> (o e) p k n", p=P) for k, v in source.items()}
    raw = [wslots[n // 2][:, (n % 2) * 2048:(n % 2) * 2048 + 2048].rearrange("p (k n) -> p k n", k=4) for n in range(SLOTS)]
    split_slot = lambda name, n: nc.alloc_sbuf_tensor_at(f"expert_w_{name}{n}", [P, 4, 512], F32R, offset=H_at + 8192 * (2 * (0, 2, 3, 4, 5, 1)[n] + (name == "lo")))
    hi = [split_slot("hi", n) for n in range(SLOTS)]
    lo = [split_slot("lo", n) for n in range(SLOTS)]

    def expert_unit(u, e):
        m, half = ("g", "u", "g", "u", "d", "d")[u // 2], (0, 0, 1, 1, 0, 1)[u // 2]
        v = source[m][bass.ds(e, 1), :, 4 * (u % 2):4 * (u % 2) + 4, 512 * half:512 * half + 512]
        return v.rearrange("a p k n -> (a p) k n")

    def fetch(u, e, tk):
        e, u = (e + 1, u - UNITS) if u >= UNITS else (e, u)
        r = u % SLOTS
        need("sp", tk[f"raw{r}"])
        load("sp", f"expert_raw{r}_loaded", raw[r], expert_unit(u, e))

    def split(u, tk, lo_by="ve"):
        r = u % SLOTS
        landed = (g.flag(f"expert_raw{r}_loaded"), g.flag(f"expert_raw{r}_loaded").n)
        need("ac", landed, tk[f"used{r}"])
        t = up("ac", ac.copy(hi[r][:, :, :], raw[r]))
        need(lo_by, t, landed, tk[f"used{r}"])
        t = up(lo_by, g.engines[lo_by].tensor_tensor(lo[r][:, :, :], raw[r], hi[r][:, :, :].bitcast(F32), ALU.subtract))
        tk[f"ready{r}"] = tk[f"raw{r}"] = t

    with Scope() as st:
        X2 = XT[:, :, 0:D]
        tmp = [st.sb(f"attn_tmp{n}", [P, 512]) for n in range(2)]
        xn = [FT[:, n, :] for n in range(3)]
        junk = FT[:, 3, :]
        wr = st.sb("w_router", [P, KD, NE])
        need("ac", merged_ready)
        got_wr = load("ac", "w_router", wr[:, :, :], A["w_router"].rearrange("o (k p) n -> p (o k) n", p=P))
        need("sp", merged_ready)
        x_tile = lambda v, j: v[j * P:(j + 1) * P, :]
        got_x2 = [load("sp", f"x_again{j}", X2[:, j, :], x_tile(A["x"].rearrange("b t n -> (b t) n"), j)) for j in range(TT)]
        need("pe", merged_ready)
        x2_ready, xn_ready, turned_x = [None] * TT, [None] * TT, [None] * TT
        logits_bank = None

        def norm2(j):
            need("ac", x2_ready[j], xn_ready[j - 1] if j else None)
            t = up("ac", ac.activation(junk, X2[:, j, :], ACT.Square, accum_out=small[:, j:j + 1]))
            need("ve", t)
            t = up("ve", ve.tensor_scalar(small[:, 16 + j:17 + j], small[:, j:j + 1], 1.0 / D, EPS, ALU.mult, ALU.add))
            need("ac", t)
            t = up("ac", ac.activation(small[:, 32 + j:33 + j], small[:, 16 + j:17 + j], ACT.Sqrt))
            need("ve", t)
            t = up("ve", ve.reciprocal(small[:, 48 + j:49 + j], small[:, 32 + j:33 + j]))
            need("ve", t, xn_stored[j - 3] if j > 2 else None, turned_x[j - 3] if j > 2 else None)
            xn_ready[j] = up("ve", ve.tensor_scalar(xn[j % 3], X2[:, j, :], small[:, 48 + j:49 + j], None, ALU.mult))
            need("sp", xn_ready[j])
            xn_stored.append(load("sp", f"xn_stored{j % 3}", x_tile(xn_rows, j), xn[j % 3]))

        def turn_rows(j):
            need("pe", xn_ready[j])
            for half in range(2):
                b = banks.take()
                for k in range(4):
                    kk = 4 * half + k
                    mm = pe.transpose(psum[b][:, k * P:(k + 1) * P], xn[j % 3][:, kk * P:(kk + 1) * P], ident[:, :])
                turned_x[j] = up("pe", mm)
                need("ac", turned_x[j], mod2_ready)
                for k in range(4):
                    kk = 4 * half + k
                    t = evacuate("ac", MG(kk, slice(j * P, (j + 1) * P)), psum[b][:, k * P:(k + 1) * P], mod2[:, 0, kk:kk + 1], mod2[:, 1, kk:kk + 1])
                banks.freed(b, t)
            return t

        MH = nc.alloc_sbuf_tensor_at("merged_hi", [P, KD, T], F32R, offset=XH_at)
        ML_ = [nc.alloc_sbuf_tensor_at(f"merged_lo{n}", [P, 4, T], F32R, offset=at) for n, at in enumerate((H_at, MG_b_at))]
        ML = lambda k, cols: ML_[k // 4][:, k % 4, cols]
        WH = [nc.alloc_sbuf_tensor_at(f"w_out_hi{n}", [P, KD, 512], F32R, offset=at) for n, at in enumerate((wslots_at + 2 * 16384, H_at + 16384))]
        WL = [nc.alloc_sbuf_tensor_at(f"w_out_lo{n}", [P, KD, 512], F32R, offset=wslots_at + 16384 * (1 - n)) for n in range(2)]
        for e in ("ac", "ve"):
            need(e, merged_ready)
        merged_parts, w_parts = [], [[], []]

        def split_w_out(n, k):
            _, w, got = w_out_blocks[n]
            need("ac", got)
            t = up("ac", ac.copy(WH[n][:, k, :], w[:, k, :]))
            need("ve", t, got)
            w_parts[n].append(up("ve", ve.tensor_tensor(WL[n][:, k, :], w[:, k, :], WH[n][:, k, :].bitcast(F32), ALU.subtract)))

        every = slice(0, T)
        for k in range(KD):
            split_w_out(0, k)
            t = up("ac", ac.copy(MH[:, k, :], MG(k, every)))
            need("ve", t)
            merged_parts.append(up("ve", ve.tensor_tensor(ML(k, every), MG(k, every), MH[:, k, :].bitcast(F32), ALU.subtract)))

        xn_stored = []
        for half in range(2):
            hs = slice(half * 512, (half + 1) * 512)
            group = 1 if half else 4
            for j in range(TT):
                if j % group == 0:
                    taken = [banks.take() for _ in range(group)]
                    for k in range(KD):
                        need("pe", merged_parts[k], w_parts[half][k])
                        for jj in range(group):
                            js, bank = slice((j + jj) * P, (j + jj + 1) * P), psum[taken[jj]]
                            pe.matmul(bank[:, :], MH[:, k, js], WH[half][:, k, :], start=k == 0, stop=False)
                            pe.matmul(bank[:, :], MH[:, k, js], WL[half][:, k, :], start=False, stop=False)
                            mm = pe.matmul(bank[:, :], ML(k, js), WH[half][:, k, :], start=False, stop=k == KD - 1)
                    last = up("pe", mm)
                b = taken[j % group]
                if half == 0:
                    split_w_out(1, j)
                need("ve", last, got_x2[j])
                t = up("ve", ve.tensor_tensor(tmp[j % 2][:, :], psum[b][:, :], ga1b[:, hs], ALU.mult))
                banks.freed(b, t)
                need("ve", t)
                x2_ready[j] = up("ve", ve.tensor_tensor(X2[:, j, hs], X2[:, j, hs], tmp[j % 2][:, :], ALU.add))
                if half:
                    need("sp", x2_ready[j])
                    x2_stored = load("sp", "x2_stored", x_tile(x2_rows, j), X2[:, j, :])
                    if j > 0:
                        norm2(j - 1)
                    if j > 1:
                        turn_rows(j - 2)
        norm2(TT - 1)
        tk = {k: None for k in ["x_read", "xT", "hidT0", "hidT1", "y0", "y1"] + [f"{n}{r}" for n in ("raw", "used") for r in range(SLOTS)]}
        need("sp", last)
        for u in range(SLOTS):
            fetch(u, 0, tk)
        turn_rows(TT - 2)
        t = turn_rows(TT - 1)
        need("pe", t, got_wr)
        b = banks.take()
        for j in range(TT):
            for k in range(KD):
                mm = pe.matmul(psum[b][:, j * NE:(j + 1) * NE], MG(k, slice(j * P, (j + 1) * P)), wr[:, k, :], start=k == 0, stop=k == KD - 1)
        logits = up("pe", mm)

        old = XT[:, :, :].rearrange("p k n -> p (k n)")
        mem_rows = old[:, 0:2048].rearrange("p (m n) -> p m n", m=2)
        memT = old[:, 2048:4096].rearrange("p (k n) -> p k n", k=KD)
        w_kv = old[:, 4096:8192].rearrange("p (k n) -> p k n", k=KD)
        need("ac", x2_stored, xn_ready[TT - 1])
        got_mem = load("ac", "mem", mem_rows, A["mem_2"].rearrange("b (m p) n -> p (b m) n", p=P))
        got_kv = load("ac", "w_kv", w_kv, A["w_kv_2"].rearrange("o (k p) n -> p (o k) n", p=P))

        def memory_steps():
            need("pe", got_mem)
            for k2 in range(4):
                b = banks.take()
                for k in range(2):
                    for m in range(2):
                        mm = pe.transpose(psum[b][:, (2 * k + m) * P:(2 * k + m + 1) * P], mem_rows[:, m, (2 * k2 + k) * P:(2 * k2 + k + 1) * P], ident[:, :])
                t = up("pe", mm)
                need("ac", t)
                t = evacuate("ac", memT[:, 2 * k2:2 * k2 + 2, :], psum[b][:, :].rearrange("p (k n) -> p k n", k=2))
                banks.freed(b, t)
            need("pe", got_kv, t)
            for tile in range(2):
                b = banks.take()
                for k in range(KD):
                    mm = pe.matmul(psum[b][:, 0:MEM], w_kv[:, k, tile * P:(tile + 1) * P], memT[:, k, :], start=k == 0, stop=k == KD - 1)
                t = up("pe", mm)
                need("ac", t)
                banks.freed(b, evacuate("ac", K2T[:, tile, :], psum[b][:, 0:MEM]))
            for m in range(2):
                b = banks.take()
                for k in range(KD):
                    mm = pe.matmul(psum[b][:, 0:DG], memT[:, k, m * P:(m + 1) * P], w_kv[:, k, DG:2 * DG], start=k == 0, stop=k == KD - 1)
                t = up("pe", mm)
                need("ac", t)
                banks.freed(b, evacuate("ac", V2[:, m, :], psum[b][:, 0:DG]))
            return g.now("ac")

        af = st.sb("affinity", [P, TT, NE])
        red = st.sb("softmax_red", [P, 2, TT, 1])
        lg = psum[b][:, 0:TT * NE].rearrange("p (j e) -> p j e", e=NE)
        need("ve", logits)
        t = up("ve", ve.tensor_reduce(red[:, 0, :, :].rearrange("p j a -> p (j a)"), lg, X, ALU.max))
        need("ve", t)
        t = up("ve", ve.tensor_tensor(af[:, :, :], lg, red[:, 0, :, :].to_broadcast([P, TT, NE]), ALU.subtract))
        banks.freed(b, t)
        need("ac", t)
        t = up("ac", ac.activation(af[:, :, :], af[:, :, :], ACT.Exp))
        need("ve", t)
        t = up("ve", ve.tensor_reduce(red[:, 1, :, :].rearrange("p j a -> p (j a)"), af[:, :, :], X, ALU.add))
        need("ve", t)
        t = up("ve", ve.reciprocal(red[:, 1, :, :], red[:, 1, :, :]))
        need("ve", t)
        af_ready = up("ve", ve.tensor_tensor(af[:, :, :], af[:, :, :], red[:, 1, :, :].to_broadcast([P, TT, NE]), ALU.mult))
        tap("af", af[:, :, :])
        AT = OT[0:NE, 0, :]
        need("pe", af_ready)
        for half in range(2):
            b = banks.take()
            for j in range(4):
                mm = pe.transpose(psum[b][0:NE, j * P:(j + 1) * P], af[:, 4 * half + j, :], ident[:, :])
            t = up("pe", mm)
            need("ve", t)
            t = evacuate("ve", AT[:, half * 512:(half + 1) * 512], psum[b][0:NE, :])
            banks.freed(b, t)
        mem_ready = memory_steps()
        for e in ("ac", "po"):
            need(e, logits, *xn_stored)
        for u in range(AHEAD):
            split(u, tk, lo_by="po")
            fetch(u + SLOTS, 0, tk)
        val = st.sb("top_values", [NE, CAP])
        idx = st.sb("top_tokens", [NE, CAP], U32)
        idxf = st.sb("top_tokens_f", [NE, CAP])
        need("ve", t)
        for r in range(CAP // 8):
            v8, i8 = val[:, 8 * r:8 * r + 8], idx[:, 8 * r:8 * r + 8]
            t = up("ve", ve.max(v8, AT))
            need("ve", t)
            t = up("ve", ve.max_index(i8, v8, AT))
            t = up("ve", ve.match_replace(AT, v8, AT, -1.0))
            need("ve", t)
        t = up("ve", ve.tensor_copy(idxf[:, :], idx[:, :]))
        need("pe", t)
        b = banks.take()
        pe.transpose(psum[b][:, 0:NE], val[:, :], ident[0:NE, 0:NE])
        t = up("pe", pe.transpose(psum[b][:, NE:2 * NE], idxf[:, :], ident[0:NE, 0:NE]))
        need("ve", t)
        up("ve", ve.tensor_copy(VALC[:, :], psum[b][:, 0:NE]))
        top_ready = up("ve", ve.tensor_copy(IDXC[:, :], psum[b][:, NE:2 * NE]))
        banks.freed(b, top_ready)
    all_engines_meet()
    for e in ("po", "ac", "sp"):
        need(e, x2_stored, *xn_stored)
    mix.__exit__()
    blk.__exit__()

    with Scope() as st:
        xs = st.sb("expert_x", [P, D])
        xm = st.sb("expert_x_mod", [P, KD, P])
        xh = st.sb("expert_xT_hi", [P, KD, P], F32R)
        xlo = st.sb("expert_xT_lo", [P, KD, P], F32R)
        hid = st.sb("expert_hidden", [P, D])
        hid_hi = st.sb("expert_hidT_hi", [P, KD, P], F32R)
        hid_lo = st.sb("expert_hidT_lo", [P, KD, P], F32R)
        y = st.sb("expert_y", [P, D])
        idx_g = st.sb("gather_tokens", [P, 1], U32)
        idx_s = st.sb("scatter_tokens", [P, 1], U32)
        silu = st.sb("expert_silu", [P, 2, 512])

        def product(bank, xhi, xlow, u, tk):
            r = u % SLOTS
            need("pe", tk[f"ready{r}"])
            for k in range(4):
                kk = 4 * (u % 2) + k
                pe.matmul(bank[:, :], xhi[:, kk, :], hi[r][:, k, :], start=kk == 0, stop=False)
                pe.matmul(bank[:, :], xhi[:, kk, :], lo[r][:, k, :], start=False, stop=False)
                mm = pe.matmul(bank[:, :], xlow[:, kk, :], hi[r][:, k, :], start=False, stop=kk == KD - 1)
            tk[f"used{r}"] = up("pe", mm)
            return tk[f"used{r}"]

        def gather(e, tk):
            need("po", tk["x_read"])
            t = up("po", po.tensor_copy(idx_g[:, :], IDXC[:, bass.ds(e, 1)]))
            need("po", t)
            f = g.flag("gathered")
            po.indirect_dma_start(xs[:, :], None, xn_rows, bass.IndirectOffsetOnAxis(idx_g[:, :], 0)).then_inc(f.sem, 16)
            f.n += 16
            tk["gathered"] = (f, f.n)

        def turn_x(tk):
            need("pe", tk["gathered"], tk["xT"])
            for half in range(2):
                for k in range(4):
                    kk = 4 * half + k
                    mm = pe.transpose(psum[4 + half][:, k * P:(k + 1) * P], xs[:, kk * P:(kk + 1) * P], ident[:, :])
                tk["x_read"] = up("pe", mm)

        def split_x(tk):
            need("ac", tk["x_read"], tk["xT"])
            for kk in range(KD):
                r = up("ac", ac.activation(xm[:, kk, :], psum[4 + kk // 4][:, (kk % 4) * P:(kk % 4 + 1) * P], ACT.Identity, scale=mod2[:, 0, kk:kk + 1], bias=mod2[:, 1, kk:kk + 1]))
            need("ac", r)
            r = up("ac", ac.copy(xh[:, :, :], xm[:, :, :]))
            need("ve", r)
            tk["xT"] = up("ve", ve.tensor_tensor(xlo[:, :, :], xm[:, :, :], xh[:, :, :].bitcast(F32), ALU.subtract))

        def turn_hidden(half, tk):
            need("pe", tk[f"hid{half}"], tk[f"hidT{half}"])
            for k in range(4):
                kk = 4 * half + k
                mm = pe.transpose(psum[6 + half][:, k * P:(k + 1) * P], hid[:, kk * P:(kk + 1) * P], ident[:, :])
            t = up("pe", mm)
            need("ac", t)
            turned = psum[6 + half][:, :].rearrange("p (k n) -> p k n", k=4)
            t = up("ac", ac.copy(hid_hi[:, 4 * half:4 * half + 4, :], turned))
            need("ve", t)
            tk[f"hidT{half}"] = up("ve", ve.tensor_tensor(hid_lo[:, 4 * half:4 * half + 4, :], turned, hid_hi[:, 4 * half:4 * half + 4, :].bitcast(F32), ALU.subtract))

        def expert(e, tk, last=False):
            tk = dict(tk)
            y_free = (g.flag("scattered"), g.flag("scattered").n)
            if not last:
                gather(e + 1, tk)
            need("pe", tk["xT"])
            for u in range(UNITS):
                if u + AHEAD < UNITS or not last:
                    split(u + AHEAD, tk)
                if u + AHEAD + SLOTS < UNITS or not last:
                    fetch(u + AHEAD + SLOTS, e, tk)
                b, half = u // 2, u // 4
                if u < 8:
                    if u % 4 == 2:
                        need("pe", tk[f"y{half}"])
                    t = product(psum[b], xh, xlo, u, tk)
                    if u % 4 == 1:
                        need("ac", t)
                        s_t = up("ac", ac.activation(silu[:, half, :], psum[b][:, :], ACT.Silu))
                    if u % 4 == 3:
                        need("ve", t, s_t)
                        tk[f"hid{half}"] = up("ve", ve.tensor_tensor(hid[:, half * 512:(half + 1) * 512], psum[b][:, :], silu[:, half, :], ALU.mult))
                    if u == 5:
                        turn_hidden(0, tk)
                    if u == 7 and not last:
                        turn_x(tk)
                else:
                    half = b - 4
                    need("pe", tk[f"hidT{u % 2}"])
                    t = product(psum[2 * half + 1], hid_hi, hid_lo, u, tk)
                    if u == 8:
                        turn_hidden(1, tk)
                        if not last:
                            split_x(tk)
                    if u % 2:
                        need("ve", t, y_free)
                        hs = slice(half * 512, (half + 1) * 512)
                        tk[f"y{half}"] = up("ve", ve.scalar_tensor_tensor(y[:, hs], psum[2 * half + 1][:, :], VALC[:, bass.ds(e, 1)], ga2b[:, hs], ALU.mult, ALU.mult))
            need("po", y_free)
            c = up("po", po.tensor_copy(idx_s[:, :], IDXC[:, bass.ds(e, 1)]))
            need("po", c, tk["y1"])
            f = g.flag("scattered")
            po.indirect_dma_start(x2_rows, bass.IndirectOffsetOnAxis(idx_s[:, :], 0), y[:, :], None, compute_op=ALU.add).then_inc(f.sem, 16)
            f.n += 16
            return tk

        gather(0, tk)
        turn_x(tk)
        split_x(tk)
        tk = expert(0, tk)
        per = {"pe_done": 16, "ac_done": 25, "ve_done": 19, "po_done": 2, "gathered": 16, "scattered": 16,
               **{f"expert_raw{r}_loaded": 32 for r in range(SLOTS)}}
        turns = []
        g.loop(NE - 2, per, lambda i: turns.append(expert(i + 1, g.carry(tk))))
        tk = expert(NE - 1, g.after(turns[0], NE - 2, per), last=True)
        scattered = (g.flag("scattered"), g.flag("scattered").n)
    all_engines_meet()
    NMIX = DMIX // P
    UNIT = 2048
    w_in2_v = A["w_in_2"].rearrange("o (k p) n -> p (o k) n", p=P)
    w_out2_v = A["w_out_2"].rearrange("o (k p) n -> p (o k) n", p=P)
    raw2 = half_of_slot[0:2] + [half_of_slot[4][:, 0:UNIT // 2]]
    tm = [half_of_slot[4][:, 512 * n:512 * n + 512] for n in range(3)]
    cn_tmp = half_of_slot[4][:, 1536:2048]
    part = lambda name, n, at: nc.alloc_sbuf_tensor_at(f"block2_w_{name}", [P, n], F32R, offset=wslots_at + 4 * at)
    lo2 = [part("lo0", UNIT, 0), part("lo1", UNIT, UNIT), part("lo2", UNIT // 2, 4 * UNIT)]
    hi2 = [part("hi0", UNIT, 2 * UNIT), part("hi1", UNIT, 3 * UNIT), part("hi2", UNIT // 2, 4 * UNIT + UNIT // 2)]
    unit_columns = lambda n: (w_in2_v[:, :, 256 * n:256 * n + 256], KD)
    out_rows_k = lambda k0, k1: (w_out2_v[:, k0:k1, 0:512], k1 - k0)
    plan = [unit_columns(n) for n in (7, 6, 0, 1, 2, 3, 4, 5, 8, 13, 9, 10, 11, 12)] + [out_rows_k(0, 4), out_rows_k(4, 8), out_rows_k(8, 10)]
    place = lambda n: 2 if n == len(plan) - 1 else n % 2
    unit = {"fetched": 0, "split": 0, "taken": 0}
    used2 = [None] * 3
    got2, ready2 = {}, {}

    def unit_view(t, n):
        source, k = plan[n]
        cols = source.shape[-1]
        return t[:, 0:k * cols].rearrange("p (k n) -> p k n", k=k)

    def fetch_unit():
        n = unit["fetched"]
        need("sp", used2[place(n)])
        got2[n] = load("sp", f"block2_w_loaded_{place(n)}", unit_view(raw2[place(n)], n), plan[n][0])
        unit["fetched"] += 1

    def split_unit():
        n = unit["split"]
        r = place(n)
        need("ac", got2[n], used2[r])
        t = up("ac", ac.copy(unit_view(hi2[r], n), unit_view(raw2[r], n)))
        need("ve", t, got2[n])
        ready2[n] = up("ve", ve.tensor_tensor(unit_view(lo2[r], n), unit_view(raw2[r], n), unit_view(hi2[r], n).bitcast(F32), ALU.subtract))
        unit["split"] += 1

    def next_unit(wait=True):
        n = unit["taken"]
        unit["taken"] += 1
        if unit["fetched"] == n:
            fetch_unit()
        if unit["split"] == n:
            split_unit()
        if unit["fetched"] == n + 1 and n + 1 < len(plan) and place(n + 1) < 2:
            fetch_unit()
        if wait:
            need("pe", ready2[n])
        return place(n), unit_view(hi2[place(n)], n), unit_view(lo2[place(n)], n)

    def prepare():
        if unit["split"] < unit["fetched"]:
            split_unit()

    need("sp", *[tk[f"raw{r}"] for r in range(6)])
    for n in range(2):
        fetch_unit()
    need("ac", *[tk[f"raw{r}"] for r in range(6)])
    for n in range(2):
        split_unit()

    two = Scope().__enter__()
    HT = two.sb("HT", [P, NMIX, T])
    HT_at = address() - 4 * NMIX * T
    arena_at = address()
    arena = two.sb("arena", [P, 8316])
    xft = Scope().__enter__()
    SB_ = xft.sb("gating_bias", [P, 2, P])
    tril = xft.sb("tril", [P, P])
    grp = xft.sb("pool_grp", [P, 2, P])
    fix = xft.sb("pool_fix", [P, 2, 16])
    invw = xft.sb("pool_inv", [P, 2])
    XH = xft.sb("XFT_hi", [P, KD, T], F32R)
    XL = xft.sb("XFT_lo", [P, KD, T], F32R)
    XF = arena[:, 0:TT * D].rearrange("p (t n) -> p t n", t=TT)
    junk = half_of_slot[5][:, 0:D]
    gf = half_of_slot[5][:, D:2 * D]
    got_gf = load("ac", "g_final", gf, A["g_final"].partition_broadcast(P).rearrange("p a n -> p (a n)") if len(A["g_final"].shape) > 1 else A["g_final"].partition_broadcast(P))
    need("sp", scattered)
    got_xf = [load("sp", f"xf_loaded{j}", XF[:, j, :], x_tile(x2_rows, j)) for j in range(TT)]
    need("ve", got_gf)
    xf_ready = [None] * TT

    def final_norm(j):
        need("ac", got_xf[j])
        t = up("ac", ac.activation(junk, XF[:, j, :], ACT.Square, accum_out=small[:, j:j + 1]))
        need("ac", t)
        need("ve", t)
        t = up("ve", ve.tensor_scalar(small[:, 16 + j:17 + j], small[:, j:j + 1], 1.0 / D, EPS, ALU.mult, ALU.add))
        need("ac", t)
        t = up("ac", ac.activation(small[:, 32 + j:33 + j], small[:, 16 + j:17 + j], ACT.Sqrt))
        need("ve", t)
        t = up("ve", ve.reciprocal(small[:, 48 + j:49 + j], small[:, 32 + j:33 + j]))
        need("ve", t)
        xf_ready[j] = up("ve", ve.scalar_tensor_tensor(XF[:, j, :], XF[:, j, :], small[:, 48 + j:49 + j], gf, ALU.mult, ALU.mult))
        need("sp", xf_ready[j])
        return load("sp", "xf_stored", x_tile(xf_rows, j), XF[:, j, :])

    def turn_final(j):
        need("pe", xf_ready[j])
        for half in range(2):
            b = banks.take()
            for k in range(4):
                kk = 4 * half + k
                mm = pe.transpose(psum[b][:, k * P:(k + 1) * P], XF[:, j, kk * P:(kk + 1) * P], ident[:, :])
            t = up("pe", mm)
            turned = psum[b][:, :].rearrange("p (k n) -> p k n", k=4)
            place = (slice(0, P), slice(4 * half, 4 * half + 4), slice(j * P, (j + 1) * P))
            need("ac", t)
            t = up("ac", ac.copy(XH[place], turned))
            need("ve", t)
            t = up("ve", ve.tensor_tensor(XL[place], turned, XH[place].bitcast(F32), ALU.subtract))
            banks.freed(b, t)
        return t

    for j in range(TT):
        xf_stored = final_norm(j)
        if j > 0:
            turn_final(j - 1)
    XFT_ready = turn_final(TT - 1)
    for e in ("ac", "ve", "po"):
        need(e, xf_stored, *[g.now(k) for k in ("pe", "ve", "ac") if k != e])
    need("pe", XFT_ready)

    def of_arena(start, a, n):
        return arena[:, start:start + a * n].rearrange("p (a n) -> p a n", a=a)

    XP = of_arena(0, 2, 16 + T)
    XC = of_arena(2080, 2, 16 + T)
    VG = half_of_slot[5].rearrange("p (a n) -> p a n", a=TT)
    HP = of_arena(4160, 2, CONV_D - 1 + T)
    CV = of_arena(6268, 2, T)
    as3 = lambda v, a: v.rearrange("p (a n) -> p a n", a=a)
    sgw, WT = as3(ga1b[:, 0:512], NH), as3(ga1b[:, 512:1024], NH)
    lng, pw = as3(ga2b[:, 0:512], 2), as3(ga2b[:, 512:1024], 2)

    def project2(block, c0, finish):
        s, wh, wl = block
        for half in range(2):
            hs = slice(half * 512, (half + 1) * 512)
            b = banks.take()
            for k in range(KD):
                pe.matmul(psum[b][:, :], wh[:, k, c0:c0 + P], XH[:, k, hs], start=k == 0, stop=False)
                pe.matmul(psum[b][:, :], wh[:, k, c0:c0 + P], XL[:, k, hs], start=False, stop=False)
                mm = pe.matmul(psum[b][:, :], wl[:, k, c0:c0 + P], XH[:, k, hs], start=False, stop=k == KD - 1)
            used2[s] = up("pe", mm)
            banks.freed(b, finish(psum[b], hs, used2[s]))
        if c0 == 0:
            prepare()

    def copy_to(dst, func=None):
        def finish(bank, hs, t):
            need("ac", t)
            return evacuate("ac", dst(hs), bank[:, :], func=func)
        return finish

    with Scope() as st:
        stats = st.sb("gating_stats", [P, TT, 6])
        mv = st.sb("gating_mv", [P, TT, 2])
        sd = st.sb("gating_sd", [P, TT, 1])
        zeros = [up("po", po.memset(x, 0.0)) for x in (HP[:, :, 0:CONV_D - 1], XC[:, :, 0:16], XP[:, :, 0:16], grp[:, :, :])][-1]
        load("ac", "small2", sgw, A["sg_w_2"].rearrange("o h t s -> t (o h) s"))
        load("ac", "small2", tril[:, :], C["tril"])
        load("ac", "small2", lng[:, 0, :], A["sg_ln_g_2"].partition_broadcast(P).rearrange("p a n -> p (a n)"))
        load("ac", "small2", lng[:, 1, :], A["sg_ln_b_2"].partition_broadcast(P).rearrange("p a n -> p (a n)"))
        load("ac", "small2", pw, A["cc_pw_w_2"].rearrange("o (k p) n -> p (o k) n", p=P))
        load("ac", "small2", fix[:, :, :], C["pool_fix"])
        load("ac", "small2", invw[:, :], C["pool_inv"])
        need("ac", zeros)
        for h in range(NH):
            q = slice(64 * (h % 2), 64 * (h % 2) + 64)
            load("ac", "small2", SB_[q, h // 2, :], A["sg_b_2"][0, h:h + 1, :].partition_broadcast(64).rearrange("p a n -> p (a n)"))
            got_small = load("ac", "small2", grp[q, h // 2, 64 * (h % 2):64 * (h % 2) + 64], A["pool_w_2"][0, h, :, :])

        block = next_unit()
        for tile in range(2):
            def sig_g(bank, hs, t, tile=tile):
                need("ac", t)
                return up("ac", ac.activation(CV[:, tile, hs], bank[:, :], ACT.Sigmoid))
            project2(block, tile * P, sig_g)
        block = next_unit()
        for tile in range(2):
            def a_times(bank, hs, t, tile=tile):
                need("ve", t, g.now("ac"), zeros)
                return up("ve", ve.tensor_tensor(HP[:, tile, CONV_D - 1 + hs.start:CONV_D - 1 + hs.stop], bank[:, :], CV[:, tile, hs], ALU.mult))
            project2(block, tile * P, a_times)
        hp_ready = g.now("ve")
        conv_t = [hp_ready, hp_ready]

        def conformer_taps(first, last_):
            for n in range(first, last_):
                for tile in range(2):
                    wc = col3[:, P3["dw"] + 2 * n + tile:P3["dw"] + 2 * n + tile + 1]
                    src = HP[:, tile, n:n + T]
                    need("ve", conv_t[tile])
                    if n == 0:
                        bias = col3[:, P3["dw_b"] + tile:P3["dw_b"] + tile + 1]
                        conv_t[tile] = up("ve", ve.tensor_scalar(CV[:, tile, :], src, wc, bias, ALU.mult, ALU.add))
                    else:
                        conv_t[tile] = up("ve", ve.scalar_tensor_tensor(CV[:, tile, :], src, wc, CV[:, tile, :], ALU.mult, ALU.add))

        need("ve", got_small)
        for h in range(NH):
            t = up("ve", ve.tensor_tensor(sgw[:, h, :], sgw[:, h, :], tril[:, :], ALU.mult))
        need("pe", t)
        b = banks.take()
        for h in range(NH):
            mm = pe.transpose(psum[b][:, h * P:(h + 1) * P], sgw[:, h, :], ident[:, :])
        t = up("pe", mm)
        need("ve", t)
        wt_ready = evacuate("ve", WT, psum[b][:, :].rearrange("p (h n) -> p h n", h=NH))
        banks.freed(b, wt_ready)

        block = next_unit()
        conformer_taps(0, 5)
        for tile in range(2):
            project2(block, tile * P, copy_to(lambda hs: XP[:, tile, 16 + hs.start:16 + hs.stop]))
        block = next_unit()
        conformer_taps(5, 9)
        for tile in range(2):
            project2(block, tile * P, copy_to(lambda hs: HT[:, tile, hs]))
        block = next_unit()
        for tile in range(2):
            def times_x(bank, hs, t, tile=tile):
                need("ve", t, g.now("ac"))
                o = XP[:, tile, 16 + hs.start:16 + hs.stop]
                return up("ve", ve.tensor_tensor(o, bank[:, :], o, ALU.mult))
            project2(block, tile * P, times_x)
        ca_ready = g.now("ve")
        block = next_unit()
        for tile in range(2):
            project2(block, tile * P, copy_to(lambda hs: HT[:, 2 + tile, hs], func=ACT.Gelu_apprx_tanh))
        u_ready = g.now("ac")
        need("ve", ca_ready)
        acc_a = VG.rearrange("p (a b) n -> p a (b n)", a=2)
        for tile in range(2):
            for n in range(CONV_A):
                wc = col3[:, P3["conv_a"] + 2 * n + tile:P3["conv_a"] + 2 * n + tile + 1]
                src = XP[:, tile, 14 + n:14 + n + T]
                if n == 0:
                    t = up("ve", ve.tensor_scalar(acc_a[:, tile, :], src, wc, None, ALU.mult))
                else:
                    need("ve", t)
                    t = up("ve", ve.scalar_tensor_tensor(acc_a[:, tile, :], src, wc, acc_a[:, tile, :], ALU.mult, ALU.add))
            need("ve", t, u_ready)
            ya_ready = up("ve", ve.tensor_tensor(HT[:, tile, :], HT[:, tile, :], acc_a[:, tile, :], ALU.mult))

        block = next_unit()
        conformer_taps(9, 12)
        need("ac", ya_ready)
        s, wh, wl = block
        for j in range(TT):
            b = banks.take()
            js = slice(j * P, (j + 1) * P)
            for k in range(KD):
                pe.matmul(psum[b][:, 0:DG], XH[:, k, js], wh[:, k, :], start=k == 0, stop=False)
                pe.matmul(psum[b][:, 0:DG], XH[:, k, js], wl[:, k, :], start=False, stop=False)
                mm = pe.matmul(psum[b][:, 0:DG], XL[:, k, js], wh[:, k, :], start=False, stop=k == KD - 1)
            used2[s] = up("pe", mm)
            if j == 3:
                prepare()
            need("ac", used2[s])
            v_ready = up("ac", ac.activation(VG[:, j, :], psum[b][:, 0:DG], ACT.Gelu_apprx_tanh))
            banks.freed(b, v_ready)
        need("ve", v_ready)
        for j in range(TT):
            t = up("ve", ve.bn_stats(stats[:, j, :], VG[:, j, :]))
        need("ve", t)
        for j in range(TT):
            t = up("ve", ve.bn_aggr(mv[:, j, :], stats[:, j, :]))
        need("ve", t)
        t = up("ve", ve.tensor_scalar(sd[:, :, :], mv[:, :, 1:2], LN_EPS, None, ALU.add))
        need("ac", t)
        t = up("ac", ac.activation(sd[:, :, :], sd[:, :, :], ACT.Sqrt))
        need("ve", t)
        t = up("ve", ve.reciprocal(sd[:, :, :], sd[:, :, :]))
        need("ve", t)
        for j in range(TT):
            t = up("ve", ve.tensor_scalar(VG[:, j, :], VG[:, j, :], mv[:, j, 0:1], sd[:, j, :], ALU.subtract, ALU.mult))
            need("po", t, got_small)
            t = up("po", po.tensor_tensor(VG[:, j, :], VG[:, j, :], lng[:, 0, :], ALU.mult))
            need("po", t)
            vn_ready = up("po", po.tensor_tensor(VG[:, j, :], VG[:, j, :], lng[:, 1, :], ALU.add))

        block = next_unit()
        for tile in range(2):
            project2(block, tile * P, copy_to(lambda hs: XC[:, tile, 16 + hs.start:16 + hs.stop]))
        xc_ready = g.now("ac")
        conformer_taps(12, 16)
        block = next_unit()
        for tile in range(2):
            project2(block, tile * P, copy_to(lambda hs: HT[:, 8 + tile, hs]))
        q_ready = g.now("ac")

        need("pe", vn_ready, wt_ready)
        for pair in range(2):
            for quad in range(2):
                for hh in range(2):
                    b = banks.take()
                    for j in range(4):
                        mm = pe.matmul(psum[b][:, j * P:(j + 1) * P], VG[:, 4 * quad + j, pair * P:(pair + 1) * P], WT[:, 2 * pair + hh, :], start=True, stop=True)
                    t = up("pe", mm)
                    q = slice(64 * hh, 64 * hh + 64)
                    hs = slice(quad * 512, (quad + 1) * 512)
                    need("ve", t, u_ready)
                    as_chunks = lambda x: x.rearrange("p (c n) -> p c n", c=4)
                    t = up("ve", ve.tensor_tensor(as_chunks(tm[0][q, :]), as_chunks(psum[b][q, :]), SB_[q, pair:pair + 1, :].to_broadcast([64, 4, P]), ALU.add))
                    banks.freed(b, t)
                    need("ve", t)
                    yb_ready = up("ve", ve.tensor_tensor(HT[q, 2 + pair, hs], HT[q, 2 + pair, hs], tm[0][q, :], ALU.mult))

        qc = cn_tmp[:, 0:2 * P].rearrange("p (a n) -> p a n", a=2)
        pr, prT = (half_of_slot[5][:, 1024 * n:1024 * n + 1024] for n in range(2))
        pr, prT = pr.rearrange("p (h m) -> p h m", h=NH), prT.rearrange("p (n l) -> p n l", l=P)
        mx = st.sb("attn_max", [P, NH, 1])
        sm = st.sb("attn_sum", [P, NH, 1])
        need("pe", mem_ready)
        need("ac", q_ready, yb_ready)
        need("ve", g.now("po"))
        for b in range(8):
            need("pe", banks.last[b])
        score = lambda h: psum[h % 2][:, (h // 2) * MEM:(h // 2 + 1) * MEM]

        def score_chunk(j, tk):
            need("ac", tk["scored"])
            tk["q"] = up("ac", ac.copy(qc, HT[:, 8:10, bass.ds(j * P, P)]))
            need("pe", tk["q"], tk["exp"])
            for h in range(NH):
                q = slice(64 * (h % 2), 64 * (h % 2) + 64)
                mm = pe.matmul(score(h), qc[q, h // 2, :], K2T[q, h // 2, :], start=True, stop=True)
            tk["scored"] = up("pe", mm)
            need("ve", tk["scored"])
            for n in range(2):
                t = up("ve", ve.tensor_reduce(mx[:, n::2, :].rearrange("p h a -> p (h a)"), psum[n][:, :].rearrange("p (h m) -> p h m", h=2), X, ALU.max))
            need("ve", t)
            tk["max"] = up("ve", ve.tensor_scalar(mx[:, :, :], mx[:, :, :], -0.125, None, ALU.mult))

        def soften_chunk(tk):
            need("ac", tk["max"], tk["turned"])
            for h in range(NH):
                tk["exp"] = up("ac", ac.activation(pr[:, h, :], score(h), ACT.Exp, scale=0.125, bias=mx[:, h, :], accum_out=sm[:, h, :]))
            need("ve", tk["exp"])
            t = up("ve", ve.reciprocal(sm[:, :, :], sm[:, :, :]))
            need("ve", t)
            tk["p"] = up("ve", ve.tensor_tensor(pr, pr, sm[:, :, :].to_broadcast([P, NH, MEM]), ALU.mult))

        def attend(j, tk, last=False):
            tk = dict(tk)
            if not last:
                score_chunk(j + 1, tk)
            for tile in range(2):
                need("ve", tk[f"conv{tile}"])
                wc = col3[:, bass.ds(P3["dw"] + 2 * TAPS_BEFORE + tile + 2 * j, 1)]
                tk[f"conv{tile}"] = up("ve", ve.scalar_tensor_tensor(CV[:, tile, :], HP[:, tile, bass.ds(j + TAPS_BEFORE, T)], wc, CV[:, tile, :], ALU.mult, ALU.add))
            need("pe", tk["p"], tk["pT"])
            for n in range(2 * NH):
                mm = pe.transpose(psum[2 + n // 4][:, (n % 4) * P:(n % 4 + 1) * P], pr[:, n // 2, (n % 2) * P:(n % 2 + 1) * P], ident[:, :])
            tk["turned"] = up("pe", mm)
            need("ac", tk["turned"], tk["applied"])
            for n in range(2):
                tk["pT"] = up("ac", ac.copy(prT[:, 4 * n:4 * n + 4, :], psum[2 + n][:, :].rearrange("p (n l) -> p n l", n=4)))
            if not last:
                soften_chunk(tk)
            need("pe", tk["pT"], tk["out"])
            for h in range(NH):
                for m in range(2):
                    mm = pe.matmul(psum[4][:, h * P:(h + 1) * P], V2[:, m, (h // 2) * P:(h // 2 + 1) * P], prT[:, 2 * h + m, :], start=m == 0, stop=m == 1)
            tk["applied"] = up("pe", mm)
            need("ve", tk["applied"])
            for hh in range(2):
                q = slice(64 * hh, 64 * hh + 64)
                tk["out"] = up("ve", ve.tensor_copy(HT[q, 8:10, bass.ds(j * P, P)], psum[4][q, :].rearrange("p (a b n) -> p a b n", a=2, b=2)[:, :, hh, :]))
            return tk

        TAPS_BEFORE = 16
        tk = {k: None for k in ("scored", "exp", "turned", "pT", "applied", "out")}
        tk["conv0"], tk["conv1"] = conv_t
        score_chunk(0, tk)
        soften_chunk(tk)
        tk = attend(0, tk)
        per = {"pe_done": 3, "ac_done": 7, "ve_done": 9}
        turns = []
        g.loop(TT - 2, per, lambda i: turns.append(attend(i + 1, g.carry(tk))))
        tk = attend(TT - 1, g.after(turns[0], TT - 2, per), last=True)
        conv_t = [tk["conv0"], tk["conv1"]]
        for b in range(8):
            need("pe", tk["out"], tk["pT"])

        def pool_steps():
            need("ve", xc_ready)
            t = up("ve", ve.tensor_copy(HT[:, 4:6, :], XC[:, :, 16:16 + T]))
            up("ve", ve.memset(XP[:, :, 0:16], 0.0))
            need("ve", g.now("ve"))
            src, dst = XC, XP
            for n in range(4):
                shift = 1 << n
                t = up("ve", ve.tensor_tensor(dst[:, :, 16:16 + T], src[:, :, 16:16 + T], src[:, :, 16 - shift:16 - shift + T], ALU.add))
                need("ve", t)
                q, tile = slice(64 * (n % 2), 64 * (n % 2) + 64), n // 2
                t = up("ve", ve.tensor_tensor(dst[q, tile, 16:32], dst[q, tile, 16:32], fix[q, tile, :], ALU.mult))
                need("ve", t)
                t = up("ve", ve.scalar_tensor_tensor(HT[q, 4 + tile, :], dst[q, tile, 16:16 + T], invw[q, tile:tile + 1], HT[q, 4 + tile, :], ALU.mult, ALU.subtract))
                need("ve", t)
                src, dst = dst, src
            pooled = t
            yield
            need("pe", pooled, got_small)
            for tile in range(2):
                for half in range(2):
                    hs = slice(half * 512, (half + 1) * 512)
                    b = banks.take()
                    t = up("pe", pe.matmul(psum[b][:, :], grp[:, tile, :], HT[:, 4 + tile, hs], start=True, stop=True))
                    need("ac", t)
                    yc_ready = up("ac", ac.activation(HT[:, 4 + tile, hs], psum[b][:, :], ACT.Identity, scale=col3[:, P3["pool_scale"] + tile:P3["pool_scale"] + tile + 1]))
                    banks.freed(b, yc_ready)
            need("ve", yc_ready)
            yield

        squares2 = memory[:, :, :, :].rearrange("p a b n -> p a (b n)")

        def conformer_steps(half):
            hs = slice(half * 512, (half + 1) * 512)
            need("pe", *conv_t)
            squares_read = g.now("pe")
            b = banks.take()
            for tile in range(2):
                mm = pe.matmul(psum[b][:, :], ones[:, :], CV[:, tile, hs], start=tile == 0, stop=tile == 1)
            t = up("pe", mm)
            need("ve", t)
            for tile in range(2):
                t = up("ve", ve.scalar_tensor_tensor(CV[:, tile, hs], psum[b][:, :], -1.0 / DG, CV[:, tile, hs], ALU.mult, ALU.add))
            banks.freed(b, t)
            need("ac", t, squares_read)
            for tile in range(2):
                t = up("ac", ac.activation(squares2[:, tile, :], CV[:, tile, hs], ACT.Square))
            yield
            need("pe", t)
            b = banks.take()
            for tile in range(2):
                mm = pe.matmul(psum[b][:, :], ones[:, :], squares2[:, tile, :], start=tile == 0, stop=tile == 1)
            t = up("pe", mm)
            need("ve", t)
            t = up("ve", ve.tensor_scalar(cn_tmp, psum[b][:, :], 1.0 / DG, LN_EPS, ALU.mult, ALU.add))
            banks.freed(b, t)
            need("ac", t)
            t = up("ac", ac.activation(cn_tmp, cn_tmp, ACT.Sqrt))
            need("ve", t)
            t = up("ve", ve.reciprocal(cn_tmp, cn_tmp))
            need("ve", t)
            for tile in range(2):
                t = up("ve", ve.tensor_tensor(CV[:, tile, hs], CV[:, tile, hs], cn_tmp, ALU.mult))
            need("ac", t)
            for tile in range(2):
                t = up("ac", ac.activation(CV[:, tile, hs], CV[:, tile, hs], ACT.Silu, scale=col3[:, P3["cc_g"] + tile:P3["cc_g"] + tile + 1], bias=col3[:, P3["cc_b"] + tile:P3["cc_b"] + tile + 1]))
            yield
            need("pe", t)
            for tile in range(2):
                b = banks.take()
                for k in range(2):
                    mm = pe.matmul(psum[b][:, :], pw[:, k, tile * P:(tile + 1) * P], CV[:, k, hs], start=k == 0, stop=k == 1)
                t = up("pe", mm)
                need("ac", t)
                banks.freed(b, evacuate("ac", HT[:, 6 + tile, hs], psum[b][:, :]))
            yield

        GH = nc.alloc_sbuf_tensor_at("gated_hi", [P, NMIX, T], F32R, offset=HT_at)
        GL_a = nc.alloc_sbuf_tensor_at("gated_lo_a", [P, 8, T], F32R, offset=arena_at)
        GL_b = nc.alloc_sbuf_tensor_at("gated_lo_b", [P, 2, T], F32R, offset=wslots_at + 4 * 5 * UNIT)
        GL = lambda tile, cols: GL_a[:, tile, cols] if tile < 8 else GL_b[:, tile - 8, cols]
        free = [None] * 3
        pooling, norm = pool_steps(), [conformer_steps(half) for half in range(2)]
        tap_step = lambda first, last_: lambda: conformer_taps(first, last_)
        step_of = lambda gen: lambda: next(gen)
        between = [None, None, None, None,
                   tap_step(24, 26), tap_step(26, 28), tap_step(28, 30), tap_step(30, CONV_D), None,
                   *[step_of(norm[n // 3]) for n in range(5)], None, None, None, None, None, None]
        need("ve", tk["out"], tk["pT"], yb_ready)
        next(pooling)
        for n, pair in enumerate((4, 0, 1, 2, 3)):
            block = next_unit()
            if n == 1:
                next(pooling)
            if n == 4:
                next(norm[1])
                need("ve", g.now("pe"), g.now("ac"))
            for t2 in range(2):
                tile = 2 * pair + t2

                def gated(bank, hs, t, tile=tile):
                    m = (tile * 2 + hs.start // 512) % 3
                    need("ac", t, free[m])
                    r = up("ac", ac.activation(tm[m], bank[:, :], ACT.Silu))
                    need("ve", r)
                    t = up("ve", ve.tensor_tensor(tm[m], HT[:, tile, hs], tm[m], ALU.mult))
                    need("ac", t)
                    t = up("ac", ac.copy(GH[:, tile, hs], tm[m]))
                    need("ve", t)
                    free[m] = up("ve", ve.tensor_tensor(GL(tile, hs), tm[m], GH[:, tile, hs].bitcast(F32), ALU.subtract))
                    between_step = between.pop(0)
                    if between_step:
                        between_step()
                    return r
                project2(block, t2 * P, gated)
        used2[2] = gated_ready = g.now("ve")
    xft.__exit__()

    with Scope() as st:
        W1_at = address()
        W1L = st.sb("w_out2_lo", [P, NMIX, 512], F32R)
        W1H = st.sb("w_out2_hi", [P, NMIX, 512], F32R)
        W1R = nc.alloc_sbuf_tensor_at("w_out2_raw", [P, NMIX, 512], F32, offset=W1_at)
        XR_ = st.sb("residual", [P, TT - 1, D])
        XR = [XR_[:, j, :] for j in range(TT - 1)] + [memory[:, :, :, :].rearrange("p a b n -> p (a b n)")]
        lnr = [ga1b, ga2b]
        stats = st.sb("ln_stats", [P, TT, 2, 6])
        mv = st.sb("ln_mv", [P, TT, 2])
        sd = st.sb("ln_sd", [P, TT, 1])
        blocks = [next_unit(wait=False) for _ in range(3)]
        for e in ("sp", "ac"):
            need(e, gated_ready, xf_stored)
        need("ve", g.now("pe"))
        got_xr = [load("ac", f"residual{j}", XR[j], x_tile(xf_rows, j)) for j in range(TT)]
        got_w1 = load("sp", "w_out2_half", W1R[:, :, :], w_out2_v[:, :, 512:1024])
        load("ac", "ln_rows", lnr[0][:, :], A["ln_g_2"].partition_broadcast(P).rearrange("p a n -> p (a n)"))
        got_ln = load("ac", "ln_rows", lnr[1][:, :], A["ln_b_2"].partition_broadcast(P).rearrange("p a n -> p (a n)"))
        w1_ready = []

        def split_w1(n):
            ks = slice(2 * n, 2 * n + 2)
            need("ac", got_w1)
            t = up("ac", ac.copy(W1H[:, ks, :], W1R[:, ks, :]))
            need("ve", t, got_w1)
            w1_ready.append(up("ve", ve.tensor_tensor(W1L[:, ks, :], W1R[:, ks, :], W1H[:, ks, :].bitcast(F32), ALU.subtract)))

        out_rows = out.rearrange("b (t p) n -> p (b t) n", p=P)

        def out_product(bank, j, k, wh, wl):
            js = slice(j * P, (j + 1) * P)
            pe.matmul(bank[:, :], GH[:, k, js], wh, start=k == 0, stop=False)
            pe.matmul(bank[:, :], GH[:, k, js], wl, start=False, stop=False)
            return pe.matmul(bank[:, :], GL(k, js), wh, start=False, stop=k == NMIX - 1)

        half0 = {}
        for half in range(2):
            hs = slice(half * 512, (half + 1) * 512)
            if half:
                need("pe", w1_ready[-1])
            for j in range(TT):
                if half == 0:
                    if j % 4 == 0:
                        taken = [banks.take() for _ in range(4)]
                        for n, (_, wh, wl) in enumerate(blocks):
                            need("pe", ready2[len(plan) - 3 + n], gated_ready if n else None)
                            for jj in range(4):
                                for k in range(wh.shape[1]):
                                    mm = out_product(psum[taken[jj]], j + jj, 4 * n + k, wh[:, k, :], wl[:, k, :])
                                half0[j + jj] = (taken[jj], up("pe", mm))
                    b, t = half0[j]
                else:
                    b = banks.take()
                    for k in range(NMIX):
                        mm = out_product(psum[b], j, k, W1H[:, k, :], W1L[:, k, :])
                    t = up("pe", mm)
                need("ve", t, got_xr[j])
                t = up("ve", ve.scalar_tensor_tensor(XR[j][:, hs], XR[j][:, hs], ALPHA, psum[b][:, :], ALU.mult, ALU.add))
                banks.freed(b, t)
                need("ve", t)
                t = up("ve", ve.bn_stats(stats[:, j, half, :], XR[j][:, hs]))
                if half:
                    need("ve", t)
                    t = up("ve", ve.bn_aggr(mv[:, j, :], stats[:, j, :, :].rearrange("p a b -> p (a b)")))
                    need("ve", t)
                    t = up("ve", ve.tensor_scalar(sd[:, j, :], mv[:, j, 1:2], LN_EPS, None, ALU.add))
                    need("ac", t)
                    t = up("ac", ac.activation(sd[:, j, :], sd[:, j, :], ACT.Sqrt))
                    need("ve", t)
                    t = up("ve", ve.reciprocal(sd[:, j, :], sd[:, j, :]))
                    need("ve", t)
                    t = up("ve", ve.tensor_scalar(XR[j], XR[j], mv[:, j, 0:1], sd[:, j, :], ALU.subtract, ALU.mult))
                    need("ve", t, got_ln)
                    t = up("ve", ve.tensor_tensor(XR[j], XR[j], lnr[0][:, :], ALU.mult))
                    e = "ve" if j == TT - 1 else "po"
                    need(e, t, got_ln)
                    t = up(e, g.engines[e].tensor_tensor(XR[j], XR[j], lnr[1][:, :], ALU.add))
                    need("sp", t)
                    stored_out = load("sp", "out_stored", out_rows[:, j, :], XR[j])
                elif j < 5:
                    split_w1(j)
        need("sp", stored_out)
    two.__exit__()
    top.__exit__()



INPUTS = [
    "x", "c", "ctx", "c_ctx", "w_ada", "b_ada", "g_norm1", "w_in", "b_gates", "w_conv", "w_fourier",
    "w_mlstm", "w_out", "g_norm2", "w_router", "w_gate_e", "w_up_e", "w_down_e", "g_final", "mem_2",
    "w_in_2", "conv_a_w_2", "sg_ln_g_2", "sg_ln_b_2", "sg_w_2", "sg_b_2", "pool_w_2", "pool_scale_2",
    "cc_dw_w_2", "cc_dw_b_2", "cc_ln_g_2", "cc_ln_b_2", "cc_pw_w_2", "w_kv_2", "w_out_2", "ln_g_2", "ln_b_2",
]


def constants():
    j = np.arange(P)
    tri = np.zeros((P, 2, P), np.float32)
    tri[:, 0, :] = np.where(j[:, None] <= j[None, :], 0.0, MASKED)
    tri[:, 1, :] = np.where(j[:, None] >= j[None, :], 0.0, MASKED)
    sel = np.zeros((32, 8, P), np.float32)
    for r in range(8):
        sel[r, r, :] = 1.0
    reset = np.ones((36, TA), np.float32)
    reset[0:4, 0::P] = 0.0
    reset[32:36, P - 1::P] = 0.0
    norm = 1.0 / math.sqrt(T * P)
    ang = 2 * np.pi * np.outer(j, j) / P
    channels = np.concatenate([np.cos(ang), np.sin(ang)], 1) * norm
    n = np.arange(512)
    angt = 2 * np.pi * (np.outer(n, n) % T) / T
    fix = np.ones((P, 2, 16), np.float32)
    inv = np.ones((P, 2), np.float32)
    for grp, w in enumerate((2, 4, 8, 16)):
        q = slice(64 * (grp % 2), 64 * (grp % 2) + 64)
        inv[q, grp // 2] = 1.0 / w
        for t in range(16):
            fix[q, grp // 2, t] = w / min(t + 1, w)
    return {
        "ident": np.eye(P, dtype=np.float32), "mask": tri, "sel": sel, "reset": reset,
        "dft_channels": channels.astype(np.float32), "dft_cos": np.cos(angt).astype(np.float32),
        "dft_sin": np.sin(angt).astype(np.float32),
        "alternating": np.where(n % 2 == 0, 1.0, -1.0).astype(np.float32)[None, :],
        "tril": np.tril(np.ones((P, P), np.float32)), "pool_fix": fix, "pool_inv": inv,
    }


def kernel(**inputs):
    import concourse.bacc as _bacc
    from concourse.bass_utils import run_bass_kernel_spmd as _run

    nc = _bacc.Bacc("TRN2", target_bir_lowering=False, num_devices=1)
    arrays = {f"in_{k}": np.ascontiguousarray(inputs[k]) for k in INPUTS}
    consts = {f"const_{k}": v for k, v in constants().items()}
    arrays.update(consts)
    aps = {k: nc.dram_tensor(k, a.shape, mybir.dt.from_np(a.dtype), kind="ExternalInput").ap() for k, a in arrays.items()}
    A = {k: aps[f"in_{k}"] for k in INPUTS}
    C = {k[6:]: aps[k] for k in consts}
    out = nc.dram_tensor("out", (1, T, D), F32, kind="ExternalOutput").ap()
    scratch = {k: nc.dram_tensor(f"{k}_rows", (T, D), F32, kind="Internal").ap() for k in ("xn", "x2", "xf")}
    scratch["ld"] = nc.dram_tensor("ld_rows", (2 * NH, TA), F32, kind="Internal").ap()
    build(nc, A, C, out, scratch)
    r = _run(nc, [arrays], core_ids=[0])
    return r.results[0]["out"]
```
